# Optimizing a Trainium2 kernel written in Bass

```python
import jax, jax.numpy as jnp
from jax import lax
import numpy as np
import math

D_MODEL = 1024
BATCH = 1
SEQ = 512
DEPTH = 1

GRID_W = 64
CTX_LEN = 256
N_Q_HEADS = 8
N_KV_HEADS = 2
HEAD_DIM = 64
GROUP = N_Q_HEADS // N_KV_HEADS
ATTN_DIM = N_Q_HEADS * HEAD_DIM
KV_DIM = N_KV_HEADS * HEAD_DIM
CONV_DIM = D_MODEL - ATTN_DIM
MIX_DIM = ATTN_DIM + CONV_DIM
CONV_K = 3
OFF_K = ATTN_DIM
OFF_V = OFF_K + KV_DIM
OFF_B = OFF_V + KV_DIM
OFF_C = OFF_B + CONV_DIM
OFF_U = OFF_C + CONV_DIM
MIX_IN_DIM = OFF_U + CONV_DIM
D_FF = 2816
N_MOD = 9
ROPE_THETA = 10000.0
Q_BLOCK = 128
ATTN_SCALE = HEAD_DIM ** -0.5
EPS = 1e-6


def rmsnorm(x, g):
    x32 = x.astype(jnp.float32)
    y = x32 * lax.rsqrt(jnp.mean(x32 * x32, axis=-1, keepdims=True) + EPS)
    return (y * g.astype(jnp.float32)).astype(x.dtype)

def modulate(h, shift, scale):
    return h * (1 + scale) + shift

def swiglu(h, w_in, w_out):
    gate, up = jnp.split(h @ w_in, 2, axis=-1)
    return (jax.nn.silu(gate) * up) @ w_out

def axial_rope_tables(n_tokens):
    rows = n_tokens // GRID_W
    row = jnp.repeat(jnp.arange(rows, dtype=jnp.float32), GRID_W)
    col = jnp.tile(jnp.arange(GRID_W, dtype=jnp.float32), rows)
    n_freq = HEAD_DIM // 4
    inv = ROPE_THETA ** (-jnp.arange(n_freq, dtype=jnp.float32) / n_freq)
    ang = jnp.concatenate([row[:, None] * inv, col[:, None] * inv], axis=-1)
    return jnp.cos(ang)[:, None, :], jnp.sin(ang)[:, None, :]

def apply_rope(x, cos, sin):
    xr = x.astype(jnp.float32).reshape(x.shape[:-1] + (HEAD_DIM // 2, 2))
    x0, x1 = xr[..., 0], xr[..., 1]
    out = jnp.stack([x0 * cos - x1 * sin, x0 * sin + x1 * cos], axis=-1)
    return out.reshape(x.shape).astype(x.dtype)

def gqa_softmax(q, k, v):
    s = jnp.einsum('bqkgd,bskd->bkgqs', q, k, preferred_element_type=jnp.float32) * ATTN_SCALE
    p = jax.nn.softmax(s, axis=-1).astype(v.dtype)
    return jnp.einsum('bkgqs,bskd->bqkgd', p, v)

def latent_attention(q, k, v, kc, vc):
    b, s = q.shape[:2]
    nb = s // Q_BLOCK
    k_all = jnp.concatenate([kc, k], axis=1)
    v_all = jnp.concatenate([vc, v], axis=1)
    qb = q.reshape(b, nb, Q_BLOCK, N_KV_HEADS, GROUP, HEAD_DIM).transpose(1, 0, 2, 3, 4, 5)
    o = lax.map(lambda qi: gqa_softmax(qi, k_all, v_all), qb)
    return o.transpose(1, 0, 2, 3, 4, 5).reshape(b, s, ATTN_DIM)

def context_attention(q, kc, vc):
    b, l = q.shape[:2]
    o = gqa_softmax(q.reshape(b, l, N_KV_HEADS, GROUP, HEAD_DIM), kc, vc)
    return o.reshape(b, l, ATTN_DIM)

def short_conv3(u, w):
    up = jnp.pad(u, ((0, 0), (1, 1), (0, 0)))
    return up[:, :-2] * w[0] + up[:, 1:-1] * w[1] + up[:, 2:] * w[2]

def split_heads(p, q_norm, k_norm):
    b, l = p.shape[:2]
    q = rmsnorm(p[..., :OFF_K].reshape(b, l, N_Q_HEADS, HEAD_DIM), q_norm)
    k = rmsnorm(p[..., OFF_K:OFF_V].reshape(b, l, N_KV_HEADS, HEAD_DIM), k_norm)
    v = p[..., OFF_V:OFF_B].reshape(b, l, N_KV_HEADS, HEAD_DIM)
    gb, gc, u = p[..., OFF_B:OFF_C], p[..., OFF_C:OFF_U], p[..., OFF_U:]
    return q, k, v, gb, gc, u

def first_inputs(seed: int = 0) -> dict:
    key = jax.random.key(seed)
    ks = jax.random.split(key, 24)
    f32 = jnp.float32
    nrm = lambda k, shape, s: jax.random.normal(k, shape, f32) * s
    gain = lambda k, shape: 1.0 + 0.05 * jax.random.normal(k, shape, f32)
    return {
        "x": nrm(ks[0], (BATCH, SEQ, D_MODEL), 1.0),
        "c": nrm(ks[1], (BATCH, D_MODEL), 1.0),
        "ctx": nrm(ks[2], (BATCH, CTX_LEN, D_MODEL), 1.0),
        "c_ctx": nrm(ks[3], (D_MODEL,), 1.0),
        "w_ada": nrm(ks[4], (DEPTH, D_MODEL, N_MOD * D_MODEL), 0.5 * D_MODEL ** -0.5),
        "b_ada": nrm(ks[5], (DEPTH, N_MOD * D_MODEL), 0.02),
        "norm_ffn1": gain(ks[6], (DEPTH, D_MODEL)),
        "w_ffn1_in": nrm(ks[7], (DEPTH, D_MODEL, 2 * D_FF), D_MODEL ** -0.5),
        "w_ffn1_out": nrm(ks[8], (DEPTH, D_FF, D_MODEL), D_FF ** -0.5),
        "norm_mix": gain(ks[9], (DEPTH, D_MODEL)),
        "w_mix_in": nrm(ks[10], (DEPTH, D_MODEL, MIX_IN_DIM), D_MODEL ** -0.5),
        "q_norm": gain(ks[11], (DEPTH, HEAD_DIM)),
        "k_norm": gain(ks[12], (DEPTH, HEAD_DIM)),
        "conv_w": nrm(ks[13], (DEPTH, CONV_K, CONV_DIM), CONV_K ** -0.5),
        "attn_out_norm": gain(ks[14], (DEPTH, ATTN_DIM)),
        "conv_out_norm": gain(ks[15], (DEPTH, CONV_DIM)),
        "w_mix_out": nrm(ks[16], (DEPTH, MIX_DIM, D_MODEL), MIX_DIM ** -0.5),
        "norm_ffn2": gain(ks[17], (DEPTH, D_MODEL)),
        "w_ffn2_in": nrm(ks[18], (DEPTH, D_MODEL, 2 * D_FF), D_MODEL ** -0.5),
        "w_ffn2_out": nrm(ks[19], (DEPTH, D_FF, D_MODEL), D_FF ** -0.5),
        "final_norm": gain(ks[20], (D_MODEL,)),
    }

def first_block(x, c, ctx, c_ctx, w_ada, b_ada, norm_ffn1, w_ffn1_in, w_ffn1_out,
              norm_mix, w_mix_in, q_norm, k_norm, conv_w, attn_out_norm, conv_out_norm,
              w_mix_out, norm_ffn2, w_ffn2_in, w_ffn2_out, final_norm):
    b, s, d = x.shape
    cos, sin = axial_rope_tables(s)

    for l in range(DEPTH):
        update_ctx = l < DEPTH - 1
        m = (jax.nn.silu(c) @ w_ada[l] + b_ada[l]).reshape(b, 1, N_MOD, d)
        mc = (jax.nn.silu(c_ctx) @ w_ada[l] + b_ada[l]).reshape(1, 1, N_MOD, d)

        x = x + 0.5 * m[:, :, 2] * swiglu(modulate(rmsnorm(x, norm_ffn1[l]), m[:, :, 0], m[:, :, 1]),
                                          w_ffn1_in[l], w_ffn1_out[l])
        ctx = ctx + 0.5 * mc[:, :, 2] * swiglu(modulate(rmsnorm(ctx, norm_ffn1[l]), mc[:, :, 0], mc[:, :, 1]),
                                               w_ffn1_in[l], w_ffn1_out[l])

        px = modulate(rmsnorm(x, norm_mix[l]), m[:, :, 3], m[:, :, 4]) @ w_mix_in[l]
        pc = modulate(rmsnorm(ctx, norm_mix[l]), mc[:, :, 3], mc[:, :, 4]) @ w_mix_in[l]
        q, k, v, gb, gc, u = split_heads(px, q_norm[l], k_norm[l])
        qc, kc, vc, gbc, gcc, uc = split_heads(pc, q_norm[l], k_norm[l])

        a = latent_attention(apply_rope(q, cos, sin), apply_rope(k, cos, sin), v, kc, vc)
        sc = gb * short_conv3(gc * u, conv_w[l])
        mix = jnp.concatenate([rmsnorm(a, attn_out_norm[l]), rmsnorm(sc, conv_out_norm[l])], axis=-1)
        x = x + m[:, :, 5] * (mix @ w_mix_out[l])

        if update_ctx:
            ac = context_attention(qc, kc, vc)
            scc = gbc * short_conv3(gcc * uc, conv_w[l])
            mixc = jnp.concatenate([rmsnorm(ac, attn_out_norm[l]), rmsnorm(scc, conv_out_norm[l])], axis=-1)
            ctx = ctx + mc[:, :, 5] * (mixc @ w_mix_out[l])
            ctx = ctx + 0.5 * mc[:, :, 8] * swiglu(modulate(rmsnorm(ctx, norm_ffn2[l]), mc[:, :, 6], mc[:, :, 7]),
                                                   w_ffn2_in[l], w_ffn2_out[l])

        x = x + 0.5 * m[:, :, 8] * swiglu(modulate(rmsnorm(x, norm_ffn2[l]), m[:, :, 6], m[:, :, 7]),
                                          w_ffn2_in[l], w_ffn2_out[l])

    return rmsnorm(x, final_norm)


CHUNK = 64
N_META = 16
DN_HEADS = 8
DN_DK = 128
DN_DV = 256
DN_CONV = 4
DN_QK = DN_HEADS * DN_DK
DN_V = DN_HEADS * DN_DV
SB_HEADS = 8
SB_DH = 128
SB_W = SB_HEADS * SB_DH
SB_BLOCK = 128
D_FF_2 = -(-8 * D_MODEL // (3 * 256)) * 256
PROJ_WIDTH = 2 * DN_QK + 2 * DN_V + 2 * DN_HEADS + 3 * SB_W + 2 * D_MODEL
RMS_EPS = 1e-6
L2_EPS = 1e-6


def _split_points():
    widths = (DN_QK, DN_QK, DN_V, DN_V, DN_HEADS, DN_HEADS, SB_W, SB_W, SB_W, D_MODEL, D_MODEL)
    return [int(s) for s in np.cumsum(widths)[:-1]]

def rmsnorm_2(x, gain):
    xf = x.astype(jnp.float32)
    y = xf * lax.rsqrt(jnp.mean(xf * xf, axis=-1, keepdims=True) + RMS_EPS)
    return (y * gain.astype(jnp.float32)).astype(x.dtype)

def l2norm(x):
    xf = x.astype(jnp.float32)
    return xf * lax.rsqrt(jnp.sum(xf * xf, axis=-1, keepdims=True) + L2_EPS)

def causal_depthwise_conv(x, w):
    K, C = w.shape
    return lax.conv_general_dilated(
        x, w[:, None, :].astype(x.dtype), window_strides=(1,), padding=[(K - 1, 0)],
        dimension_numbers=('NWC', 'WIO', 'NWC'), feature_group_count=C)

def gated_delta_rule(q, k, v, g, beta):
    B, T, H, DK = q.shape
    DV = v.shape[-1]
    N = T // CHUNK
    f32 = jnp.float32

    def to_chunks(a):
        a = a.astype(f32).reshape((B, N, CHUNK, H) + a.shape[3:])
        return jnp.moveaxis(a, (1, 3), (0, 2))

    q = to_chunks(q) * (DK ** -0.5)
    k = to_chunks(k)
    v = to_chunks(v)
    beta = to_chunks(beta)
    g = jnp.cumsum(to_chunks(g), axis=-1)
    idx = jnp.arange(CHUNK)
    incl = idx[:, None] >= idx[None, :]
    strict = idx[:, None] > idx[None, :]
    decay = jnp.exp(jnp.where(incl, g[..., :, None] - g[..., None, :], -jnp.inf))
    kb = k * beta[..., None]
    lower = jnp.where(strict, jnp.einsum('nbhid,nbhjd->nbhij', kb, k) * decay, 0.0)
    eye = jnp.eye(CHUNK, dtype=f32)
    rhs = jnp.concatenate([v * beta[..., None], kb * jnp.exp(g)[..., None]], axis=-1)
    sol = lax.linalg.triangular_solve(eye + lower, rhs, left_side=True, lower=True)
    u, w = sol[..., :DV], sol[..., DV:]
    attn = jnp.einsum('nbhid,nbhjd->nbhij', q, k) * decay
    q_dec = q * jnp.exp(g)[..., None]
    k_dec = k * jnp.exp(g[..., -1:] - g)[..., None]
    g_last = jnp.exp(g[..., -1])

    def step(S, xs):
        u_c, w_c, attn_c, qd_c, kd_c, gl_c = xs
        v_new = u_c - jnp.einsum('bhcd,bhde->bhce', w_c, S)
        o = jnp.einsum('bhcd,bhde->bhce', qd_c, S) + jnp.einsum('bhij,bhje->bhie', attn_c, v_new)
        S = S * gl_c[..., None, None] + jnp.einsum('bhcd,bhce->bhde', kd_c, v_new)
        return S, o

    S0 = jnp.zeros((B, H, DK, DV), f32)
    _, o = lax.scan(step, S0, (u, w, attn, q_dec, k_dec, g_last))
    return jnp.moveaxis(o, (0, 2), (1, 3)).reshape(B, T, H, DV)

def stick_breaking_attention(q, k, v):
    B, T, H, D = q.shape
    nq = -(-T // SB_BLOCK)
    Tp = nq * SB_BLOCK
    pad = ((0, 0), (0, Tp - T), (0, 0), (0, 0))
    f32 = jnp.float32
    qh = jnp.pad(q.astype(f32), pad).reshape(B, nq, SB_BLOCK, H, D).transpose(1, 0, 3, 2, 4)
    kh = jnp.pad(k.astype(f32), pad).transpose(0, 2, 1, 3)
    vh = jnp.pad(v.astype(f32), pad).transpose(0, 2, 1, 3)
    key_pos = jnp.arange(Tp)
    scale = D ** -0.5

    def block(args):
        q_blk, start = args
        z = jnp.einsum('bhqd,bhkd->bhqk', q_blk, kh) * scale
        q_pos = start + jnp.arange(SB_BLOCK)
        visible = key_pos[None, :] < q_pos[:, None]
        log_keep = jnp.where(visible, jax.nn.log_sigmoid(-z), 0.0)
        log_w = jax.nn.log_sigmoid(z) + lax.cumsum(log_keep, axis=3, reverse=True) - log_keep
        w = jnp.where(visible, jnp.exp(log_w), 0.0)
        return jnp.einsum('bhqk,bhkd->bhqd', w, vh)

    o = lax.map(block, (qh, jnp.arange(nq) * SB_BLOCK))
    return o.transpose(1, 0, 3, 2, 4).reshape(B, Tp, H, D)[:, :T]

def hybrid_mixer(hn, w_in, conv_q, conv_k, conv_v, a_log, dt_bias, dn_gain, sbq_gain, sbk_gain,
                 w_branch_dn, w_branch_sb, w_out):
    B, T, _ = hn.shape
    proj = hn @ w_in
    (dq, dk, dv, dz, da, db, sq, sk, sv, gate_dn, gate_sb) = jnp.split(proj, _split_points(), axis=-1)

    def heads(a, d):
        return a.reshape(B, T, -1, d)

    q = l2norm(heads(jax.nn.silu(causal_depthwise_conv(dq, conv_q)), DN_DK))
    k = l2norm(heads(jax.nn.silu(causal_depthwise_conv(dk, conv_k)), DN_DK))
    v = heads(jax.nn.silu(causal_depthwise_conv(dv, conv_v)), DN_DV)
    g = -jnp.exp(a_log.astype(jnp.float32)) * jax.nn.softplus(da.astype(jnp.float32) + dt_bias.astype(jnp.float32))
    beta = jax.nn.sigmoid(db.astype(jnp.float32))
    pad_l = (-N_META) % CHUNK
    pad_r = (-(T + pad_l)) % CHUNK

    def chunk_pad(a):
        return jnp.pad(a, ((0, 0), (pad_l, pad_r)) + ((0, 0),) * (a.ndim - 2))

    o_dn = gated_delta_rule(chunk_pad(q), chunk_pad(k), chunk_pad(v), chunk_pad(g), chunk_pad(beta))
    o_dn = o_dn[:, pad_l:pad_l + T]
    o_dn = rmsnorm_2(o_dn, dn_gain) * jax.nn.silu(heads(dz, DN_DV).astype(jnp.float32))
    o_dn = o_dn.astype(hn.dtype).reshape(B, T, DN_V)

    qs = rmsnorm_2(heads(sq, SB_DH), sbq_gain)
    ks = rmsnorm_2(heads(sk, SB_DH), sbk_gain)
    o_sb = stick_breaking_attention(qs, ks, heads(sv, SB_DH)).astype(hn.dtype).reshape(B, T, SB_W)

    merged = jax.nn.sigmoid(gate_dn) * (o_dn @ w_branch_dn) + jax.nn.sigmoid(gate_sb) * (o_sb @ w_branch_sb)
    return merged @ w_out

def swiglu_2(hn, w_ffn_in, w_ffn_out):
    gate, up = jnp.split(hn @ w_ffn_in, 2, axis=-1)
    return (jax.nn.silu(gate) * up) @ w_ffn_out

def second_inputs(seed: int = 0) -> dict:
    key = jax.random.key(seed)
    ks = jax.random.split(key, 20)
    f32 = jnp.float32

    def nrm(k, shape, fan_in):
        return jax.random.normal(k, shape, f32) * (fan_in ** -0.5)

    def gain(k, n):
        return 1.0 + 0.02 * jax.random.normal(k, (DEPTH, n), f32)

    dt = jnp.exp(jax.random.uniform(ks[7], (DEPTH, DN_HEADS), f32) * (math.log(0.1) - math.log(1e-3)) + math.log(1e-3))
    return {
        'x': jax.random.normal(ks[0], (BATCH, SEQ, D_MODEL), f32),
        'meta_tokens': jax.random.normal(ks[1], (N_META, D_MODEL), f32),
        'norm_mix_gain': gain(ks[2], D_MODEL),
        'w_in': nrm(ks[3], (DEPTH, D_MODEL, PROJ_WIDTH), D_MODEL),
        'conv_q': nrm(ks[4], (DEPTH, DN_CONV, DN_QK), DN_CONV),
        'conv_k': nrm(ks[5], (DEPTH, DN_CONV, DN_QK), DN_CONV),
        'conv_v': nrm(ks[6], (DEPTH, DN_CONV, DN_V), DN_CONV),
        'dn_a_log': jnp.log(jax.random.uniform(ks[8], (DEPTH, DN_HEADS), f32, 1.0, 16.0)),
        'dn_dt_bias': dt + jnp.log(-jnp.expm1(-dt)),
        'dn_out_norm_gain': gain(ks[9], DN_DV),
        'sb_q_norm_gain': gain(ks[10], SB_DH),
        'sb_k_norm_gain': gain(ks[11], SB_DH),
        'w_branch_dn': nrm(ks[12], (DEPTH, DN_V, D_MODEL), DN_V),
        'w_branch_sb': nrm(ks[13], (DEPTH, SB_W, D_MODEL), SB_W),
        'w_out': nrm(ks[14], (DEPTH, D_MODEL, D_MODEL), D_MODEL),
        'norm_ffn_gain': gain(ks[15], D_MODEL),
        'w_ffn_in': nrm(ks[16], (DEPTH, D_MODEL, 2 * D_FF_2), D_MODEL),
        'w_ffn_out': nrm(ks[17], (DEPTH, D_FF_2, D_MODEL), D_FF_2),
    }

def second_block(x, meta_tokens, norm_mix_gain, w_in, conv_q, conv_k, conv_v, dn_a_log, dn_dt_bias,
              dn_out_norm_gain, sb_q_norm_gain, sb_k_norm_gain, w_branch_dn, w_branch_sb, w_out,
              norm_ffn_gain, w_ffn_in, w_ffn_out):
    B = x.shape[0]
    meta = jnp.broadcast_to(meta_tokens[None].astype(x.dtype), (B, N_META, D_MODEL))
    h = jnp.concatenate([meta, x], axis=1)
    for l in range(DEPTH):
        h = h + hybrid_mixer(rmsnorm_2(h, norm_mix_gain[l]), w_in[l], conv_q[l], conv_k[l], conv_v[l],
                             dn_a_log[l], dn_dt_bias[l], dn_out_norm_gain[l], sb_q_norm_gain[l],
                             sb_k_norm_gain[l], w_branch_dn[l], w_branch_sb[l], w_out[l])
        h = h + swiglu_2(rmsnorm_2(h, norm_ffn_gain[l]), w_ffn_in[l], w_ffn_out[l])
    return h[:, N_META:]


def setup_inputs(seed=0):
    out = dict(first_inputs(seed))
    for name, value in second_inputs(seed + 1).items():
        if name != "x":
            out[name + "_2"] = value
    return out


def reference(
    x, c, ctx, c_ctx, w_ada, b_ada, norm_ffn1, w_ffn1_in, w_ffn1_out, norm_mix, w_mix_in,
    q_norm, k_norm, conv_w, attn_out_norm, conv_out_norm, w_mix_out, norm_ffn2, w_ffn2_in,
    w_ffn2_out, final_norm, meta_tokens_2, norm_mix_gain_2, w_in_2, conv_q_2, conv_k_2,
    conv_v_2, dn_a_log_2, dn_dt_bias_2, dn_out_norm_gain_2, sb_q_norm_gain_2, sb_k_norm_gain_2,
    w_branch_dn_2, w_branch_sb_2, w_out_2, norm_ffn_gain_2, w_ffn_in_2, w_ffn_out_2,
):
    x = first_block(
        x, c, ctx, c_ctx, w_ada, b_ada, norm_ffn1, w_ffn1_in, w_ffn1_out, norm_mix, w_mix_in,
        q_norm, k_norm, conv_w, attn_out_norm, conv_out_norm, w_mix_out, norm_ffn2, w_ffn2_in,
        w_ffn2_out, final_norm,
    )
    return second_block(
        x, meta_tokens_2, norm_mix_gain_2, w_in_2, conv_q_2, conv_k_2, conv_v_2, dn_a_log_2,
        dn_dt_bias_2, dn_out_norm_gain_2, sb_q_norm_gain_2, sb_k_norm_gain_2, w_branch_dn_2,
        w_branch_sb_2, w_out_2, norm_ffn_gain_2, w_ffn_in_2, w_ffn_out_2,
    )


_drawn_inputs = setup_inputs


def setup_inputs(seed=0):
    import zlib

    import numpy as np

    out = dict(_drawn_inputs(seed))
    spreads = {}
    factors = {'norm_ffn1': 5.793,
     'q_norm': 8.0,
     'k_norm': 8.0,
     'attn_out_norm': 4.316,
     'conv_out_norm': 4.358,
     'norm_ffn2': 6.478,
     'norm_mix_gain_2': 4.062,
     'dn_out_norm_gain_2': 8.0,
     'sb_q_norm_gain_2': 27.492,
     'sb_k_norm_gain_2': 26.957,
     'norm_ffn_gain_2': 12.953}
    for name, (base, spread) in spreads.items():
        noise = np.random.default_rng([zlib.crc32(name.encode()), seed]).standard_normal(out[name].shape)
        drawn = base * np.exp(spread * noise) if base else spread * noise
        out[name] = __import__('jax').numpy.asarray(drawn.astype(out[name].dtype))
    for name, factor in factors.items():
        out[name] = (out[name] * factor).astype(out[name].dtype)
    return out
```

```python
from contextlib import ExitStack

import concourse.bass as bass
from concourse import mybir

P = 128
F32 = mybir.dt.float32
F32R = mybir.dt.float32r
ALU = mybir.AluOpType
ACT = mybir.ActivationFunctionType
AX = mybir.AxisListType

D = 1024
KT = 8
TX = 512
TC = 256
T1 = TX + TC
T2 = 528
NH = 8
FF = 22
FF_PARTS = [(0, 8), (8, 7), (15, 7)]
CH = 128
EPS = 1e-6

SMALL = {}
_at = 0
for _name, _n in (("b_ada", 72), ("norm_ffn1", 8), ("norm_mix", 8), ("norm_ffn2", 8), ("final_norm", 8),
                  ("q_norm", 1), ("k_norm", 1), ("attn_out", 4), ("conv_out", 4), ("conv_w", 12),
                  ("norm_mix2", 8), ("norm_ffn_2", 8), ("conv_q", 32), ("conv_k", 32), ("conv_v", 64),
                  ("dn_gain", 2), ("sbq", 1), ("sbk", 1), ("a_log", 1), ("dt_bias", 1), ("c", 16)):
    SMALL[_name] = (_at, _n)
    _at += _n
NSMALL = _at

CONST = {}
_at = 0
for _name, _n in (("ident", 128), ("ones", 128), ("tri", 128), ("incl", 128), ("strict", 128),
                  ("level", 7 * 128)):
    CONST[_name] = (_at, _n)
    _at += _n
NCONST = _at
CONST1 = {"ones64": (0, 128), "rot": (128, 128), "cos": (256, 512), "sin": (768, 512)}
NCONST1 = 1280


def unit_plan():
    plan = []

    def ada(j):
        plan.extend(("w_ada", 8 * j + i, 8, False) for i in range(8))

    def ffn(n):
        for p, (f0, nf) in enumerate(FF_PARTS):
            for f in range(f0, f0 + nf):
                plan.append((f"w_in{n}", f, 8, True))
                plan.append((f"w_in{n}", FF + f, 8, True))
            plan.extend((f"w_out{n}_{p}", o, nf, True) for o in range(KT))

    ada(0)
    ada(1)
    ada(2)
    ffn(1)
    for j in range(3, 9):
        ada(j)
    plan.extend(("w_mix_in", i, 8, True) for i in range(19))
    plan.extend(("w_mix_out", i, 8, True) for i in range(8))
    ffn(2)
    plan.append(("w_proj", 0, 8, True))
    dn = [[("w_proj", 1 + 6 * h + i, 8, True) for i in range(6)] for h in range(NH)]
    dnb = [[("w_bdn", 2 * h + i, 8, True) for i in range(2)] for h in range(NH)]
    sb = [[("w_proj", 49 + 3 * h + i, 8, True) for i in range(3)] for h in range(NH)]
    sbb = [[("w_bsb", h, 8, True)] for h in range(NH)]
    plan += dn[0]
    for h in range(NH):
        nxt = dn[h + 1] if h + 1 < NH else []
        plan += nxt[:3] + (dnb[h - 1] if h else []) + nxt[3:]
    plan += dnb[NH - 1]
    plan += sb[0]
    for h in range(NH):
        if h == 0:
            plan += [("w_proj", 73 + i, 8, True) for i in range(8)]
        nxt = sb[h + 1] if h + 1 < NH else []
        plan += nxt[:1] + (sbb[h - 1] if h else []) + nxt[1:]
    plan += sbb[NH - 1]
    plan += [("w_proj", 81 + i, 8, True) for i in range(8)]
    plan += [("w_o2", i, 8, True) for i in range(8)]
    ffn(3)
    return plan


class Queues:

    def __init__(self, nc, ctx):
        self.nc = nc
        self.ctx = ctx
        self.engines = {"pe": nc.tensor, "act": nc.scalar, "dve": nc.vector, "pool": nc.gpsimd, "sp": nc.sync}
        self.queue = {e: [] for e in self.engines}
        self.sem = {e: self.semaphore(f"s_{e}") for e in ("pe", "act", "dve", "pool")}
        self.count = {e: 0 for e in self.sem}
        self.seen = {e: {} for e in self.engines}
        self.dma_count = {}

    def semaphore(self, name):
        return self.ctx.enter_context(self.nc.semaphore(name))

    def wait(self, eng, after):
        for tok in after:
            if tok is None:
                continue
            name, sem, value = tok
            if self.seen[eng].get(name, 0) < value:
                self.seen[eng][name] = value
                self.queue[eng].append(lambda e, sem=sem, value=value: e.wait_ge(sem, value))

    def do(self, eng, instruction, after=(), mark=True):
        if eng != "pe" and self.count[eng]:
            self.wait(eng, [self.last(eng)])
        self.wait(eng, after)
        if not mark:
            self.queue[eng].append(instruction)
            return None
        self.count[eng] += 1
        sem = self.sem[eng]
        self.queue[eng].append(lambda e: instruction(e).then_inc(sem, 1))
        return self.last(eng)

    def last(self, eng):
        return (eng, self.sem[eng], self.count[eng])

    def dma(self, eng, out, in_, name_sem, after=()):
        name, sem = name_sem
        self.wait(eng, after)
        self.dma_count[name] = self.dma_count.get(name, 0) + 16
        self.queue[eng].append(lambda e: e.dma_start(out, in_).then_inc(sem, 16))
        return (name, sem, self.dma_count[name])

    def barrier(self):
        toks = [self.last(e) for e in self.sem]
        for eng in self.sem:
            self.wait(eng, toks)

    def act(self, out, in_, func, after=(), **kw):
        return self.do("act", lambda e: e.activation(out, in_, func, **kw), after)

    def copy(self, out, in_, after=()):
        return self.act(out, in_, ACT.Copy, after)

    def tt(self, out, a, b, op, after=(), eng="dve"):
        return self.do(eng, lambda e: e.tensor_tensor(out, a, b, op), after)

    def ts(self, out, a, s1, s2, op0, op1, after=(), eng="dve"):
        if s2 is None:
            return self.do(eng, lambda e: e.tensor_scalar(out, a, s1, None, op0), after)
        return self.do(eng, lambda e: e.tensor_scalar(out, a, s1, s2, op0, op1), after)

    def stt(self, out, a, s, b, op0, op1, after=()):
        return self.do("dve", lambda e: e.scalar_tensor_tensor(out=out, in0=a, scalar=s, in1=b, op0=op0, op1=op1),
                       after)

    def mm(self, out, lhsT, rhs, start, stop, after=(), mark=True):
        return self.do("pe", lambda e: e.matmul(out, lhsT, rhs, start=start, stop=stop), after, mark)

    def tr(self, out, in_, ident, after=(), mark=True):
        return self.do("pe", lambda e: e.transpose(out, in_, ident), after, mark)


class Bank:

    def __init__(self, ap):
        self.ap = ap
        self.free = []


class Pool:
    def __init__(self, banks):
        self.banks = banks
        self.n = 0

    def take(self):
        b = self.banks[self.n % len(self.banks)]
        self.n += 1
        return b


class Weights:

    RAW = 4
    PARTS = 3
    AHEAD = 2

    def __init__(self, q, dram, plan):
        self.q, self.dram, self.plan = q, dram, plan
        sb = lambda name, dt: q.ctx.enter_context(q.nc.sbuf_tensor(name, [P, 8, P], dt))
        self.raw = [sb(f"w_raw{i}", F32) for i in range(self.RAW)]
        self.hi = [sb(f"w_hi{i}", F32R) for i in range(self.PARTS)]
        self.lo = [sb(f"w_lo{i}", F32R) for i in range(self.PARTS)]
        self.sems = [(f"s_w{i}", q.semaphore(f"s_w{i}")) for i in range(self.RAW)]
        self.loaded = []
        self.raw_free = {}
        self.part_free = []
        self.split = {}
        self.n_split = 0
        self.n_unit = 0
        self.used = 0
        self.now = None
        self.pump()

    def pump(self):
        while len(self.loaded) < len(self.plan):
            n = len(self.loaded)
            if n >= self.RAW and n - self.RAW not in self.raw_free:
                break
            name, i, nt, _ = self.plan[n]
            s = n % self.RAW
            self.loaded.append(self.q.dma("sp", self.raw[s][:, 0:nt, :].rearrange("p a b -> p (a b)"),
                                          self.dram[name][i], self.sems[s], self.raw_free.get(n - self.RAW, ())))

    def split_next(self):
        n = self.n_split
        self.n_split += 1
        name, i, nt, parts = self.plan[n]
        if not parts:
            return
        s = n % self.RAW
        m = self.used
        self.used += 1
        r = m % self.PARTS
        free = [self.part_free[m - self.PARTS]] if m >= self.PARTS else []
        raw, hi, lo = self.raw[s][:, 0:nt, :], self.hi[r][:, 0:nt, :], self.lo[r][:, 0:nt, :]
        t_hi = self.q.copy(hi, raw, [self.loaded[n], *free])
        t_lo = self.q.tt(lo, raw, hi.bitcast(F32), ALU.subtract, [self.loaded[n], t_hi, *free])
        self.raw_free[n] = (t_hi, t_lo)
        self.split[n] = (hi, lo, [t_hi, t_lo])
        self.pump()

    def next(self, key):
        n = self.n_unit
        self.n_unit += 1
        name, i, nt, parts = self.plan[n]
        assert (name, i) == key, (key, self.plan[n])
        while self.n_split < len(self.plan) and self.n_split <= n + self.AHEAD:
            if self.used - len(self.part_free) >= self.PARTS and self.plan[self.n_split][3]:
                break
            self.split_next()
        self.now = n
        if parts:
            return self.split[n]
        return self.raw[n % self.RAW][:, 0:nt, :], None, [self.loaded[n]]

    def release(self, tok):
        if self.plan[self.now][3]:
            self.part_free.append(tok)
        else:
            self.raw_free[self.now] = (tok,)
            self.pump()


def drive(main, filler, ratio):
    owed = 0.0
    for _ in main:
        owed += ratio
        while owed >= 1:
            owed -= 1
            if next(filler, "end") == "end":
                owed = -1e9
    for _ in filler:
        pass


def program(nc, ins, out):
    with ExitStack() as ctx:
        q = Queues(nc, ctx)
        build(q, ins, out)
        block = ctx.enter_context(nc.Block())
        for name, reg in (("pe", block.tensor), ("act", block.scalar), ("dve", block.vector),
                          ("pool", block.gpsimd), ("sp", block.sync)):
            def run(eng, name=name):
                for step in q.queue[name]:
                    step(eng)
            reg(run)


def build(q, ins, out):
    nc, ctx = q.nc, q.ctx

    def sb_in(c, name, shape, dt=F32):
        return c.enter_context(nc.sbuf_tensor(name, shape, dt))

    ps = ctx.enter_context(nc.psum_tensor("ps", [P, 8, 512], F32))
    flat = ps[:].rearrange("p a b -> p (a b)")
    small = sb_in(ctx, "small", [P, NSMALL])
    const = sb_in(ctx, "const", [P, NCONST])
    s_load = ("s_load", q.semaphore("s_load"))
    s_load2 = ("s_load2", q.semaphore("s_load2"))
    t_small = q.dma("act", small[:], ins["small"], s_load)
    W = Weights(q, ins, unit_plan())
    t_const = q.dma("act", const[:], ins["const"], s_load2)

    def sm(name, i=0, n=1, rows=(0, P)):
        a, _ = SMALL[name]
        return small[rows[0]:rows[1], a + i:a + i + n]

    def cs(name, r=P, n=P, i=0):
        a, _ = CONST[name]
        return const[0:r, a + i * P:a + i * P + n]

    def pairs(lo, hi):
        return Pool([Bank(flat[:, i * 1024:(i + 1) * 1024]) for i in range(lo, hi)])

    def singles(lo, hi):
        return Pool([Bank(ps[:, i, :]) for i in range(lo, hi)])

    def halves(ap, cols):
        if cols == COLS2:
            return ap.rearrange("p (a b) -> p a b", a=2)[:, :, 0:264]
        return ap[:, 0:sum(n for _, n in cols)]

    def as_halves(ap, cols):
        return ap.rearrange("p (a b) -> p a b", a=2) if cols == COLS2 else ap

    COLS1 = [(0, 512), (512, 256)]
    COLSX = [(0, 512)]
    COLS2 = [(0, 264), (264, 264)]

    def spot(cols, i):
        return (i * 512, cols[i][1])

    def product(key, xh, xl, cols, pool, after, tiles=None, pause=None):
        wh, wl, t_w = W.next(key)
        b = pool.take()
        nt = wh.shape[1]
        after = [*after, *t_w, *b.free]
        tok = None
        for i, (c0, n) in enumerate(cols):
            o0, _ = spot(cols, i)
            for k in range(nt):
                for p, (w, x) in enumerate(((wh, xh), (wh, xl), (wl, xh))):
                    end = i == len(cols) - 1 and k == nt - 1 and p == 2
                    tok = q.mm(b.ap[:, o0:o0 + n], w[:, k, :], x[:, k, c0:c0 + n], k == 0 and p == 0,
                               k == nt - 1 and p == 2, after, mark=end)
                    after = ()
        W.release(tok)
        return b, tok

    def parts(hi, lo, src, after=()):
        t = q.copy(hi, src, after)
        return q.tt(lo, src, hi.bitcast(F32), ALU.subtract, [t, *after])

    def rstd(src, scale, eps, v, t, y, after):
        a = q.ts(v, src, scale, eps, ALU.mult, ALU.add, after)
        b = q.act(t, v, ACT.Ln, [a])
        c = q.act(y, t, ACT.Exp, [b], scale=-0.5)
        q.tt(t, y, y, ALU.mult, [c])
        q.tt(t, t, v, ALU.mult)
        q.ts(t, t, -0.5, 1.5, ALU.mult, ALU.add)
        return a, q.tt(y, y, t, ALU.mult)

    def ada(j, pool, M, sc):
        b = pool.take()
        for i in range(8):
            w, _, t_w = W.next(("w_ada", 8 * j + i))
            for k in range(KT):
                tok = q.mm(b.ap[:, 2 * i:2 * i + 2], w[:, k, :], sc[:, 2 * k:2 * k + 2], k == 0, k == KT - 1,
                           [*t_w, *b.free, t_sc[0]] if k == 0 else (), mark=k == KT - 1)
            W.release(tok)
        bias = sm("b_ada", 8 * j, 8).unsqueeze(2).broadcast_to([P, 8, 2])
        b.free = [q.tt(M[:, j, :, :], b.ap[:, 0:16].rearrange("p (a b) -> p a b", b=2), bias, ALU.add, [tok])]
        return b.free[0]

    def norm(X, T, cols, groups, A, B, xh, xl, pool, tmp, after, t_mod=()):
        sq, v, t, y = tmp
        b = pool.take()
        freed = [None, None]
        for k in range(KT):
            a = q.act(sq[k % 2], X[:, k, :], ACT.Square, [*after, freed[k % 2]])
            for i, (c0, n) in enumerate(cols):
                o0, _ = spot(cols, i)
                tok = q.mm(b.ap[:, o0:o0 + n], cs("ones"), sq[k % 2][:, c0:c0 + n], k == 0, k == KT - 1,
                           [a, t_const, *b.free], mark=i == len(cols) - 1)
            freed[k % 2] = tok
        f, r = rstd(halves(b.ap, cols), 1.0 / D, EPS, as_halves(v, cols), as_halves(t, cols), as_halves(y, cols),
                    [tok])
        b.free = [f]
        last = r
        for k in range(KT):
            s = sq[k % 2]
            q.tt(s, X[:, k, :], y, ALU.mult, [r, tok])
            for g, (c0, n) in enumerate(groups):
                last = q.ts(s[:, c0:c0 + n], s[:, c0:c0 + n], A(k, g), B(k, g), ALU.mult, ALU.add, t_mod)
            if xh is not None:
                last = parts(xh[:, k, :], xl[:, k, :], s, [last])
        return last

    def ffn(name, X, T, cols, groups, xh, xl, hh, hl, gate, pool, tmp, t_x):
        s, hf = tmp
        t_h = None
        for p, (f0, nf) in enumerate(FF_PARTS):
            for f in range(f0, f0 + nf):
                b, tok = product((f"w_in{name}", f), xh, xl, cols, pool, [t_x])
                b.free = [q.act(as_halves(s[f % 2], cols), halves(b.ap, cols), ACT.Silu, [tok, t_h])]
                b2, tok2 = product((f"w_in{name}", FF + f), xh, xl, cols, pool, [t_x])
                m = q.tt(as_halves(hf[f % 2], cols), as_halves(s[f % 2], cols), halves(b2.ap, cols), ALU.mult,
                         [tok2, *b.free])
                b2.free = [m]
                t_h = parts(hh[:, f - f0, :], hl[:, f - f0, :], hf[f % 2], [m])
            for o in range(KT):
                b, tok = product((f"w_out{name}_{p}", o), hh, hl, cols, pool, [t_h])
                if gate is None:
                    x = as_halves(X[:, o, :], cols)
                    b.free = [q.tt(x, x, halves(b.ap, cols), ALU.add, [tok])]
                else:
                    for g, (c0, n) in enumerate(groups):
                        b.free = [q.stt(X[:, o, c0:c0 + n], b.ap[:, c0:c0 + n], gate(o, g), X[:, o, c0:c0 + n],
                                        ALU.mult, ALU.add, [tok])]
        return b.free[0]

    H = sb_in(ctx, "H", [P, KT, T2])
    s_meta = ("s_meta", q.semaphore("s_meta"))
    t_meta = q.dma("act", H[:, :, 0:16], ins["meta"], s_meta)
    G1 = [(0, TX), (TX, TC)]
    GX = [(0, TX)]
    with ExitStack() as b1:
        X = sb_in(b1, "X", [P, KT, T1])
        s_x = ("s_x", q.semaphore("s_x"))
        t_xin = q.dma("act", X[:].rearrange("p a b -> p (a b)"), ins["x"], s_x)
        M = sb_in(b1, "M", [P, 9, KT, 2])
        AM = sb_in(b1, "AM", [P, 3, KT, 2])
        GM = sb_in(b1, "GM", [P, 2, KT, 2])
        sc = sb_in(b1, "sc", [P, 16])
        t_sc = [q.act(sc[:], sm("c", 0, 16), ACT.Silu, [t_small])]

        def scales(i, j, gain):
            g = sm(gain, 0, 8).unsqueeze(2).broadcast_to([P, KT, 2])
            return q.stt(AM[:, i, :, :], M[:, j, :, :], 1.0, g, ALU.add, ALU.mult)

        def Af(i):
            return lambda k, g: AM[:, i, k, g:g + 1]

        def Bf(j):
            return lambda k, g: M[:, j, k, g:g + 1]

        def Gf(i):
            return lambda o, g: GM[:, i, o, g:g + 1]

        with ExitStack() as c:
            xh = sb_in(c, "f1_xh", [P, KT, T1], F32R)
            xl = sb_in(c, "f1_xl", [P, KT, T1], F32R)
            hh = sb_in(c, "f1_hh", [P, 8, T1], F32R)
            hl = sb_in(c, "f1_hl", [P, 8, T1], F32R)
            tm = [sb_in(c, f"f1_t{i}", [P, T1]) for i in range(4)]
            hf32 = [hh[:, i, :].bitcast(F32) for i in range(2)]
            pool = pairs(0, 4)
            for j in range(3):
                ada(j, pool, M, sc)
            scales(0, 1, "norm_ffn1")
            q.ts(GM[:, 0, :, :], M[:, 2, :, :], 0.5, None, ALU.mult, None)
            v5 = sb_in(c, "f1_v", [P, T1])
            t = norm(X, T1, COLS1, G1, Af(0), Bf(0), xh, xl, pool,
                     ([tm[0][:], tm[1][:]], v5[:], tm[2][:], tm[3][:]), [t_xin])
            ffn("1", X, T1, COLS1, G1, xh, xl, hh, hl, Gf(0), pool, ([tm[0][:], tm[1][:]], [tm[2][:], tm[3][:]]), t)
        q.barrier()

        with ExitStack() as c:
            const1 = sb_in(c, "const1", [P, NCONST1])
            s_c1 = ("s_c1", q.semaphore("s_c1"))
            t_c1 = q.dma("sp", const1[:], ins["const1"], s_c1, [q.last(e) for e in q.sem])

            def c1(name):
                a, n = CONST1[name]
                return const1[:, a:a + n]

            qT = sb_in(c, "qT", [P, 4, TX])
            kT = sb_in(c, "kT", [P, 2, T1])
            vp = sb_in(c, "vp", [P, 6, 4, P])
            mixc = sb_in(c, "mixc", [P, 4, TX])
            pool = pairs(0, 4)
            with ExitStack() as cc:
                xh = sb_in(cc, "m_xh", [P, KT, T1], F32R)
                xl = sb_in(cc, "m_xl", [P, KT, T1], F32R)
                tm = [sb_in(cc, f"m_t{i}", [P, T1]) for i in range(5)]
                gb = sb_in(cc, "gb", [P, TX])
                gc = sb_in(cc, "gc", [P, TX])
                cu = sb_in(cc, "cu", [P, TX + 2])
                q.do("dve", lambda e: e.memset(cu[:], 0.0))
                q.do("dve", lambda e: e.memset(vp[:], 0.0))
                for j in range(3, 9):
                    ada(j, pool, M, sc)
                scales(1, 4, "norm_mix")
                scales(2, 7, "norm_ffn2")
                q.ts(GM[:, 1, :, :], M[:, 8, :, :], 0.5, None, ALU.mult, None)
                t = norm(X, T1, COLS1, G1, Af(1), Bf(3), xh, xl, pool,
                         ([tm[0][:], tm[1][:]], tm[4][:], tm[2][:], tm[3][:]), [])

                def qk_norm(b, tok, dst, T, cols, gain):
                    raw, v, w, y = tm[0][:, 0:T], tm[1][:, 0:T], tm[2][:, 0:T], tm[3][:, 0:T]
                    sqv = tm[4][:, 0:T]
                    e = q.copy(raw, halves(b.ap, cols), [tok, q.last("dve")])
                    b.free = [e]
                    a = q.act(sqv, raw, ACT.Square, [e])
                    b2 = pool.take()
                    for i, (c0, n) in enumerate(cols):
                        m = q.mm(b2.ap[:, c0:c0 + n], c1("ones64"), sqv[:, c0:c0 + n], True, True,
                                 [a, t_c1, *b2.free])
                    f, r = rstd(b2.ap[:, 0:T], 1.0 / 64, EPS, v, w, y, [m])
                    b2.free = [f]
                    n1 = q.stt(raw, raw, gain, y, ALU.mult, ALU.mult, [r])
                    b3 = pool.take()
                    m = q.mm(b3.ap[:, 0:TX], c1("rot"), raw[:, 0:TX], True, True, [n1, *b3.free])
                    q.tt(v[:, 0:TX], raw[:, 0:TX], c1("cos"), ALU.mult)
                    x = q.tt(w[:, 0:TX], b3.ap[:, 0:TX], c1("sin"), ALU.mult, [m])
                    b3.free = [x]
                    if T > TX:
                        q.ts(dst[:, TX:T], raw[:, TX:T], 1.0, None, ALU.mult, None)
                    return q.tt(dst[:, 0:TX], v[:, 0:TX], w[:, 0:TX], ALU.add)

                for i in range(4):
                    b, tok = product(("w_mix_in", i), xh, xl, COLSX, pool, [t])
                    qk_norm(b, tok, qT[:, i, :], TX, COLSX, sm("q_norm"))
                for i in range(2):
                    b, tok = product(("w_mix_in", 4 + i), xh, xl, COLS1, pool, [t])
                    qk_norm(b, tok, kT[:, i, :], T1, COLS1, sm("k_norm"))
                b, tok = product(("w_mix_in", 6), xh, xl, COLS1, pool, [t])
                e = q.copy(tm[0][:], b.ap[:, 0:T1], [tok, q.last("dve")])
                b.free = [e]
                for half in range(2):
                    b = pool.take()
                    for i in range(3):
                        blk = 3 * half + i
                        m = q.tr(b.ap[:, i * P:(i + 1) * P], tm[0][:, blk * P:(blk + 1) * P], cs("ident"),
                                 [e, *b.free])
                    src = b.ap[:, 0:384].rearrange("p (a b) -> p a b", b=P)
                    for g in range(2):
                        for par in range(2):
                            b.free = [q.ts(vp[:, 3 * half:3 * half + 3, 2 * g + par, 64 * par:64 * par + 64],
                                           src[:, :, 64 * g:64 * g + 64], 1.0, None, ALU.mult, None, [m])]
                for i in range(4):
                    b, tok = product(("w_mix_in", 7 + 3 * i), xh, xl, COLSX, pool, [t])
                    b.free = [q.copy(gb[:], b.ap[:, 0:TX], [tok, q.last("dve")])]
                    b, tok = product(("w_mix_in", 8 + 3 * i), xh, xl, COLSX, pool, [t])
                    g = q.copy(gc[:], b.ap[:, 0:TX], [tok, q.last("dve")])
                    b.free = [g]
                    b, tok = product(("w_mix_in", 9 + 3 * i), xh, xl, COLSX, pool, [t])
                    b.free = [q.tt(cu[:, 1:TX + 1], gc[:], b.ap[:, 0:TX], ALU.mult, [tok, g])]
                    y = mixc[:, i, :]
                    q.ts(y, cu[:, 0:TX], sm("conv_w", i), None, ALU.mult, None)
                    q.stt(y, cu[:, 1:TX + 1], sm("conv_w", 4 + i), y, ALU.mult, ALU.add)
                    q.stt(y, cu[:, 2:TX + 2], sm("conv_w", 8 + i), y, ALU.mult, ALU.add)
                    q.tt(y, y, gb[:], ALU.mult)
            q.barrier()

            mixh = sb_in(c, "mixh", [P, KT, TX], F32R)
            mixl = sb_in(c, "mixl", [P, KT, TX], F32R)
            att = sb_in(c, "att", [P, 4, TX])
            PT = [sb_in(c, f"PT{i}", [P, 6, TX]) for i in range(2)]
            pr = [sb_in(c, f"pr{i}", [P, T1]) for i in range(2)]
            st = sb_in(c, "st", [P, 2, 4])
            pool = pairs(0, 3)
            poolo = singles(6, 8)
            n = 0
            pt_free = [None, None]
            pr_free = [None, None]
            for pair in range(4):
                g = pair // 2
                bo = poolo.take()
                for par in range(2):
                    r0 = 64 * par
                    h = 2 * pair + par
                    for qb in range(4):
                        z = n % 2
                        n += 1
                        b = pool.take()
                        for i, (c0, nn) in enumerate(COLS1):
                            m = q.mm(b.ap[:, c0:c0 + nn], qT[r0:r0 + 64, pair, qb * P:(qb + 1) * P],
                                     kT[r0:r0 + 64, g, c0:c0 + nn], True, True, b.free, mark=i == 1)
                        mx = q.do("dve", lambda e, z=z, b=b: e.reduce_max(st[:, z, 0:1], b.ap[:, 0:T1], AX.X),
                                  [m, q.last("act")])
                        nm = q.ts(st[:, z, 1:2], st[:, z, 0:1], -0.125, None, ALU.mult, None)
                        ex = q.act(pr[z][:], b.ap[:, 0:T1], ACT.Exp, [nm, pr_free[z]], bias=st[:, z, 1:2],
                                   scale=0.125, accum_out=st[:, z, 2:3])
                        b.free = [ex]
                        q.do("dve", lambda e, z=z: e.reciprocal(st[:, z, 3:4], st[:, z, 2:3]), [ex])
                        nr = q.ts(pr[z][:], pr[z][:], st[:, z, 3:4], None, ALU.mult, None)
                        b = pool.take()
                        for i in range(6):
                            o0 = i * P if i < 3 else 512 + (i - 3) * P
                            m = q.tr(b.ap[:, o0:o0 + P], pr[z][:, i * P:(i + 1) * P], cs("ident"),
                                     [nr, *b.free], mark=i == 5)
                        pr_free[z] = m
                        src = b.ap.rearrange("p (a b) -> p a b", a=2)[:, :, 0:384].rearrange(
                            "p a (b c) -> p a b c", c=P)
                        dst = PT[h % 2][:, :, qb * P:(qb + 1) * P].rearrange("p (a b) c -> p a b c", a=2)
                        for a in range(2):
                            ev = q.copy(dst[:, a], src[:, a], [m, pt_free[h % 2]])
                        b.free = [ev]
                    for i in range(6):
                        m = q.mm(bo.ap, vp[:, i, 2 * g + par, :], PT[h % 2][:, i, :], par == 0 and i == 0,
                                 par == 1 and i == 5, [ev, *bo.free], mark=i == 5)
                    pt_free[h % 2] = m
                bo.free = [q.ts(att[:, pair, :], bo.ap, 1.0, None, ALU.mult, None, [m])]
            tv = [PT[0][:, i, :] for i in range(6)]
            for half, (src, gain) in enumerate(((att, "attn_out"), (mixc, "conv_out"))):
                b = pool.take()
                for k in range(4):
                    a = q.act(tv[k], src[:, k, :], ACT.Square, [q.last("dve"), q.last("pe")])
                    m = q.mm(b.ap[:, 0:TX], cs("ones"), tv[k], k == 0, k == 3, [a, *b.free])
                f, r = rstd(b.ap[:, 0:TX], 1.0 / 512, EPS, tv[4], tv[5], pr[0][:, 0:TX], [m])
                b.free = [f]
                for k in range(4):
                    y = q.stt(tv[k], src[:, k, :], sm(gain, k), pr[0][:, 0:TX], ALU.mult, ALU.mult, [m])
                    t = parts(mixh[:, 4 * half + k, :], mixl[:, 4 * half + k, :], tv[k], [y])
            for o in range(KT):
                b, tok = product(("w_mix_out", o), mixh, mixl, COLSX, pool, [t])
                b.free = [q.stt(X[:, o, 0:TX], b.ap[:, 0:TX], M[:, 5, o, 0:1], X[:, o, 0:TX], ALU.mult, ALU.add,
                                [tok])]
        q.barrier()

        with ExitStack() as c:
            xh = sb_in(c, "f2_xh", [P, KT, TX], F32R)
            xl = sb_in(c, "f2_xl", [P, KT, TX], F32R)
            hh = sb_in(c, "f2_hh", [P, 8, TX], F32R)
            hl = sb_in(c, "f2_hl", [P, 8, TX], F32R)
            tm = [sb_in(c, f"f2_t{i}", [P, TX]) for i in range(5)]
            pool = pairs(0, 4)
            XV = X[:, :, 0:TX]
            t = norm(XV, TX, COLSX, GX, Af(2), Bf(6), xh, xl, pool,
                     ([tm[0][:], tm[1][:]], tm[4][:], tm[2][:], tm[3][:]), [])
            t = ffn("2", XV, TX, COLSX, GX, xh, xl, hh, hl, Gf(1), pool,
                    ([tm[0][:], tm[1][:]], [tm[2][:], tm[3][:]]), t)
            sqt = [tm[0][:], tm[1][:]]
            b = pool.take()
            for k in range(KT):
                a = q.act(sqt[k % 2], XV[:, k, :], ACT.Square, [t, q.last("pe")])
                m = q.mm(b.ap[:, 0:TX], cs("ones"), sqt[k % 2], k == 0, k == KT - 1, [a, *b.free])
            f, r = rstd(b.ap[:, 0:TX], 1.0 / D, EPS, tm[4][:], tm[2][:], tm[3][:], [m])
            for k in range(KT):
                t_h = q.stt(H[:, k, 16:T2], XV[:, k, :], sm("final_norm", k), tm[3][:], ALU.mult, ALU.mult,
                            [t_meta])
    q.barrier()

    zeros = None

    def norm2(gain, xh, xl, pool, tmp):
        sq, v, t, y = tmp
        b = pool.take()
        freed = [None, None]
        for k in range(KT):
            a = q.act(sq[k % 2], H[:, k, :], ACT.Square, [freed[k % 2], q.last("dve")])
            for i, (c0, n) in enumerate(COLS2):
                m = q.mm(b.ap[:, 512 * i:512 * i + n], cs("ones"), sq[k % 2][:, c0:c0 + n], k == 0, k == KT - 1,
                         [a, *b.free])
            freed[k % 2] = m
        f, r = rstd(halves(b.ap, COLS2), 1.0 / D, EPS, as_halves(v, COLS2), as_halves(t, COLS2),
                    as_halves(y, COLS2), [m])
        b.free = [f]
        for k in range(KT):
            s = q.stt(sq[k % 2], H[:, k, :], sm(gain, k), y, ALU.mult, ALU.mult, [r, m])
            last = parts(xh[:, k, :], xl[:, k, :], sq[k % 2], [s])
        return last

    with ExitStack() as b2:
        acc = sb_in(b2, "acc", [P, KT, T2])
        with ExitStack() as c:
            hh_ = sb_in(c, "n_h", [P, KT, T2], F32R)
            hl_ = sb_in(c, "n_l", [P, KT, T2], F32R)
            pool = pairs(0, 2)
            chain = singles(4, 8)
            rm = [sb_in(c, f"r{i}", [P, T2]) for i in range(5)]
            t_n = norm2("norm_mix2", hh_, hl_, pool, ([rm[0][:], rm[1][:]], rm[2][:], rm[3][:], rm[4][:]))
            with ExitStack() as d:
                delta_net(q, d, sb_in, ins, hh_, hl_, t_n, acc, pool, chain, rm, product, rstd, parts, sm, cs,
                          halves, as_halves, COLS2, W)
            q.barrier()
            accs = sb_in(c, "accs", [P, KT, T2])
            with ExitStack() as d:
                stick(q, d, sb_in, hh_, hl_, t_n, acc, accs, pool, chain, rm, product, rstd, parts, sm, cs,
                      halves, as_halves, COLS2, W)
            q.barrier()
        with ExitStack() as c:
            mh = sb_in(c, "g_h", [P, KT, T2], F32R)
            ml = sb_in(c, "g_l", [P, KT, T2], F32R)
            pool = pairs(0, 4)
            for k in range(KT):
                t = parts(mh[:, k, :], ml[:, k, :], acc[:, k, :])
            for o in range(KT):
                b, tok = product(("w_o2", o), mh, ml, COLS2, pool, [t])
                x = as_halves(H[:, o, :], COLS2)
                b.free = [q.tt(x, x, halves(b.ap, COLS2), ALU.add, [tok])]
    q.barrier()
    with ExitStack() as c:
        xh = sb_in(c, "f3_xh", [P, KT, T2], F32R)
        xl = sb_in(c, "f3_xl", [P, KT, T2], F32R)
        hh = sb_in(c, "f3_hh", [P, 8, T2], F32R)
        hl = sb_in(c, "f3_hl", [P, 8, T2], F32R)
        tm = [sb_in(c, f"f3_t{i}", [P, T2]) for i in range(5)]
        pool = pairs(0, 4)
        t = norm2("norm_ffn_2", xh, xl, pool, ([tm[0][:], tm[1][:]], tm[4][:], tm[2][:], tm[3][:]))
        t = ffn("3", H, T2, COLS2, None, xh, xl, hh, hl, None, pool,
                ([tm[0][:], tm[1][:]], [tm[2][:], tm[3][:]]), t)
        s_out = ("s_out", q.semaphore("s_out"))
        t = q.dma("sp", out, H[:, :, 16:T2], s_out, [t])
        q.wait("sp", [t])


def delta_net(q, ctx, sb_in, ins, hn_h, hn_l, t_n, acc, pool, chain, rm, product, rstd, parts, sm, cs,
              halves, as_halves, COLS2, W):
    FULL = [(0, P, 4)]
    GROUPS = [(0, P, 4), (4, 16, 1)]
    SIZES = [P] * 4 + [16]
    sel = sb_in(ctx, "sel", [64, NH * P])
    s_sel = ("s_sel", q.semaphore("s_sel"))
    t_sel = q.dma("sp", sel[:], ins["sel"], s_sel, [q.last(e) for e in q.sem])
    gbt = sb_in(ctx, "gbt", [64, T2])
    gcol = sb_in(ctx, "gcol", [P, 5, 40])
    nb = sb_in(ctx, "nb", [P, 5, 40])
    q.do("dve", lambda e: e.memset(gbt[:], 0.0))
    b, tok = product(("w_proj", 0), hn_h, hn_l, COLS2, pool, [t_n])
    za, ea, la = (rm[i][0:8, :] for i in range(3))
    eb = rm[3][32:40, :]
    ha = lambda ap: as_halves(ap, COLS2)
    q.ts(ha(za), halves(b.ap, COLS2)[0:8], sm("dt_bias", 0, 1, (0, 8)), None, ALU.add, None, [tok])
    q.stt(ea, za, -1.0, za, ALU.mult, ALU.max)
    f = q.ts(ha(eb), halves(b.ap, COLS2)[32:40], -1.0, None, ALU.mult, None)
    b.free = [f]
    t = q.act(ea, ea, ACT.Exp, [f], scale=-1.0)
    t = q.act(la, ea, ACT.Ln, [t], bias=1.0)
    e2 = q.act(eb, eb, ACT.Exp, [f])
    al = rm[4][0:8, 0:1]
    t = q.act(al, sm("a_log", 0, 1, (0, 8)), ACT.Exp)
    q.ts(za, za, 0.0, None, ALU.max, None)
    q.tt(za, za, la, ALU.add, [t])
    q.ts(za, za, al, -1.0, ALU.mult, ALU.mult)
    q.do("dve", lambda e: e.memset(ea, 1.0))
    for c, n in enumerate(SIZES):
        s = slice(c * P, c * P + n)
        q.do("dve", lambda e, s=s: e.tensor_tensor_scan(gbt[0:8, s], ea[:, s], za[:, s], 0.0, ALU.mult, ALU.add))
    q.ts(eb, eb, 1.0, None, ALU.add, None)
    t_g = q.do("dve", lambda e: e.reciprocal(gbt[32:40, :], eb))
    b = pool.take()
    for c, n in enumerate(SIZES):
        m = q.tr(b.ap[0:n, 40 * c:40 * c + 40], gbt[0:40, c * P:c * P + n], cs("ident", 40, 40), [t_g, *b.free])
    for c0, n, C in GROUPS:
        src = b.ap[0:n, 40 * c0:40 * (c0 + C)].rearrange("p (a b) -> p a b", b=40)
        q.ts(gcol[0:n, c0:c0 + C, :], src, 1.0, None, ALU.mult, None, [m])
        t_col = q.ts(nb[0:n, c0:c0 + C, :], src, -1.0, None, ALU.mult, None)
    b.free = [t_col]

    F = [[sb_in(ctx, f"dnf{s}_{i}", [P, T2]) for i in range(6)] for s in range(2)]
    craw = sb_in(ctx, "craw", [P, T2 + 3])
    q.do("dve", lambda e: e.memset(craw[:], 0.0))
    ready = [None, None]
    used = [None, None]

    def project(h):
        s = h % 2
        for i in range(6):
            b, tok = product(("w_proj", 1 + 6 * h + i), hn_h, hn_l, COLS2, pool, [])
            dst = F[s][i][:]
            if i < 4:
                e = q.copy(ha(craw[:, 3:T2 + 3]), halves(b.ap, COLS2), [tok, q.last("dve")])
                b.free = [e]
                name, base = (("conv_q", h), ("conv_k", h), ("conv_v", 2 * h), ("conv_v", 2 * h + 1))[i]
                tiles = 16 if name == "conv_v" else 8
                q.ts(dst, craw[:, 0:T2], sm(name, base), None, ALU.mult, None, [e, used[s]])
                for j in range(1, 4):
                    t = q.stt(dst, craw[:, j:j + T2], sm(name, j * tiles + base), dst, ALU.mult, ALU.add)
                t = q.act(dst, dst, ACT.Silu, [t])
            else:
                t = q.act(ha(dst), halves(b.ap, COLS2), ACT.Silu, [tok, used[s]])
                b.free = [t]
            ready[s] = t
            yield
        for i in range(2):
            sqv = rm[0][:]
            a = q.act(sqv, F[s][i][:], ACT.Square, [q.last("dve"), q.last("pe")])
            b = pool.take()
            for j, (c0, n) in enumerate(COLS2):
                m = q.mm(b.ap[:, 512 * j:512 * j + n], cs("ones"), sqv[:, c0:c0 + n], True, True, [a, *b.free])
            f, r = rstd(halves(b.ap, COLS2), 1.0, EPS, ha(rm[0][:]), ha(rm[1][:]), ha(rm[2][:]), [m])
            b.free = [f]
            ready[s] = q.stt(F[s][i][:], F[s][i][:], float(P) ** -0.5 if i == 0 else 1.0, rm[2][:], ALU.mult,
                             ALU.mult, [ready[s]])
            yield

    gB = sb_in(ctx, "gB", [P, T2])
    bB = sb_in(ctx, "bB", [P, T2])
    DT = sb_in(ctx, "DT", [P, 5, P])
    AT = sb_in(ctx, "AT", [P, 5, P])
    LT = sb_in(ctx, "LT", [P, 5, P])
    LM = [sb_in(ctx, f"LM{i}", [P, 5, P]) for i in range(2)]
    U = sb_in(ctx, "U", [P, 5, P])
    Tm = sb_in(ctx, "Tm", [P, 5, P])
    Xm = sb_in(ctx, "Xm", [P, 5, P])
    kd = sb_in(ctx, "kd", [P, 5, P])
    vb = sb_in(ctx, "vb", [P, 5, 2 * P])
    ekd = sb_in(ctx, "ekd", [P, 5])
    S = sb_in(ctx, "S", [P, 2 * P])
    R = sb_in(ctx, "R", [P, 2 * P])
    V = sb_in(ctx, "V", [P, 2 * P])
    O = sb_in(ctx, "O", [P, 2, T2])
    oh = [sb_in(ctx, f"oh{i}", [P, 2, T2], F32R) for i in range(1)]
    ol = [sb_in(ctx, f"ol{i}", [P, 2, T2], F32R) for i in range(1)]
    t_o = [None]
    o_free = [None]

    def tok3(ap, c0, n, C):
        return ap[:, c0 * P:c0 * P + C * n].rearrange("p (a b) -> p a b", b=n)

    def delta(h):
        s = h % 2
        qf, kf, v0, v1, z0, z1 = (F[s][i][:] for i in range(6))
        for dst, r in ((gB, 0), (bB, 32)):
            for i, (c0, n) in enumerate(COLS2):
                b = chain.take()
                m = q.mm(b.ap[:, 0:n], sel[r:r + 8, h * P:(h + 1) * P], gbt[r:r + 8, c0:c0 + n], True, True,
                         [t_g, t_sel, *b.free])
                t_b = q.copy(dst[:, c0:c0 + n], b.ap[:, 0:n], [m, q.last("dve"), q.last("pe")])
                b.free = [t_b]
        yield
        for c0, n, C in GROUPS:
            g3 = tok3(gB[0:n, :], c0, n, C)
            col = gcol[0:n, c0:c0 + C, h:h + 1]
            dt = DT[0:n, c0:c0 + C, 0:n]
            q.tt(dt, g3, col.broadcast_to([n, C, n]), ALU.subtract, [t_b, t_col])
            t = q.ts(dt, dt, 0.0, None, ALU.min, None)
            t = q.act(dt, dt, ACT.Exp, [t])
            q.tt(dt, dt, cs("incl", n, n).unsqueeze(1).broadcast_to([n, C, n]), ALU.mult, [t])
            last = tok3(gB[0:n, :], c0, n, C)[:, :, n - 1:n]
            q.tt(ekd[0:n, c0:c0 + C].unsqueeze(2), last, col, ALU.subtract)
        t_e = q.last("dve")
        for c0, n, C in GROUPS:
            t_kd = q.act(ekd[0:n, c0:c0 + C], ekd[0:n, c0:c0 + C], ACT.Exp, [t_e])
        t_eg = q.act(gB[:], gB[:], ACT.Exp, [t_e])
        yield
        for src, dst, w in ((kf, kd, 0), (v0, vb, 0), (v1, vb, P)):
            for c0, n, C in GROUPS:
                b = chain.take()
                for c in range(C):
                    m = q.tr(b.ap[0:n, c * P:(c + 1) * P], src[:, (c0 + c) * P:(c0 + c) * P + n], cs("ident"),
                             [ready[s], *b.free])
                ps3 = b.ap[0:n, 0:C * P].rearrange("p (a b) -> p a b", b=P)
                if dst is kd:
                    sc = ekd[0:n, c0:c0 + C].unsqueeze(2).broadcast_to([n, C, P])
                else:
                    sc = gcol[0:n, c0:c0 + C, 32 + h:33 + h].broadcast_to([n, C, P])
                b.free = [q.tt(dst[0:n, c0:c0 + C, w:w + P], ps3, sc, ALU.mult, [m, t_kd])]
            yield
        for c0, n, C in GROUPS:
            b, b2 = chain.take(), chain.take()
            for c in range(C):
                cc = slice((c0 + c) * P, (c0 + c) * P + n)
                m = q.mm(b.ap[0:n, c * n:(c + 1) * n], kf[:, cc], kf[:, cc], True, True, [ready[s], *b.free])
            for c in range(C):
                cc = slice((c0 + c) * P, (c0 + c) * P + n)
                m2 = q.mm(b2.ap[0:n, c * n:(c + 1) * n], kf[:, cc], qf[:, cc], True, True, [ready[s], *b2.free])
            dt, at, lt = (a[0:n, c0:c0 + C, 0:n] for a in (DT, AT, LT))
            v3 = lambda bb: bb.ap[0:n, 0:C * n].rearrange("p (a b) -> p a b", b=n)
            b.free = [q.tt(lt, v3(b), dt, ALU.mult, [m])]
            b2.free = [q.tt(at, v3(b2), dt, ALU.mult, [m2])]
            q.tt(lt, lt, tok3(bB[0:n, :], c0, n, C), ALU.mult)
            t_lt = q.tt(lt, lt, cs("strict", n, n).unsqueeze(1).broadcast_to([n, C, n]), ALU.mult)
        yield
        t_q = q.tt(qf, qf, gB[:], ALU.mult, [t_eg])
        t_k = q.tt(kf, kf, gB[:], ALU.mult)

        def level(i, n):
            return cs("level", n, n, i)

        for c0, n, C in GROUPS:
            lt, u, tm_ = (a[0:n, c0:c0 + C, 0:n] for a in (LT, U, Tm))
            q.tt(u, lt, level(0, n).unsqueeze(1).broadcast_to([n, C, n]), ALU.mult)
            t_u = q.tt(u, cs("ident", n, n).unsqueeze(1).broadcast_to([n, C, n]), u, ALU.subtract)
            b = chain.take()
            for c in range(C):
                m = q.tr(b.ap[0:n, c * n:(c + 1) * n], U[0:n, c0 + c, 0:n], cs("ident", n, n), [t_u, *b.free])
            t_t = q.copy(tm_, b.ap[0:n, 0:C * n].rearrange("p (a b) -> p a b", b=n), [m])
            b.free = [t_t]
        m_x = None
        lm_used = [None, None]
        for i in range(1, 7):
            todo = [g for g in GROUPS if g[1] > (1 << i)]
            lm = LM[i % 2]
            for c0, n, C in todo:
                t_lm = q.tt(lm[0:n, c0:c0 + C, 0:n], LT[0:n, c0:c0 + C, 0:n],
                            level(i, n).unsqueeze(1).broadcast_to([n, C, n]), ALU.mult,
                            [t_lt, lm_used[i % 2]], eng="pool")
            for c0, n, C in todo:
                v3 = lambda bb: bb.ap[0:n, 0:C * n].rearrange("p (a b) -> p a b", b=n)
                b = chain.take()
                for c in range(C):
                    m = q.mm(b.ap[0:n, c * n:(c + 1) * n], lm[0:n, c0 + c, 0:n], Tm[0:n, c0 + c, 0:n], True, True,
                             [t_lm, t_t, *b.free], mark=c == C - 1)
                lm_used[i % 2] = m
                t_x = q.copy(Xm[0:n, c0:c0 + C, 0:n], v3(b), [m, m_x])
                b.free = [t_x]
                yield
                bu, bt = chain.take(), chain.take()
                last_level = (2 << i) >= n
                for c in range(C):
                    m = q.mm(bu.ap[0:n, c * n:(c + 1) * n], Xm[0:n, c0 + c, 0:n], U[0:n, c0 + c, 0:n], True, True,
                             [t_x, t_u, *bu.free], mark=c == C - 1)
                m_x = m
                if not last_level:
                    for c in range(C):
                        m2 = q.mm(bt.ap[0:n, c * n:(c + 1) * n], U[0:n, c0 + c, 0:n], Xm[0:n, c0 + c, 0:n], True,
                                  True, bt.free, mark=c == C - 1)
                    m_x = m2
                    t_t = q.tt(Tm[0:n, c0:c0 + C, 0:n], Tm[0:n, c0:c0 + C, 0:n], v3(bt), ALU.subtract, [m2])
                    bt.free = [t_t]
                t_u = q.tt(U[0:n, c0:c0 + C, 0:n], U[0:n, c0:c0 + C, 0:n], v3(bu), ALU.subtract, [m, m_x])
                bu.free = [t_u]
                yield
        t_s = None
        for c, n in enumerate(SIZES):
            cc = slice(c * P, c * P + n)
            if c:
                b = chain.take()
                m = q.mm(b.ap[0:n, 0:256], kf[:, cc], S[:], True, True, [t_k, t_s, *b.free])
                t_r = q.stt(R[0:n, :], b.ap[0:n, 0:256], nb[0:n, c, 32 + h:33 + h], vb[0:n, c, :], ALU.mult,
                            ALU.add, [m])
                b.free = [t_r]
                rhs = R[0:n, :]
                yield
            else:
                rhs, t_r = vb[0:n, c, :], t_u
            b = chain.take()
            m = q.mm(b.ap[0:n, 0:256], U[0:n, c, 0:n], rhs, True, True, [t_r, t_u, *b.free])
            t_v = q.copy(V[0:n, :], b.ap[0:n, 0:256], [m])
            b.free = [t_v]
            b = chain.take()
            for x in range(2):
                o = b.ap[:, x * P:x * P + n]
                if c:
                    q.mm(o, S[:, x * P:(x + 1) * P], qf[:, cc], True, False, [t_q, *b.free], mark=False)
                m = q.mm(o, V[0:n, x * P:(x + 1) * P], AT[0:n, c, 0:n], c == 0, True, [t_v, *b.free])
            t_o[0] = q.ts(O[:, :, cc], b.ap[:, 0:2 * P].rearrange("p (a b) -> p a b", a=2)[:, :, 0:n], 1.0, None,
                          ALU.mult, None, [m])
            b.free = [t_o[0]]
            if c < 4:
                b = chain.take()
                m2 = q.mm(b.ap[:, 0:256], kd[0:n, c, :], V[0:n, :], True, True, b.free)
                if c:
                    t_s = q.stt(S[:], S[:], gB[:, c * P + n - 1:c * P + n], b.ap[:, 0:256], ALU.mult, ALU.add,
                                [m2])
                else:
                    t_s = q.ts(S[:], b.ap[:, 0:256], 1.0, None, ALU.mult, None, [m2])
                b.free = [t_s]
            yield
        bb = [chain.take(), chain.take()]
        for x in range(2):
            a = q.act(rm[3][:], O[:, x, :], ACT.Square, [t_o[0], q.last("pe")])
            for i, (c0, n) in enumerate(COLS2):
                m = q.mm(bb[i].ap[:, 0:n], cs("ones"), rm[3][:, c0:c0 + n], x == 0, x == 1, [a, *bb[i].free])
        yield
        for i, (c0, n) in enumerate(COLS2):
            f, r = rstd(bb[i].ap[:, 0:n], 1.0 / 256, EPS, kf[:, c0:c0 + n], qf[:, c0:c0 + n],
                        rm[4][:, c0:c0 + n], [m])
            bb[i].free = [f]
        for x, z in enumerate((z0, z1)):
            q.stt(O[:, x, :], O[:, x, :], sm("dn_gain", x), rm[4][:], ALU.mult, ALU.mult, [r])
            w = q.tt(O[:, x, :], O[:, x, :], z, ALU.mult)
            t_o[0] = parts(oh[0][:, x, :], ol[0][:, x, :], O[:, x, :], [w, o_free[0]])
        used[s] = t_o[0]
        yield

    def branch(h, t_in, first):
        xh, xl = oh[0], ol[0]
        for u in range(2):
            wh, wl, t_w = W.next(("w_bdn", 2 * h + u))
            for j in range(4):
                o = 4 * u + j
                b = pool.take()
                for i, (c0, n) in enumerate(COLS2):
                    for k in range(2):
                        for p, (w, x) in enumerate(((wh, xh), (wh, xl), (wl, xh))):
                            tok = q.mm(b.ap[:, 512 * i:512 * i + n], w[:, 2 * j + k, :], x[:, k, c0:c0 + n],
                                       k == 0 and p == 0, k == 1 and p == 2, [*t_w, t_in, *b.free],
                                       mark=k == 1 and p == 2)
                if j == 3:
                    W.release(tok)
                a = ha(acc[:, o, :])
                if first:
                    b.free = [q.ts(a, halves(b.ap, COLS2), 1.0, None, ALU.mult, None, [tok])]
                else:
                    b.free = [q.tt(a, a, halves(b.ap, COLS2), ALU.add, [tok])]
            yield
        o_free[0] = tok

    for _ in project(0):
        pass
    for h in range(NH):
        def filler(h=h, t_prev=t_o[0]):
            p = project(h + 1) if h + 1 < NH else iter(())
            for _ in zip(range(3), p):
                yield
            if h:
                yield from branch(h - 1, t_prev, h == 1)
            yield from p
        drive(delta(h), filler(), 0.5)
    for _ in branch(NH - 1, t_o[0], False):
        pass


def stick(q, ctx, sb_in, hn_h, hn_l, t_n, acc, accs, pool, chain, rm, product, rstd, parts, sm, cs,
          halves, as_halves, COLS2, W):
    SIZES = [P] * 4 + [16]
    ha = lambda ap: as_halves(ap, COLS2)
    Fs = [[sb_in(ctx, f"sbf{s}_{i}", [P, T2]) for i in range(3)] for s in range(2)]
    vt = sb_in(ctx, "vt", [P, 5, P])
    Z = sb_in(ctx, "Z", [P, 5, T2])
    SP = sb_in(ctx, "SP", [P, 5, T2])
    oh = sb_in(ctx, "sbh", [P, 1, T2], F32R)
    ol = sb_in(ctx, "sbl", [P, 1, T2], F32R)
    oc = sb_in(ctx, "oc", [P, T2])
    ready, used = [None, None], [None, None]
    t_o = [None]
    o_free = [None]

    def gates(base, a, add):
        for o in range(KT):
            b, tok = product(("w_proj", base + o), hn_h, hn_l, COLS2, pool, [t_n])
            e = q.act(ha(rm[0][:]), halves(b.ap, COLS2), ACT.Exp, [tok, q.last("dve")], scale=-1.0)
            b.free = [e]
            q.ts(rm[0][:], rm[0][:], 1.0, None, ALU.add, None, [e])
            q.do("dve", lambda e: e.reciprocal(rm[1][:], rm[0][:]))
            t = q.tt(a[:, o, :], a[:, o, :], rm[1][:], ALU.mult)
            if add is not None:
                t = q.tt(add[:, o, :], add[:, o, :], a[:, o, :], ALU.add)
            yield

    def project(h):
        s = h % 2
        for i in range(3):
            b, tok = product(("w_proj", 49 + 3 * h + i), hn_h, hn_l, COLS2, pool, [])
            dst = Fs[s][i][:]
            e = q.copy(ha(dst), halves(b.ap, COLS2), [tok, used[s]])
            b.free = [e]
            ready[s] = e
            yield
            if i < 2:
                a = q.act(rm[2][:], dst, ACT.Square, [q.last("dve"), q.last("pe")])
                b = pool.take()
                for j, (c0, n) in enumerate(COLS2):
                    m = q.mm(b.ap[:, 512 * j:512 * j + n], cs("ones"), rm[2][:, c0:c0 + n], True, True,
                             [a, *b.free])
                f, r = rstd(halves(b.ap, COLS2), 1.0 / P, EPS, ha(rm[2][:]), ha(rm[0][:]), ha(rm[1][:]), [m])
                b.free = [f]
                t = q.stt(dst, dst, sm("sbq" if i == 0 else "sbk"), rm[1][:], ALU.mult, ALU.mult, [r])
                if i == 0:
                    t = q.ts(dst, dst, float(P) ** -0.5, None, ALU.mult, None)
                yield
        ready[s] = t

    def head(h):
        s = h % 2
        qf, kf, vf = (Fs[s][i][:] for i in range(3))
        for c0, n, C in ((0, P, 4), (4, 16, 1)):
            b = chain.take()
            for c in range(C):
                m = q.tr(b.ap[0:n, c * P:(c + 1) * P], vf[:, (c0 + c) * P:(c0 + c) * P + n], cs("ident"),
                         [q.last("act"), ready[s], *b.free])
            b.free = [q.copy(vt[0:n, c0:c0 + C, :], b.ap[0:n, 0:C * P].rearrange("p (a b) -> p a b", b=P), [m])]
        t_vt = b.free[0]

        def spans(jb):
            lo = jb * P
            if T2 - lo > 512:
                return [(lo, 264), (lo + 264, 264)]
            return [(lo, T2 - lo)]

        zc = {}
        for jb, n in enumerate(SIZES):
            for c0, w in spans(jb):
                b = chain.take()
                m = q.mm(b.ap[0:n, 0:w], kf[:, jb * P:jb * P + n], qf[:, c0:c0 + w], True, True,
                         [ready[s], *b.free])
                z, sp = Z[0:n, jb, c0:c0 + w], SP[0:n, jb, c0:c0 + w]
                e = q.copy(z, b.ap[0:n, 0:w], [m, q.last("pe"), q.last("dve")])
                e = q.act(sp, b.ap[0:n, 0:w], ACT.Abs)
                b.free = [e]
            lo = jb * P
            z, sp = Z[0:n, jb, lo:T2], SP[0:n, jb, lo:T2]
            t = q.act(sp, sp, ACT.Exp, [q.last("dve")], scale=-1.0)
            t = q.act(sp, sp, ACT.Ln, [t], bias=1.0)
            q.stt(sp, z, 0.0, sp, ALU.max, ALU.add, [t])
            zc[jb] = q.tt(SP[0:n, jb, lo:lo + n], SP[0:n, jb, lo:lo + n], cs("strict", n, n), ALU.mult)
            yield
        for jb, n in enumerate(SIZES):
            for c0, w in spans(jb):
                b = chain.take()
                terms = [(cs("tri", n, n), jb, c0, w)]
                for j2 in range(jb + 1, 5):
                    a = max(c0, j2 * P)
                    if a < c0 + w:
                        terms.append((cs("ones", SIZES[j2], n), j2, a, c0 + w - a))
                for i, (lhs, j2, a, ww) in enumerate(terms):
                    m = q.mm(b.ap[0:n, a - c0:a - c0 + ww], lhs, SP[0:SIZES[j2], j2, a:a + ww], i == 0,
                             i == len(terms) - 1, [zc[4], *b.free], mark=i == len(terms) - 1)
                z = Z[0:n, jb, c0:c0 + w]
                b.free = [q.tt(z, z, b.ap[0:n, 0:w], ALU.subtract, [m])]
            lo = jb * P
            d = Z[0:n, jb, lo:lo + n]
            t = q.ts(d, d, 0.0, None, ALU.min, None)
            t = q.act(Z[0:n, jb, lo:T2], Z[0:n, jb, lo:T2], ACT.Exp, [t])
            zc[jb] = q.tt(d, d, cs("strict", n, n), ALU.mult, [t])
            yield
        for c0, w in ((0, 264), (264, 264)):
            b = chain.take()
            terms = []
            for jb in range(5):
                a = max(c0, jb * P)
                if a < c0 + w:
                    terms.append((jb, a, c0 + w - a))
            for i, (jb, a, ww) in enumerate(terms):
                m = q.mm(b.ap[:, a - c0:a - c0 + ww], vt[0:SIZES[jb], jb, :], Z[0:SIZES[jb], jb, a:a + ww], i == 0,
                         i == len(terms) - 1, [t_vt, zc[4], *b.free], mark=i == len(terms) - 1)
            e = q.copy(oc[:, c0:c0 + w], b.ap[:, 0:w], [m, q.last("dve")])
            b.free = [e]
        t_o[0] = parts(oh[:, 0, :], ol[:, 0, :], oc[:], [e, o_free[0]])
        used[s] = m
        yield

    def branch(h, t_in):
        wh, wl, t_w = W.next(("w_bsb", h))
        for o in range(KT):
            b = pool.take()
            for i, (c0, n) in enumerate(COLS2):
                for p, (w, x) in enumerate(((wh, oh), (wh, ol), (wl, oh))):
                    tok = q.mm(b.ap[:, 512 * i:512 * i + n], w[:, o, :], x[:, 0, c0:c0 + n], p == 0, p == 2,
                               [*t_w, t_in, *b.free], mark=p == 2)
            a = ha(accs[:, o, :])
            if h == 0:
                b.free = [q.ts(a, halves(b.ap, COLS2), 1.0, None, ALU.mult, None, [tok])]
            else:
                b.free = [q.tt(a, a, halves(b.ap, COLS2), ALU.add, [tok])]
        W.release(tok)
        o_free[0] = tok
        yield

    for _ in project(0):
        pass
    for h in range(NH):
        def filler(h=h, t_prev=t_o[0]):
            if h == 0:
                yield from gates(73, acc, None)
            p = project(h + 1) if h + 1 < NH else iter(())
            for _ in zip(range(1), p):
                yield
            if h:
                yield from branch(h - 1, t_prev)
            yield from p
        drive(head(h), filler(), 1.0)
    for _ in branch(NH - 1, t_o[0]):
        pass
    for _ in gates(81, accs, acc):
        pass


def _tiles(np, w, rows=None):
    k, n = w.shape
    return np.ascontiguousarray(w.reshape(k // P, P, n // P, P).transpose(2, 1, 0, 3)).reshape(n // P, P, k)


def _constants(np):
    i = np.arange(P)
    c = np.zeros((P, NCONST), np.float32)

    def put(name, a, at=0):
        c[:, CONST[name][0] + at:CONST[name][0] + at + a.shape[1]] = a

    put("ident", np.eye(P, dtype=np.float32))
    put("ones", np.ones((P, P), np.float32))
    put("tri", (i[:, None] >= i[None, :]).astype(np.float32))
    put("incl", (i[None, :] >= i[:, None]).astype(np.float32))
    put("strict", (i[None, :] > i[:, None]).astype(np.float32))
    for lv in range(7):
        b = 1 << lv
        m = (i[:, None] // (2 * b) == i[None, :] // (2 * b)) & ((i[:, None] // b) % 2 == 0) & \
            ((i[None, :] // b) % 2 == 1)
        put("level", m.astype(np.float32), lv * P)
    c1 = np.zeros((P, NCONST1), np.float32)
    c1[:, 0:128] = (i[:, None] // 64 == i[None, :] // 64)
    rot = np.zeros((P, P), np.float32)
    for a in range(0, P, 2):
        rot[a + 1, a] = -1.0
        rot[a, a + 1] = 1.0
    c1[:, 128:256] = rot
    tok = np.arange(TX)
    inv = (np.float32(10000.0) ** (-np.arange(16, dtype=np.float32) / np.float32(16))).astype(np.float32)
    row = (tok // 64).astype(np.float32)
    col = (tok % 64).astype(np.float32)
    ang = np.concatenate([row[:, None] * inv, col[:, None] * inv], axis=-1).astype(np.float32)
    pos = (i % 64) // 2
    c1[:, 256:768] = np.cos(ang).T[pos]
    c1[:, 768:1280] = np.sin(ang).T[pos]
    sel = np.zeros((64, NH * P), np.float32)
    for h in range(NH):
        sel[h, h * P:(h + 1) * P] = 1.0
        sel[32 + h, h * P:(h + 1) * P] = 1.0
    return c, c1, sel


def kernel(**inputs):
    import numpy as np
    import concourse.bacc as bacc
    from concourse.bass_utils import run_bass_kernel_spmd

    g = {k: np.asarray(v) for k, v in inputs.items()}

    def cols(v):
        return v.reshape(-1, P).T

    def feat(x):
        return x.T.reshape(KT, P, -1).transpose(1, 0, 2)

    a = {}
    sm = np.zeros((P, NSMALL), np.float32)

    def put(name, v, rows=P):
        s, n = SMALL[name]
        sm[0:rows, s:s + n] = v

    put("b_ada", cols(g["b_ada"][0]))
    put("norm_ffn1", cols(g["norm_ffn1"][0]))
    put("norm_mix", cols(g["norm_mix"][0]))
    put("norm_ffn2", cols(g["norm_ffn2"][0]))
    put("final_norm", cols(g["final_norm"]))
    put("q_norm", np.concatenate([g["q_norm"][0]] * 2)[:, None])
    put("k_norm", np.concatenate([g["k_norm"][0]] * 2)[:, None])
    put("attn_out", cols(g["attn_out_norm"][0]))
    put("conv_out", cols(g["conv_out_norm"][0]))
    put("conv_w", cols(g["conv_w"][0].reshape(-1)))
    put("norm_mix2", cols(g["norm_mix_gain_2"][0]))
    put("norm_ffn_2", cols(g["norm_ffn_gain_2"][0]))
    for n in "qkv":
        put("conv_" + n, cols(g[f"conv_{n}_2"][0].reshape(-1)))
    put("dn_gain", cols(g["dn_out_norm_gain_2"][0]))
    put("sbq", g["sb_q_norm_gain_2"][0][:, None])
    put("sbk", g["sb_k_norm_gain_2"][0][:, None])
    put("a_log", g["dn_a_log_2"][0][:, None], NH)
    put("dt_bias", g["dn_dt_bias_2"][0][:, None], NH)
    put("c", np.stack([cols(g["c"][0]), cols(g["c_ctx"])], axis=2).reshape(P, 16))
    a["small"] = sm
    a["const"], a["const1"], a["sel"] = _constants(np)
    a["x"] = np.concatenate([feat(g["x"][0]), feat(g["ctx"][0])], axis=2).reshape(P, -1)
    a["meta"] = np.ascontiguousarray(feat(g["meta_tokens_2"]))

    a["w_ada"] = _tiles(np, g["w_ada"][0])
    for n, wi, wo in (("1", "w_ffn1_in", "w_ffn1_out"), ("2", "w_ffn2_in", "w_ffn2_out"),
                      ("3", "w_ffn_in_2", "w_ffn_out_2")):
        a[f"w_in{n}"] = _tiles(np, g[wi][0])
        for p, (f0, nf) in enumerate(FF_PARTS):
            a[f"w_out{n}_{p}"] = _tiles(np, g[wo][0][f0 * P:(f0 + nf) * P])
    w = g["w_mix_in"][0]
    k0, k1 = w[:, 512:576], w[:, 576:640]
    order = [w[:, 0:512], k0, k0, k1, k1, w[:, 640:768]]
    for i in range(4):
        for base in (768, 1280, 1792):
            order.append(w[:, base + i * P:base + (i + 1) * P])
    a["w_mix_in"] = _tiles(np, np.concatenate(order, axis=1))
    a["w_mix_out"] = _tiles(np, g["w_mix_out"][0])
    w = g["w_in_2"][0]
    z = np.zeros((D, 24), np.float32)
    order = [w[:, 6144:6152], z, w[:, 6152:6160], z, np.zeros((D, 64), np.float32)]
    for h in range(NH):
        order += [w[:, h * P:(h + 1) * P], w[:, 1024 + h * P:1024 + (h + 1) * P],
                  w[:, 2048 + 256 * h:2048 + 256 * (h + 1)], w[:, 4096 + 256 * h:4096 + 256 * (h + 1)]]
    for h in range(NH):
        order += [w[:, 6160 + 1024 * j + h * P:6160 + 1024 * j + (h + 1) * P] for j in range(3)]
    order.append(w[:, 9232:11280])
    a["w_proj"] = _tiles(np, np.concatenate(order, axis=1))
    w = g["w_branch_dn_2"][0].reshape(NH, 2, P, 2, 4, P)
    a["w_bdn"] = np.ascontiguousarray(w.transpose(0, 3, 2, 4, 1, 5)).reshape(2 * NH, P, 8 * P)
    a["w_bsb"] = np.ascontiguousarray(g["w_branch_sb_2"][0]).reshape(NH, P, 8 * P)
    a["w_o2"] = _tiles(np, g["w_out_2"][0])

    nc = bacc.Bacc("TRN2", target_bir_lowering=False, num_devices=1)
    ins = {n: nc.dram_tensor("in_" + n, v.shape, F32, kind="ExternalInput").ap() for n, v in a.items()}
    out = nc.dram_tensor("out", (P, KT, TX), F32, kind="ExternalOutput").ap()
    program(nc, ins, out)
    r = run_bass_kernel_spmd(nc, [{"in_" + n: v for n, v in a.items()}], core_ids=[0])
    y = r.results[0]["out"]
    return np.ascontiguousarray(y.transpose(1, 0, 2).reshape(D, TX).T).reshape(1, TX, D)
```

```python
from contextlib import ExitStack

import concourse.bass as bass
from concourse import mybir

BASE = 16512
TOP = 229344
P = 128
F32 = mybir.dt.float32
F32R = mybir.dt.float32r
ALU = mybir.AluOpType
ACT = mybir.ActivationFunctionType
AX = mybir.AxisListType

D = 1024
KT = 8
TX = 512
TC = 256
T1 = TX + TC
T2 = 528
NH = 8
FF = 22
FF_PARTS = [(0, 8), (8, 7), (15, 7)]
CH = 128
EPS = 1e-6

SMALL = {}
_at = 0
for _name, _n in (("b_ada", 72), ("norm_ffn1", 8), ("norm_mix", 8), ("norm_ffn2", 8), ("final_norm", 8),
                  ("q_norm", 1), ("k_norm", 1), ("attn_out", 4), ("conv_out", 4), ("conv_w", 12),
                  ("norm_mix2", 8), ("norm_ffn_2", 8), ("conv_q", 32), ("conv_k", 32), ("conv_v", 64),
                  ("dn_gain", 2), ("sbq", 1), ("sbk", 1), ("a_log", 1), ("dt_bias", 1), ("c", 16)):
    SMALL[_name] = (_at, _n)
    _at += _n
NSMALL = _at

CONST = {}
_at = 0
for _name, _n in (("ident", 128), ("ones", 128), ("tri", 128), ("incl", 128), ("strict", 128),
                  ("level", 7 * 128)):
    CONST[_name] = (_at, _n)
    _at += _n
NCONST = _at
CONST1 = {"ones64": (0, 128), "rot": (128, 128), "cos": (256, 512), "sin": (768, 512)}
NCONST1 = 1280


def unit_plan():
    plan = []

    def ada(j):
        plan.extend(("w_ada", 8 * j + i, 8, False) for i in range(8))


    def ffn(n):
        for p, (f0, nf) in enumerate(FF_PARTS):
            for f in range(f0, f0 + nf):
                plan.append((f"w_in{n}", f, 8, True))
                plan.append((f"w_in{n}", FF + f, 8, True))
            plan.extend((f"w_out{n}_{p}", o, nf, True) for o in range(KT))

    for j in range(4):
        ada(j)
    ffn(1)
    ada(4)
    ada(5)
    ada(6)
    ada(7)
    plan.extend(("w_mix_in", i, 8, True) for i in range(19))
    ada(8)
    plan.extend(("w_mix_out", i, 8, True) for i in range(8))
    ffn(2)
    plan.append(("w_proj", 0, 8, True))
    dn = [[("w_proj", 1 + 6 * h + i, 8, True) for i in range(6)] for h in range(NH)]
    dnb = [[("w_bdn", 2 * h + i, 8, True) for i in range(2)] for h in range(NH)]
    sb = [[("w_proj", 49 + 3 * h + i, 8, True) for i in range(3)] for h in range(NH)]
    sbb = [[("w_bsb", h, 8, True)] for h in range(NH)]
    plan += dn[0]
    for h in range(NH):
        nxt = dn[h + 1] if h + 1 < NH else []
        plan += nxt[:3] + (dnb[h - 1] if h else []) + nxt[3:]
    plan += dnb[NH - 1]
    plan += sb[0]
    plan += [("w_proj", 73 + i, 8, True) for i in range(8)]
    plan += sb[1]
    for h in range(NH):
        nxt = sb[h + 2] if h + 2 < NH else []
        plan += nxt[:1] + (sbb[h - 1] if h else []) + nxt[1:]
    plan += sbb[NH - 1]
    plan += [("w_proj", 81 + i, 8, True) for i in range(8)]
    plan += [("w_o2", i, 8, True) for i in range(8)]
    ffn(3)
    return plan


class Queues:

    def __init__(self, nc, ctx):
        self.nc = nc
        self.ctx = ctx
        self.engines = {"pe": nc.tensor, "act": nc.scalar, "dve": nc.vector, "pool": nc.gpsimd, "sp": nc.sync}
        self.queue = {e: [] for e in self.engines}
        self.sem = {e: self.semaphore(f"s_{e}") for e in ("pe", "act", "dve", "pool")}
        self.count = {e: 0 for e in self.sem}
        self.seen = {e: {} for e in self.engines}
        self.dma_count = {}
        self.table = None

    def semaphore(self, name):
        return self.ctx.enter_context(self.nc.semaphore(name))

    def wait(self, eng, after):
        for tok in after:
            if tok is None:
                continue
            name, sem, value = tok
            if self.seen[eng].get(name, 0) < value:
                self.seen[eng][name] = value
                self.queue[eng].append(lambda e, sem=sem, value=value: e.wait_ge(sem, value))

    def do(self, eng, instruction, after=(), mark=True):
        if eng != "pe" and self.count[eng]:
            self.wait(eng, [self.last(eng)])
        self.wait(eng, after)
        if not mark:
            self.queue[eng].append(instruction)
            return None
        self.count[eng] += 1
        sem = self.sem[eng]
        self.queue[eng].append(lambda e: instruction(e).then_inc(sem, 1))
        return self.last(eng)

    def last(self, eng):
        return (eng, self.sem[eng], self.count[eng])

    def dma(self, eng, out, in_, name_sem, after=()):
        name, sem = name_sem
        self.wait(eng, after)
        self.dma_count[name] = self.dma_count.get(name, 0) + 16
        self.queue[eng].append(lambda e: e.dma_start(out, in_).then_inc(sem, 16))
        return (name, sem, self.dma_count[name])

    def act(self, out, in_, func, after=(), **kw):
        if func in (ACT.Exp, ACT.Ln) and self.table != "exp":
            self.queue["act"].append(lambda e: e.preload_act_table_set("natural_log_exp_and_others"))
            self.table = "exp"
        elif func in (ACT.Silu, ACT.Sigmoid):
            self.table = func
        return self.do("act", lambda e: e.activation(out, in_, func, **kw), after)

    def copy(self, out, in_, after=()):
        return self.act(out, in_, ACT.Copy, after)

    def tt(self, out, a, b, op, after=(), eng="dve"):
        return self.do(eng, lambda e: e.tensor_tensor(out, a, b, op), after)

    def ts(self, out, a, s1, s2, op0, op1, after=(), eng="dve"):
        if s2 is None:
            return self.do(eng, lambda e: e.tensor_scalar(out, a, s1, None, op0), after)
        return self.do(eng, lambda e: e.tensor_scalar(out, a, s1, s2, op0, op1), after)

    def stt(self, out, a, s, b, op0, op1, after=()):
        return self.do("dve", lambda e: e.scalar_tensor_tensor(out=out, in0=a, scalar=s, in1=b, op0=op0, op1=op1),
                       after)

    def mm(self, out, lhsT, rhs, start, stop, after=(), mark=True):
        return self.do("pe", lambda e: e.matmul(out, lhsT, rhs, start=start, stop=stop), after, mark)

    def tr(self, out, in_, ident, after=(), mark=True):
        return self.do("pe", lambda e: e.transpose(out, in_, ident), after, mark)


class Mem:

    def __init__(self, nc, at):
        self.nc, self.at = nc, at

    def put(self, name, shape, dt=F32):
        n = 4
        for d in shape[1:]:
            n *= d
        t = self.nc.alloc_sbuf_tensor_at(name, shape, dt, offset=self.at)
        self.at += (n + 31) // 32 * 32
        assert self.at <= TOP, (name, self.at - TOP)
        return t


class Bank:

    def __init__(self, ap):
        self.ap = ap
        self.free = []


class Pool:
    def __init__(self, banks):
        self.banks = banks
        self.n = 0

    def take(self):
        b = self.banks[self.n % len(self.banks)]
        self.n += 1
        return b


class Weights:

    RAW = 4
    PARTS = 3
    AHEAD = 2

    def __init__(self, q, mem, dram, plan):
        self.q, self.dram, self.plan = q, dram, plan
        sb = lambda name, dt: mem.put(name, [P, 8, P], dt)
        self.raw = [sb(f"w_raw{i}", F32) for i in range(self.RAW)]
        self.hi = [sb(f"w_hi{i}", F32R) for i in range(self.PARTS)]
        self.lo = [sb(f"w_lo{i}", F32R) for i in range(self.PARTS)]
        self.sems = [(f"s_w{i}", q.semaphore(f"s_w{i}")) for i in range(self.RAW)]
        self.loaded = []
        self.raw_free = {}
        self.part_free = []
        self.split = {}
        self.n_split = 0
        self.n_unit = 0
        self.used = 0
        self.now = None
        self.lo_engine = "dve"
        self.pump()

    def pump(self):
        while len(self.loaded) < len(self.plan):
            n = len(self.loaded)
            if n >= self.RAW and n - self.RAW not in self.raw_free:
                break
            name, i, nt, _ = self.plan[n]
            s = n % self.RAW
            self.loaded.append(self.q.dma("sp", self.raw[s][:, 0:nt, :].rearrange("p a b -> p (a b)"),
                                          self.dram[name][i], self.sems[s], self.raw_free.get(n - self.RAW, ())))

    def split_next(self):
        n = self.n_split
        self.n_split += 1
        name, i, nt, parts = self.plan[n]
        if not parts:
            return
        s = n % self.RAW
        m = self.used
        self.used += 1
        r = m % self.PARTS
        free = [self.part_free[m - self.PARTS]] if m >= self.PARTS else []
        raw, hi, lo = self.raw[s][:, 0:nt, :], self.hi[r][:, 0:nt, :], self.lo[r][:, 0:nt, :]
        t_hi = self.q.copy(hi, raw, [self.loaded[n], *free])
        t_lo = self.q.tt(lo, raw, hi.bitcast(F32), ALU.subtract, [self.loaded[n], t_hi, *free], eng=self.lo_engine)
        self.raw_free[n] = (t_hi, t_lo)
        self.split[n] = (hi, lo, [t_hi, t_lo])
        self.pump()

    def next(self, key):
        n = self.n_unit
        self.n_unit += 1
        name, i, nt, parts = self.plan[n]
        assert (name, i) == key, (key, self.plan[n])
        while self.n_split < len(self.plan) and self.n_split <= n + self.AHEAD:
            if self.used - len(self.part_free) >= self.PARTS and self.plan[self.n_split][3]:
                break
            self.split_next()
        self.now = n
        if parts:
            return self.split[n]
        return self.raw[n % self.RAW][:, 0:nt, :], None, [self.loaded[n]]

    def release(self, tok):
        if self.plan[self.now][3]:
            self.part_free.append(tok)
        else:
            self.raw_free[self.now] = (tok,)
            self.pump()


def drive(main, filler, ratio):
    owed = 0.0
    for _ in main:
        owed += ratio
        while owed >= 1:
            owed -= 1
            if next(filler, "end") == "end":
                owed = -1e9
    for _ in filler:
        pass


def run(steps):
    while True:
        try:
            next(steps)
        except StopIteration as e:
            return e.value


def program(nc, ins, out):
    with ExitStack() as ctx:
        q = Queues(nc, ctx)
        build(q, ins, out)
        block = ctx.enter_context(nc.Block())
        for name, reg in (("pe", block.tensor), ("act", block.scalar), ("dve", block.vector),
                          ("pool", block.gpsimd), ("sp", block.sync)):
            def run(eng, name=name):
                for step in q.queue[name]:
                    step(eng)
            reg(run)


COLS1 = [(0, 512), (512, 256)]
COLSX = [(0, 512)]
COLS2 = [(0, 264), (264, 264)]


def halves(ap, cols):
    if cols == COLS2:
        return ap.rearrange("p (a b) -> p a b", a=2)[:, :, 0:264]
    return ap[:, 0:sum(n for _, n in cols)]


def as_halves(ap, cols):
    return ap.rearrange("p (a b) -> p a b", a=2) if cols == COLS2 else ap


class Ops:

    def __init__(self, q, mem, ins):
        self.q = q
        self.small = mem.put("small", [P, NSMALL])
        self.const = mem.put("const", [P, NCONST])
        self.t_small = q.dma("act", self.small[:], ins["small"], ("s_load", q.semaphore("s_load")))
        self.t_const = q.dma("act", self.const[:], ins["const"], ("s_load2", q.semaphore("s_load2")))

    def sm(self, name, i=0, n=1, rows=(0, P)):
        a, _ = SMALL[name]
        return self.small[rows[0]:rows[1], a + i:a + i + n]

    def cs(self, name, r=P, n=P, i=0):
        a, _ = CONST[name]
        return self.const[0:r, a + i * P:a + i * P + n]

    def product_steps(self, key, xh, xl, cols, pool, ready):
        q = self.q
        wh, wl, t_w = self.W.next(key)
        b = pool.take()
        nt = wh.shape[1]
        tok = None
        for k in range(nt):
            after = [*(t_w if k == 0 else ()), *(b.free if k == 0 else ()),
                     ready[k] if isinstance(ready, list) else ready]
            for i, (c0, n) in enumerate(cols):
                for p, (w, x) in enumerate(((wh, xh), (wh, xl), (wl, xh))):
                    end = i == len(cols) - 1 and k == nt - 1 and p == 2
                    tok = q.mm(b.ap[:, i * 512:i * 512 + n], w[:, k, :], x[:, k, c0:c0 + n], k == 0 and p == 0,
                               k == nt - 1 and p == 2, after, mark=end)
                    after = ()
            if k < nt - 1:
                yield
        self.W.release(tok)
        return b, tok

    def product(self, *args):
        return run(self.product_steps(*args))

    def parts(self, hi, lo, src, after=(), eng="dve"):
        t = self.q.copy(hi, src, after)
        return self.q.tt(lo, src, hi.bitcast(F32), ALU.subtract, [t, *after], eng=eng)

    def rstd(self, src, scale, eps, v, t, y, after):
        q = self.q
        a = q.ts(v, src, scale, eps, ALU.mult, ALU.add, after)
        b = q.act(t, v, ACT.Ln, [a])
        c = q.act(y, t, ACT.Exp, [b], scale=-0.5)
        q.stt(t, y, -0.5, v, ALU.mult, ALU.mult, [c])
        q.tt(t, t, y, ALU.mult)
        return a, q.stt(y, t, 1.5, y, ALU.add, ALU.mult)


class Stats:

    def __init__(self, o, acc, sq, cols):
        self.o, self.acc, self.sq, self.cols = o, acc, sq, cols
        self.n = 0
        self.free = [None, None]
        self.t = None

    def add(self, src, after):
        q, i = self.o.q, self.n % 2
        if self.n == 0:
            self.t = q.act(self.acc, src, ACT.Square, after)
        else:
            a = q.act(self.sq[i], src, ACT.Square, [*after, self.free[i]])
            self.t = q.tt(self.acc, self.acc, self.sq[i], ALU.add, [a, self.t], eng="pool")
            self.free[i] = self.t
        self.n += 1

    def finish(self, pool, dim, v, t, y, after=()):
        q, cols = self.o.q, self.cols
        b = pool.take()
        for i, (c0, n) in enumerate(cols):
            m = q.mm(b.ap[:, 512 * i:512 * i + n], self.o.cs("ones"), self.acc[:, c0:c0 + n], True, True,
                     [self.t, self.o.t_const, *b.free])
        f, r = self.o.rstd(halves(b.ap, cols), 1.0 / dim, EPS, as_halves(v, cols), as_halves(t, cols),
                           as_halves(y, cols), [m, *after])
        b.free = [f]
        return r


def build(q, ins, out):
    nc, ctx = q.nc, q.ctx
    ps = ctx.enter_context(nc.psum_tensor("ps", [P, 8, 512], F32))
    flat = ps[:].rearrange("p a b -> p (a b)")
    mem = Mem(nc, BASE)
    o = Ops(q, mem, ins)
    W = o.W = Weights(q, mem, ins, unit_plan())
    sm, cs = o.sm, o.cs

    def pairs(lo, hi):
        return Pool([Bank(flat[:, i * 1024:(i + 1) * 1024]) for i in range(lo, hi)])

    def singles(lo, hi):
        return Pool([Bank(ps[:, i, :]) for i in range(lo, hi)])

    def load(name, dst, src, after=(), eng="act"):
        return q.dma(eng, dst, src, (name, q.semaphore(name)), after)

    def everyone():
        return [q.last(e) for e in q.sem]

    def barrier(*more):
        toks = everyone() + list(more)
        for eng in q.sem:
            q.wait(eng, toks)
        q.wait("sp", more)

    M = mem.put("M", [P, 9, KT, 2])
    AM = mem.put("AM", [P, 3, KT, 2])
    GM = mem.put("GM", [P, 2, KT, 2])
    sc = mem.put("sc", [P, 16])
    t_sc = q.act(sc[:], sm("c", 0, 16), ACT.Silu, [o.t_small])
    low = mem.at
    high = low + 2 * 4 * TX * 4 + 512
    x_spill = nc.dram_tensor("x_spill", (P, KT, TX), F32).ap()
    h_spill = nc.dram_tensor("h_spill", (P, KT, T2), F32).ap()

    mem = Mem(nc, low)
    mixc = mem.put("mixc", [P, 4, TX])
    att = mem.put("att", [P, 4, TX])
    mem = Mem(nc, high)
    xh = mem.put("x1h", [P, KT, T1], F32R)
    xl = mem.put("x1l", [P, KT, T1], F32R)
    after_xn = mem.at
    X = mem.put("X", [P, KT, T1])
    hh = mem.put("h1h", [P, 8, T1], F32R)
    hl = mem.put("h1l", [P, 8, T1], F32R)
    tm = [mem.put(f"f1_t{i}", [P, T1])[:] for i in range(6)]
    row = mem.put("row", [2, 2, 512])

    def ada(j, pool):
        toks = []
        for u in range(2):
            b = pool.take()
            for v in range(4):
                w, _, t_w = W.next(("w_ada", 8 * j + 4 * u + v))
                w = w.rearrange("p a b -> p (a b)").rearrange("p (a b) -> p a b", a=2)
                for i in range(2):
                    k = 2 * v + i
                    tok = q.mm(b.ap[0:2, 0:512], sc[:, 2 * k:2 * k + 2], w[:, i, :], k == 0, k == KT - 1,
                               [*t_w, *b.free, t_sc], mark=i == 1)
                W.release(tok)
            e = q.copy(row[:, u, :], b.ap[0:2, 0:512], [tok])
            b.free = [e]
            toks.append(e)
        b = pool.take()
        for i in range(8):
            m = q.tr(b.ap[:, 2 * i:2 * i + 2], row[:, i // 4, (i % 4) * P:(i % 4 + 1) * P], cs("ident", 2, 2),
                     [*toks, o.t_const, *b.free], mark=i == 7)
        bias = sm("b_ada", 8 * j, 8).unsqueeze(2).broadcast_to([P, 8, 2])
        b.free = [q.tt(M[:, j, :, :], b.ap[:, 0:16].rearrange("p (a b) -> p a b", b=2), bias, ALU.add, [m])]

    def scales(i, j, gain):
        g = sm(gain, 0, 8).unsqueeze(2).broadcast_to([P, KT, 2])
        return q.stt(AM[:, i, :, :], M[:, j, :, :], 1.0, g, ALU.add, ALU.mult)

    def modulate(X, y, r, groups, A, B, h, l, s):
        out_toks = []
        for k in range(KT):
            t = s[k % len(s)]
            before = [out_toks[k - len(s)]] if k >= len(s) else []
            m = q.tt(t, X[:, k, :], y, ALU.mult, [r, *before], eng="pool" if k % 3 == 2 else "dve")
            for g, (c0, n) in enumerate(groups):
                m = q.ts(t[:, c0:c0 + n], t[:, c0:c0 + n], A(k, g), B(k, g), ALU.mult, ALU.add, [m])
            out_toks.append(o.parts(h[:, k, :], l[:, k, :], t, [m]))
        return out_toks

    def scaled(X, y, r, gain, h, l, s):
        out_toks = []
        for k in range(KT):
            t = s[k % len(s)]
            m = q.stt(t, X[:, k, :], sm(gain, k), y, ALU.mult, ALU.mult, [r, *out_toks[k - len(s):k - len(s) + 1]]
                      if k >= len(s) else [r])
            out_toks.append(o.parts(h[:, k, :], l[:, k, :], t, [m]))
        return out_toks

    def ffn(name, X, cols, groups, xh, xl, hh, hl, gate, pool, tmp, t_x, stats):
        s, hf = tmp
        m_old = [None, None]
        t_old = [None, None]
        for p, (f0, nf) in enumerate(FF_PARTS):
            t_h = []
            for f in range(f0, f0 + nf):
                i = f % 2
                b, tok = o.product((f"w_in{name}", f), xh, xl, cols, pool, t_x)
                a = q.act(as_halves(s[i], cols), halves(b.ap, cols), ACT.Silu, [tok, m_old[i]])
                b.free = [a]
                b2, tok2 = o.product((f"w_in{name}", FF + f), xh, xl, cols, pool, t_x)
                m = q.tt(as_halves(hf[i], cols), as_halves(s[i], cols), halves(b2.ap, cols), ALU.mult,
                         [tok2, a, t_old[i]])
                b2.free = [m]
                m_old[i] = m
                t_old[i] = o.parts(hh[:, f - f0, :], hl[:, f - f0, :], hf[i], [m])
                t_h.append(t_old[i])
            for k in range(KT):
                b, tok = o.product((f"w_out{name}_{p}", k), hh, hl, cols, pool, t_h)
                if gate is None:
                    x = as_halves(X[:, k, :], cols)
                    b.free = [q.tt(x, x, halves(b.ap, cols), ALU.add, [tok])]
                else:
                    for g, (c0, n) in enumerate(groups):
                        b.free = [q.stt(X[:, k, c0:c0 + n], b.ap[:, c0:c0 + n], gate(k, g), X[:, k, c0:c0 + n],
                                        ALU.mult, ALU.add, [tok])]
                if p == 2 and stats is not None:
                    stats.add(X[:, k, :], b.free)
        return b.free[0]

    t_x = load("s_x", X[:].rearrange("p a b -> p (a b)"), ins["x"])
    G1 = [(0, TX), (TX, TC)]
    GX = [(0, TX)]

    def Af(i):
        return lambda k, g: AM[:, i, k, g:g + 1]

    def Bf(j):
        return lambda k, g: M[:, j, k, g:g + 1]

    def Gf(i):
        return lambda k, g: GM[:, i, k, g:g + 1]

    pool = pairs(0, 4)
    st = Stats(o, tm[5], [tm[0], tm[1]], COLS1)
    for k in range(KT):
        st.add(X[:, k, :], [t_x])
    ada(0, pool)
    r = st.finish(pool, D, tm[2], tm[3], tm[4])
    ada(1, pool)
    scales(0, 1, "norm_ffn1")
    t = modulate(X, tm[4], r, G1, Af(0), Bf(0), xh, xl, [tm[0], tm[1], tm[2], tm[3]])
    ada(2, pool)
    ada(3, pool)
    q.ts(GM[:, 0, :, :], M[:, 2, :, :], 0.5, None, ALU.mult, None)
    st = Stats(o, tm[5], [tm[0], tm[1]], COLS1)
    ffn("1", X, COLS1, G1, xh, xl, hh, hl, Gf(0), pool, ([tm[0], tm[1]], [tm[2], tm[3]]), t, st)
    ada(4, pool)
    scales(1, 4, "norm_mix")
    r = st.finish(pool, D, tm[2], tm[3], tm[4], [q.last("act")])
    t_spill = load("s_xsp", x_spill, X[:, :, 0:TX], everyone(), "sp")
    t = modulate(X, tm[4], r, G1, Af(1), Bf(3), xh, xl, [tm[0], tm[1], tm[2], tm[3]])
    for j in range(5, 8):
        ada(j, pool)
    scales(2, 7, "norm_ffn2")
    barrier(t_spill)

    mem = Mem(nc, after_xn)
    row = mem.put("row2", [2, 2, 512])
    const1 = mem.put("const1", [P, NCONST1])
    t_c1 = load("s_c1", const1[:], ins["const1"], everyone(), "sp")

    def c1(name):
        a, n = CONST1[name]
        return const1[:, a:a + n]

    qT = mem.put("qT", [P, 4, TX])
    kT = mem.put("kT", [P, 2, T1])
    vp = mem.put("vp", [P, 6, 4, P])
    qkt = [mem.put(f"m_t{i}", [P, T1])[:] for i in range(5)]
    gb = mem.put("gb", [P, TX])
    gc = mem.put("gc", [P, TX])
    cu = mem.put("cu", [P, TX + 2])
    PT = [mem.put(f"PT{i}", [P, 6, TX]) for i in range(2)]
    pr = [mem.put(f"pr{i}", [P, T1]) for i in range(2)]
    sx = mem.put("sx", [P, 4, 4])
    W.lo_engine = "pool"
    q.do("pool", lambda e: e.memset(cu[:], 0.0))
    t_vp = q.do("pool", lambda e: e.memset(vp[:], 0.0))

    def qk_norm(b, tok, dst, T, cols, gain):
        raw, v, w, y, sqv = (a[:, 0:T] for a in qkt)
        e = q.copy(raw, halves(b.ap, cols), [tok, q.last("dve"), q.last("pool")])
        b.free = [e]
        a = q.act(sqv, raw, ACT.Square, [e])
        b2 = pool.take()
        for i, (c0, n) in enumerate(cols):
            m = q.mm(b2.ap[:, c0:c0 + n], c1("ones64"), sqv[:, c0:c0 + n], True, True, [a, t_c1, *b2.free])
        f, r = o.rstd(b2.ap[:, 0:T], 1.0 / 64, EPS, v, w, y, [m])
        b2.free = [f]
        n1 = q.stt(raw, raw, gain, y, ALU.mult, ALU.mult, [r])
        b3 = pool.take()
        m = q.mm(b3.ap[:, 0:TX], c1("rot"), raw[:, 0:TX], True, True, [n1, *b3.free])
        x1 = q.tt(v[:, 0:TX], raw[:, 0:TX], c1("cos"), ALU.mult, [n1], eng="pool")
        if T > TX:
            q.ts(dst[:, TX:T], raw[:, TX:T], 1.0, None, ALU.mult, None)
        x2 = q.tt(w[:, 0:TX], b3.ap[:, 0:TX], c1("sin"), ALU.mult, [m])
        b3.free = [x2]
        return q.tt(dst[:, 0:TX], v[:, 0:TX], w[:, 0:TX], ALU.add, [x1])

    prev = None
    for i in range(7):
        cols = COLSX if i < 4 else COLS1
        b, tok = o.product(("w_mix_in", i), xh, xl, cols, pool, t)
        if prev is not None:
            qk_norm(*prev)
        if i < 4:
            prev = (b, tok, qT[:, i, :], TX, COLSX, sm("q_norm"))
        elif i < 6:
            prev = (b, tok, kT[:, i - 4, :], T1, COLS1, sm("k_norm"))
    e = q.copy(pr[0][:], b.ap[:, 0:T1], [tok])
    b.free = [e]
    for half in range(2):
        b = pool.take()
        for i in range(3):
            blk = 3 * half + i
            m = q.tr(b.ap[:, i * P:(i + 1) * P], pr[0][:, blk * P:(blk + 1) * P], cs("ident"), [e, *b.free],
                     mark=i == 2)
        src = b.ap[:, 0:384].rearrange("p (a b) -> p a b", b=P)
        for g in range(2):
            for par in range(2):
                b.free = [q.ts(vp[:, 3 * half:3 * half + 3, 2 * g + par, 64 * par:64 * par + 64],
                               src[:, :, 64 * g:64 * g + 64], 1.0, None, ALU.mult, None, [m, t_vp])]
    t_qkv = q.last("dve")
    m_v = m
    all_free = [f for bb in pool.banks for f in bb.free]
    pool = pairs(0, 3)
    poolo = singles(6, 7)
    poolc = singles(7, 8)
    for bb in pool.banks + poolo.banks + poolc.banks:
        bb.free = list(all_free)

    def conv_steps():
        for i in range(4):
            b, tok = yield from o.product_steps(("w_mix_in", 7 + 3 * i), xh, xl, COLSX, poolc, None)
            b.free = [q.copy(gb[:], b.ap[:, 0:TX], [tok, q.last("dve")])]
            yield
            b, tok = yield from o.product_steps(("w_mix_in", 8 + 3 * i), xh, xl, COLSX, poolc, None)
            g = q.copy(gc[:], b.ap[:, 0:TX], [tok, q.last("dve")])
            b.free = [g]
            yield
            b, tok = yield from o.product_steps(("w_mix_in", 9 + 3 * i), xh, xl, COLSX, poolc, None)
            b.free = [q.tt(cu[:, 1:TX + 1], gc[:], b.ap[:, 0:TX], ALU.mult, [tok, g, t_vp])]
            y = mixc[:, i, :]
            q.ts(y, cu[:, 0:TX], sm("conv_w", i), None, ALU.mult, None)
            q.stt(y, cu[:, 1:TX + 1], sm("conv_w", 4 + i), y, ALU.mult, ALU.add)
            q.stt(y, cu[:, 2:TX + 2], sm("conv_w", 8 + i), y, ALU.mult, ALU.add)
            q.tt(y, y, gb[:], ALU.mult)
            yield
        ada(8, poolc)
        q.ts(GM[:, 1, :, :], M[:, 8, :, :], 0.5, None, ALU.mult, None)

    def attention_steps():
        norm_tok, tr_tok, ev_tok = {}, {}, {}
        pv_tok = {}
        bo = None

        def scores(n):
            h, qb, z = n // 4, n % 4, n % 2
            pair, par, g = h // 2, h % 2, h // 4
            r0 = 64 * par
            b = pool.take()
            for i, (c0, nn) in enumerate(COLS1):
                m = q.mm(b.ap[:, c0:c0 + nn], qT[r0:r0 + 64, pair, qb * P:(qb + 1) * P],
                         kT[r0:r0 + 64, g, c0:c0 + nn], True, True, [t_qkv, *b.free], mark=i == 1)
            x = sx[:, n % 4, :]
            q.do("dve", lambda e, x=x, b=b: e.reduce_max(x[:, 0:1], b.ap[:, 0:T1], AX.X), [m])
            nm = q.ts(x[:, 1:2], x[:, 0:1], -0.125, None, ALU.mult, None)
            ex = q.act(pr[z][:], b.ap[:, 0:T1], ACT.Exp, [nm, tr_tok.get(n - 2, m_v)], bias=x[:, 1:2],
                       scale=0.125, accum_out=x[:, 2:3])
            b.free = [ex]
            q.do("dve", lambda e, x=x: e.reciprocal(x[:, 3:4], x[:, 2:3]), [ex])
            norm_tok[n] = q.ts(pr[z][:], pr[z][:], x[:, 3:4], None, ALU.mult, None)

        def turn(n):
            h, qb, z = n // 4, n % 4, n % 2
            b = pool.take()
            for i in range(6):
                c0 = i * P if i < 3 else 512 + (i - 3) * P
                m = q.tr(b.ap[:, c0:c0 + P], pr[z][:, i * P:(i + 1) * P], cs("ident"), [norm_tok[n], *b.free],
                         mark=i == 5)
            tr_tok[n] = m
            src = b.ap.rearrange("p (a b) -> p a b", a=2)[:, :, 0:384].rearrange("p a (b c) -> p a b c", c=P)
            dst = PT[h % 2][:, :, qb * P:(qb + 1) * P].rearrange("p (a b) c -> p a b c", a=2)
            for a in range(2):
                ev_tok[h] = q.copy(dst[:, a], src[:, a], [m, pv_tok.get(h - 2)])
            b.free = [ev_tok[h]]

        def values(h):
            nonlocal bo
            pair, par, g = h // 2, h % 2, h // 4
            if par == 0:
                bo = poolo.take()
            for i in range(6):
                m = q.mm(bo.ap, vp[:, i, 2 * g + par, :], PT[h % 2][:, i, :], par == 0 and i == 0,
                         par == 1 and i == 5, [ev_tok[h], *bo.free], mark=i == 5)
                if i % 2 == 1:
                    yield
            pv_tok[h] = m
            if par == 1:
                bo.free = [q.ts(att[:, pair, :], bo.ap, 1.0, None, ALU.mult, None, [m])]

        scores(0)
        yield
        for n in range(32):
            if n + 1 < 32:
                scores(n + 1)
                yield
            if n >= 4 and n % 4 == 0:
                yield from values(n // 4 - 1)
            turn(n)
            yield
        yield from values(7)

    drive(attention_steps(), conv_steps(), 1.25)
    barrier()

    W.lo_engine = "dve"
    mem = Mem(nc, high)
    Nh = mem.put("Nh", [P, KT, T2], F32R)
    Nl = mem.put("Nl", [P, KT, T2], F32R)
    after_n = mem.at
    H = mem.put("H", [P, KT, T2])
    hh = mem.put("h2h", [P, 8, T2], F32R)
    hl = mem.put("h2l", [P, 8, T2], F32R)
    tm = [mem.put(f"f2_t{i}", [P, T2])[:] for i in range(6)]
    tv = [mem.put(f"tv{i}", [P, TX])[:] for i in range(3)]
    t_h = [load("s_meta", H[:, :, 0:16], ins["meta"], everyone(), "sp"),
           load("s_xback", H[:, :, 16:T2], x_spill, [t_spill], "sp")]
    XV = H[:, :, 16:T2]
    tmx = [a[:, 0:TX] for a in tm]
    mh, ml = Nh[:, :, 0:TX], Nl[:, :, 0:TX]
    pool = pairs(0, 4)
    t = [None] * 8
    for half, (src, gain) in enumerate(((mixc, "conv_out"), (att, "attn_out"))):
        st = Stats(o, (tmx[5], tv[2])[half], [tv[0], tv[1]], COLSX)
        for k in range(4):
            st.add(src[:, k, :], [q.last("dve")])
        r = st.finish(pool, 512, tmx[0], tmx[1], tmx[4], [])
        done = []
        for k in range(4):
            y = (tmx[2], tmx[3])[k % 2]
            m = q.stt(y, src[:, k, :], sm(gain, k), tmx[4], ALU.mult, ALU.mult, [r])
            kk = 4 * (1 - half) + k
            t[kk] = o.parts(mh[:, kk, :], ml[:, kk, :], y, [m])
    st = Stats(o, tmx[5], [tv[0], tv[1]], COLSX)
    for k in range(KT):
        b, tok = o.product(("w_mix_out", k), mh, ml, COLSX, pool, t)
        b.free = [q.stt(XV[:, k, :], b.ap[:, 0:TX], M[:, 5, k, 0:1], XV[:, k, :], ALU.mult, ALU.add,
                        [tok, *t_h])]
        st.add(XV[:, k, :], b.free)
    r = st.finish(pool, D, tmx[0], tmx[1], tmx[4], [q.last("act")])
    t = modulate(XV, tmx[4], r, GX, Af(2), Bf(6), mh, ml, [tmx[0], tmx[1], tmx[2], tmx[3]])
    st = Stats(o, tmx[5], [tv[0], tv[1]], COLSX)
    ffn("2", XV, COLSX, GX, mh, ml, hh[:, :, 0:TX], hl[:, :, 0:TX], Gf(1), pool,
        ([tmx[0], tmx[1]], [tmx[2], tmx[3]]), t, st)
    r = st.finish(pool, D, tmx[0], tmx[1], tmx[4], [q.last("act")])
    st = Stats(o, tm[5], [tm[2], tm[3]], COLS2)
    for k in range(KT):
        m = q.stt(XV[:, k, :], XV[:, k, :], sm("final_norm", k), tmx[4], ALU.mult, ALU.mult, [r])
        st.add(H[:, k, :], [m])

    t_spill = load("s_hsp", h_spill, H[:], everyone(), "sp")
    r = st.finish(pool, D, tm[0], tm[1], tm[4], [q.last("act")])
    t_n = scaled(H, tm[4], r, "norm_mix2", Nh, Nl, [tm[0], tm[1], tm[2], tm[3]])
    barrier(t_spill)
    acc = Mem(nc, low).put("acc", [P, KT, T2])
    pool = pairs(0, 2)
    chain = singles(4, 8)
    W.lo_engine = "pool"
    delta_net(o, Mem(nc, after_n), ins, Nh, Nl, t_n, acc, pool, chain)
    barrier()
    stick(o, Mem(nc, after_n), Nh, Nl, acc, pool, chain)
    barrier()
    W.lo_engine = "dve"
    t_h = load("s_hback", H[:], h_spill, [t_spill, *everyone()], "sp")
    pool = pairs(0, 4)
    t = [o.parts(Nh[:, k, :], Nl[:, k, :], acc[:, k, :]) for k in range(KT)]
    st = Stats(o, tm[5], [tm[2], tm[3]], COLS2)
    for k in range(KT):
        b, tok = o.product(("w_o2", k), Nh, Nl, COLS2, pool, t)
        x = as_halves(H[:, k, :], COLS2)
        b.free = [q.tt(x, x, halves(b.ap, COLS2), ALU.add, [tok, t_h])]
        st.add(H[:, k, :], b.free)
    r = st.finish(pool, D, tm[0], tm[1], tm[4], [q.last("act")])
    t = scaled(H, tm[4], r, "norm_ffn_2", Nh, Nl, [tm[0], tm[1], tm[2], tm[3]])
    t = ffn("3", H, COLS2, None, Nh, Nl, hh, hl, None, pool, ([tm[0], tm[1]], [tm[2], tm[3]]), t, None)
    t = load("s_out", out, H[:, :, 16:T2], [t], "sp")
    q.wait("sp", [t])


def delta_net(o, mem, ins, hn_h, hn_l, t_n, acc, pool, chain):
    q, W, sm, cs = o.q, o.W, o.sm, o.cs
    WIDE = [(0, P, 4), (4, 16, 1)]
    GROUPS = [(0, P, 2), (2, P, 2), (4, 16, 1)]
    SIZES = [P] * 4 + [16]
    ha = lambda ap: as_halves(ap, COLS2)
    sel = mem.put("sel", [64, NH * P])
    t_sel = q.dma("sp", sel[:], ins["sel"], ("s_sel", q.semaphore("s_sel")), [q.last(e) for e in q.sem])
    gbt = mem.put("gbt", [64, T2])
    gcol = mem.put("gcol", [P, 5, 40])
    nb = mem.put("nb", [P, 5, 40])
    rm = [mem.put(f"r{i}", [P, T2])[:] for i in range(6)]
    F = [mem.put(f"dnf{s}", [P, 6, T2]) for s in range(2)]
    craw = mem.put("craw", [P, T2 + 3])
    gB = mem.put("gB", [P, T2])
    DT = mem.put("DT", [P, 5, P])
    AT = mem.put("AT", [P, 5, P])
    LT = mem.put("LT", [P, 5, P])
    LM = [mem.put(f"LM{i}", [P, 5, P]) for i in range(2)]
    UT = mem.put("UT", [P, 2, 5, P])
    Xm = mem.put("Xm", [P, 5, P])
    kd = mem.put("kd", [P, 5, P])
    vb = mem.put("vb", [P, 5, 2 * P])
    ekd = mem.put("ekd", [P, 5])
    S = mem.put("S", [P, 2 * P])
    R = mem.put("R", [P, 2 * P])
    V = mem.put("V", [P, 2 * P])
    O = mem.put("O", [P, 2, T2])
    oh = mem.put("oh", [P, 2, T2], F32R)
    ol = mem.put("ol", [P, 2, T2], F32R)
    q.do("pool", lambda e: e.memset(craw[:], 0.0))
    t_z = q.do("pool", lambda e: e.memset(gbt[:], 0.0))
    b, tok = o.product(("w_proj", 0), hn_h, hn_l, COLS2, pool, t_n)
    za, ea, la = (rm[i][0:8, :] for i in range(3))
    eb = rm[3][32:40, :]
    q.ts(ha(za), halves(b.ap, COLS2)[0:8], sm("dt_bias", 0, 1, (0, 8)), None, ALU.add, None, [tok])
    q.stt(ea, za, -1.0, za, ALU.mult, ALU.max)
    f = q.ts(ha(eb), halves(b.ap, COLS2)[32:40], -1.0, None, ALU.mult, None)
    b.free = [f]
    t = q.act(ea, ea, ACT.Exp, [f], scale=-1.0)
    t = q.act(la, ea, ACT.Ln, [t], bias=1.0)
    q.act(eb, eb, ACT.Exp, [f])
    al = rm[4][0:8, 0:1]
    t = q.act(al, sm("a_log", 0, 1, (0, 8)), ACT.Exp)
    q.ts(za, za, 0.0, None, ALU.max, None)
    q.tt(za, za, la, ALU.add, [t])
    q.ts(za, za, al, -1.0, ALU.mult, ALU.mult)
    q.do("dve", lambda e: e.memset(ea, 1.0))
    for c, n in enumerate(SIZES):
        s = slice(c * P, c * P + n)
        q.do("dve", lambda e, s=s: e.tensor_tensor_scan(gbt[0:8, s], ea[:, s], za[:, s], 0.0, ALU.mult, ALU.add),
             [t_z])
    q.ts(eb, eb, 1.0, None, ALU.add, None)
    t_g = q.do("dve", lambda e: e.reciprocal(gbt[32:40, :], eb))
    b = pool.take()
    for c, n in enumerate(SIZES):
        m = q.tr(b.ap[0:n, 40 * c:40 * c + 40], gbt[0:40, c * P:c * P + n], cs("ident", 40, 40), [t_g, *b.free])
    for c0, n, C in WIDE:
        src = b.ap[0:n, 40 * c0:40 * (c0 + C)].rearrange("p (a b) -> p a b", b=40)
        q.ts(gcol[0:n, c0:c0 + C, :], src, 1.0, None, ALU.mult, None, [m])
        t_col = q.ts(nb[0:n, c0:c0 + C, :], src, -1.0, None, ALU.mult, None)
    b.free = [t_col]

    ready = [None, None]
    used = [None, None]
    ones_in = [None]

    def project(h):
        s = h % 2
        f6 = F[s]
        for i in range(6):
            b, tok = yield from o.product_steps(("w_proj", 1 + 6 * h + i), hn_h, hn_l, COLS2, pool, None)
            dst = f6[:, i, :]
            if i < 4:
                e = q.copy(ha(craw[:, 3:T2 + 3]), halves(b.ap, COLS2), [tok, q.last("dve"), t_z])
                b.free = [e]
                name, base = (("conv_q", h), ("conv_k", h), ("conv_v", 2 * h), ("conv_v", 2 * h + 1))[i]
                tiles = 16 if name == "conv_v" else 8
                q.ts(dst, craw[:, 0:T2], sm(name, base), None, ALU.mult, None, [e, used[s]])
                for j in range(1, 4):
                    t = q.stt(dst, craw[:, j:j + T2], sm(name, j * tiles + base), dst, ALU.mult, ALU.add)
            else:
                b.free = [q.copy(ha(dst), halves(b.ap, COLS2), [tok, used[s]])]
            yield
        t = q.act(f6[:], f6[:], ACT.Silu, [t])
        ready[s] = t
        for i in range(2):
            sqv, v, w, y = rm[0], rm[1], rm[2], rm[5]
            a = q.act(sqv, f6[:, i, :], ACT.Square, [t, q.last("dve"), ones_in[0]])
            b = pool.take()
            for j, (c0, n) in enumerate(COLS2):
                m = q.mm(b.ap[:, 512 * j:512 * j + n], cs("ones"), sqv[:, c0:c0 + n], True, True, [a, *b.free])
            ones_in[0] = m
            f, r = o.rstd(halves(b.ap, COLS2), 1.0, EPS, ha(v), ha(w), ha(y), [m])
            b.free = [f]
            ready[s] = q.stt(f6[:, i, :], f6[:, i, :], float(P) ** -0.5 if i == 0 else 1.0, y, ALU.mult,
                             ALU.mult, [ready[s]])
            yield

    t_o = [None]
    o_free = [None]

    def tok3(ap, c0, n, C):
        return ap[:, c0 * P:c0 * P + C * n].rearrange("p (a b) -> p a b", b=n)

    def wide(ap, n, C):
        return ap.unsqueeze(1).broadcast_to([n, C, n])

    def delta(h):
        s = h % 2
        qf, kf, v0, v1 = (F[s][:, i, :] for i in range(4))
        bB = rm[3]
        for dst, r in ((gB[:], 0), (bB, 32)):
            for i, (c0, n) in enumerate(COLS2):
                b = chain.take()
                m = q.mm(b.ap[:, 0:n], sel[r:r + 8, h * P:(h + 1) * P], gbt[r:r + 8, c0:c0 + n], True, True,
                         [t_g, t_sel, *b.free])
                t_b = q.copy(dst[:, c0:c0 + n], b.ap[:, 0:n], [m, q.last("dve"), q.last("pe")])
                b.free = [t_b]
            yield
        for c0, n, C in WIDE:
            g3 = tok3(gB[0:n, :], c0, n, C)
            col = gcol[0:n, c0:c0 + C, h:h + 1]
            dt = DT[0:n, c0:c0 + C, 0:n]
            q.tt(dt, g3, col.broadcast_to([n, C, n]), ALU.subtract, [t_b, t_col])
            t = q.ts(dt, dt, 0.0, None, ALU.min, None)
            t = q.act(dt, dt, ACT.Exp, [t])
            q.tt(ekd[0:n, c0:c0 + C].unsqueeze(2), g3[:, :, n - 1:n], col, ALU.subtract)
            q.tt(dt, dt, wide(cs("incl", n, n), n, C), ALU.mult, [t])
        t_e = q.last("dve")
        yield
        for c0, n, C in WIDE:
            t_kd = q.act(ekd[0:n, c0:c0 + C], ekd[0:n, c0:c0 + C], ACT.Exp, [t_e])
        t_eg = q.act(gB[:], gB[:], ACT.Exp, [t_e])
        for c0, n, C in WIDE:
            b, b2 = chain.take(), chain.take()
            for c in range(C):
                cc = slice((c0 + c) * P, (c0 + c) * P + n)
                m = q.mm(b.ap[0:n, c * n:(c + 1) * n], kf[:, cc], kf[:, cc], True, True, [ready[s], *b.free],
                         mark=c == C - 1)
            for c in range(C):
                cc = slice((c0 + c) * P, (c0 + c) * P + n)
                m2 = q.mm(b2.ap[0:n, c * n:(c + 1) * n], kf[:, cc], qf[:, cc], True, True, b2.free,
                          mark=c == C - 1)
            dt, at, lt = (a[0:n, c0:c0 + C, 0:n] for a in (DT, AT, LT))
            v3 = lambda bb: bb.ap[0:n, 0:C * n].rearrange("p (a b) -> p a b", b=n)
            b.free = [q.tt(lt, v3(b), dt, ALU.mult, [m])]
            q.tt(lt, lt, tok3(bB[0:n, :], c0, n, C), ALU.mult)
            q.tt(lt, lt, wide(cs("strict", n, n), n, C), ALU.mult)
            u = UT[0:n, 0, c0:c0 + C, 0:n]
            q.tt(u, lt, wide(cs("level", n, n, 0), n, C), ALU.mult)
            t_u = q.tt(u, wide(cs("ident", n, n), n, C), u, ALU.subtract)
            b2.free = [q.tt(at, v3(b2), dt, ALU.mult, [m2])]
            yield
        t_lt = t_u

        t_ut = {}
        for c0, n, C in GROUPS:
            b = chain.take()
            for c in range(C):
                m = q.tr(b.ap[0:n, c * n:(c + 1) * n], UT[0:n, 0, c0 + c, 0:n], cs("ident", n, n), [t_u, *b.free],
                         mark=c == C - 1)
            t = q.copy(UT[0:n, 1, c0:c0 + C, 0:n], b.ap[0:n, 0:C * n].rearrange("p (a b) -> p a b", b=n), [m])
            b.free = [t]
            t_ut[c0] = t
        yield
        turns = []

        def turn(src, dst, w, c0, n, C):
            b = chain.take()
            for c in range(C):
                m = q.tr(b.ap[0:n, c * P:(c + 1) * P], src[:, (c0 + c) * P:(c0 + c) * P + n], cs("ident"),
                         [ready[s], *b.free], mark=c == C - 1)
            ps3 = b.ap[0:n, 0:C * P].rearrange("p (a b) -> p a b", b=P)
            if dst is kd:
                col = ekd[0:n, c0:c0 + C].unsqueeze(2).broadcast_to([n, C, P])
            else:
                col = gcol[0:n, c0:c0 + C, 32 + h:33 + h].broadcast_to([n, C, P])
            b.free = [q.tt(dst[0:n, c0:c0 + C, w:w + P], ps3, col, ALU.mult, [m, t_kd])]

        for src, dst, w in ((kf, kd, 0), (v0, vb, 0), (v1, vb, P)):
            for g in WIDE:
                if not (dst is kd and g[1] == 16):
                    turns.append((src, dst, w, *g))

        lm_used = [None, None]
        x_used = {}
        for i in range(1, 7):
            todo = [g for g in GROUPS if g[1] > (1 << i)]
            lm = LM[i % 2]
            t_lm = None
            for c0, n, C in [g for g in WIDE if g[1] > (1 << i)]:
                t_lm = q.tt(lm[0:n, c0:c0 + C, 0:n], LT[0:n, c0:c0 + C, 0:n],
                            wide(cs("level", n, n, i), n, C), ALU.mult, [t_lt, lm_used[i % 2]], eng="pool")
            t_x = {}
            for c0, n, C in todo:
                b = chain.take()
                for c in range(C):
                    m = q.mm(b.ap[0:n, c * n:(c + 1) * n], lm[0:n, c0 + c, 0:n], UT[0:n, 1, c0 + c, 0:n], True,
                             True, [t_lm, t_ut[c0], *b.free], mark=c == C - 1)
                lm_used[i % 2] = m
                t_x[c0] = q.copy(Xm[0:n, c0:c0 + C, 0:n], b.ap[0:n, 0:C * n].rearrange("p (a b) -> p a b", b=n),
                                 [m, x_used.get(c0)])
                b.free = [t_x[c0]]
            if turns:
                turn(*turns.pop(0))
            yield
            for c0, n, C in todo:
                b = chain.take()
                both = (2 << i) < n
                for c in range(C):
                    m = q.mm(b.ap[0:n, c * n:(c + 1) * n], Xm[0:n, c0 + c, 0:n], UT[0:n, 0, c0 + c, 0:n], True,
                             True, [t_x[c0], t_ut[c0], *b.free], mark=c == C - 1)
                if both:
                    for c in range(C):
                        m = q.mm(b.ap[0:n, (C + c) * n:(C + c + 1) * n], UT[0:n, 0, c0 + c, 0:n],
                                 Xm[0:n, c0 + c, 0:n], True, True, mark=c == C - 1)
                x_used[c0] = m
                if both:
                    a = UT[0:n, :, c0:c0 + C, 0:n]
                    d = b.ap[0:n, 0:2 * C * n].rearrange("p (x a b) -> p x a b", x=2, b=n)
                else:
                    a = UT[0:n, 0, c0:c0 + C, 0:n]
                    d = b.ap[0:n, 0:C * n].rearrange("p (a b) -> p a b", b=n)
                t_ut[c0] = q.tt(a, a, d, ALU.subtract, [m])
                b.free = [t_ut[c0]]
            if i == 2:
                t_q = q.tt(qf, qf, gB[:], ALU.mult, [t_eg])
            yield
        while turns:
            turn(*turns.pop(0))
        t_k = q.tt(kf, kf, gB[:], ALU.mult, [q.last("pe"), t_eg])
        yield
        t_s = None
        m_s = None
        for c, n in enumerate(SIZES):
            cc = slice(c * P, c * P + n)
            t_u = t_ut[{0: 0, 1: 0, 2: 2, 3: 2, 4: 4}[c]]
            if c:
                b = chain.take()
                m = q.mm(b.ap[0:n, 0:256], kf[:, cc], S[:], True, True, [t_k, t_s, *b.free])
                t_r = q.stt(R[0:n, :], b.ap[0:n, 0:256], nb[0:n, c, 32 + h:33 + h], vb[0:n, c, :], ALU.mult,
                            ALU.add, [m])
                b.free = [t_r]
                rhs = R[0:n, :]
                yield
            else:
                rhs, t_r = vb[0:n, c, :], t_k
            b = chain.take()
            m = q.mm(b.ap[0:n, 0:256], U_(UT, n, c), rhs, True, True, [t_r, t_u, *b.free])
            t_v = q.copy(V[0:n, :], b.ap[0:n, 0:256], [m])
            b.free = [t_v]
            bo = chain.take()
            if c:
                yield
            if c < 4:
                b = chain.take()
                m2 = q.mm(b.ap[:, 0:256], kd[0:n, c, :], V[0:n, :], True, True, [t_v, *b.free])
            for x in range(2):
                ob = bo.ap[:, x * P:x * P + n]
                if c:
                    q.mm(ob, S[:, x * P:(x + 1) * P], qf[:, cc], True, False, [t_q, t_s, *bo.free], mark=False)
                m = q.mm(ob, V[0:n, x * P:(x + 1) * P], AT[0:n, c, 0:n], c == 0, True, [t_v, *bo.free],
                         mark=x == 1)
            if c < 4:
                if c:
                    t_s = q.stt(S[:], S[:], gB[:, c * P + n - 1:c * P + n], b.ap[:, 0:256], ALU.mult, ALU.add,
                                [m2, m])
                else:
                    t_s = q.ts(S[:], b.ap[:, 0:256], 1.0, None, ALU.mult, None, [m2])
                b.free = [t_s]
            t_o[0] = q.ts(O[:, :, cc], bo.ap[:, 0:2 * P].rearrange("p (a b) -> p a b", a=2)[:, :, 0:n], 1.0, None,
                          ALU.mult, None, [m])
            bo.free = [t_o[0]]
            yield
        bb = [chain.take(), chain.take()]
        for x in range(2):
            a = q.act(rm[3 + x], O[:, x, :], ACT.Square, [t_o[0], q.last("pe")])
            for i, (c0, n) in enumerate(COLS2):
                m = q.mm(bb[i].ap[:, 0:n], cs("ones"), rm[3 + x][:, c0:c0 + n], x == 0, x == 1,
                         [a, *bb[i].free])
        yield
        for i, (c0, n) in enumerate(COLS2):
            f, r = o.rstd(bb[i].ap[:, 0:n], 1.0 / 256, EPS, kf[:, c0:c0 + n], qf[:, c0:c0 + n],
                          rm[4][:, c0:c0 + n], [m])
            bb[i].free = [f]
            yield
        for x in range(2):
            q.stt(O[:, x, :], O[:, x, :], sm("dn_gain", x), rm[4], ALU.mult, ALU.mult, [r])
            w = q.tt(O[:, x, :], O[:, x, :], F[s][:, 4 + x, :], ALU.mult)
            t_o[0] = o.parts(oh[:, x, :], ol[:, x, :], O[:, x, :], [w, o_free[0]])
        used[s] = t_o[0]
        yield

    def branch(h, t_in, first):
        for u in range(2):
            wh, wl, t_w = W.next(("w_bdn", 2 * h + u))
            for j in range(4):
                k8 = 4 * u + j
                b = pool.take()
                for i, (c0, n) in enumerate(COLS2):
                    for k in range(2):
                        for p, (w, x) in enumerate(((wh, oh), (wh, ol), (wl, oh))):
                            end = k == 1 and p == 2
                            tok = q.mm(b.ap[:, 512 * i:512 * i + n], w[:, 2 * j + k, :], x[:, k, c0:c0 + n],
                                       k == 0 and p == 0, end, [*t_w, t_in, *b.free], mark=end and i == 1)
                if j == 3:
                    W.release(tok)
                a = ha(acc[:, k8, :])
                if first:
                    b.free = [q.ts(a, halves(b.ap, COLS2), 1.0, None, ALU.mult, None, [tok])]
                else:
                    b.free = [q.tt(a, a, halves(b.ap, COLS2), ALU.add, [tok])]
                yield
        o_free[0] = tok

    run(project(0))
    for h in range(NH):
        def filler(h=h, t_prev=t_o[0]):
            p = project(h + 1) if h + 1 < NH else iter(())
            for _ in zip(range(24), p):
                yield
            if h:
                yield from branch(h - 1, t_prev, h == 1)
            yield from p
        drive(delta(h), filler(), 1.8)
    run(branch(NH - 1, t_o[0], False))


def U_(UT, n, c):
    return UT[0:n, 0, c, 0:n]


def stick(o, mem, hn_h, hn_l, acc, pool, chain):
    q, W, sm, cs = o.q, o.W, o.sm, o.cs
    SIZES = [P] * 4 + [16]
    ha = lambda ap: as_halves(ap, COLS2)
    accs = mem.put("accs", [P, KT, T2])
    rm = [mem.put(f"sr{i}", [P, T2])[:] for i in range(5)]
    Fs = [mem.put(f"sbf{s}", [P, 3, T2]) for s in range(2)]
    vts = [mem.put(f"vt{i}", [P, 5, P]) for i in range(2)]
    Zs = [mem.put(f"Z{i}", [P, 5, T2]) for i in range(2)]
    SPs = [mem.put(f"SP{i}", [P, 5, T2]) for i in range(2)]
    oh = mem.put("sbh", [P, 1, T2], F32R)
    ol = mem.put("sbl", [P, 1, T2], F32R)
    oc = mem.put("oc", [P, T2])
    ready, used = [None, None], [None, None]
    z_used = [None, None]
    t_o = [None]
    o_free = [None]
    state = {}

    def gates(base, a, add):
        for k in range(KT):
            b, tok = yield from o.product_steps(("w_proj", base + k), hn_h, hn_l, COLS2, pool, None)
            t = rm[3 + k % 2]
            e = q.act(ha(t), halves(b.ap, COLS2), ACT.Sigmoid, [tok, q.last("dve")])
            b.free = [e]
            q.tt(a[:, k, :], a[:, k, :], t, ALU.mult, [e])
            if add is not None:
                q.tt(add[:, k, :], add[:, k, :], a[:, k, :], ALU.add)
            yield

    def project(h):
        s = h % 2
        for i in range(3):
            b, tok = yield from o.product_steps(("w_proj", 49 + 3 * h + i), hn_h, hn_l, COLS2, pool, None)
            dst = Fs[s][:, i, :]
            e = q.copy(ha(dst), halves(b.ap, COLS2), [tok, used[s]])
            b.free = [e]
            ready[s] = e
            if i < 2:
                a = q.act(rm[2], dst, ACT.Square, [q.last("dve"), state.get("ones")])
                yield
                b = pool.take()
                for j, (c0, n) in enumerate(COLS2):
                    m = q.mm(b.ap[:, 512 * j:512 * j + n], cs("ones"), rm[2][:, c0:c0 + n], True, True,
                             [a, *b.free])
                state["ones"] = m
                f, r = o.rstd(halves(b.ap, COLS2), 1.0 / P, EPS, ha(rm[3]), ha(rm[0]), ha(rm[1]), [m])
                b.free = [f]
                t = q.stt(dst, dst, sm("sbq" if i == 0 else "sbk"), rm[1], ALU.mult, ALU.mult, [r])
                if i == 0:
                    t = q.ts(dst, dst, float(P) ** -0.5, None, ALU.mult, None)
                state["t"] = t
            yield

    def spans(jb):
        lo = jb * P
        if T2 - lo > 512:
            return [(lo, 264), (lo + 264, 264)]
        return [(lo, T2 - lo)]

    def scores(h):
        s = h % 2
        qf, kf, vf = (Fs[s][:, i, :] for i in range(3))
        Z, SP, vt = Zs[s], SPs[s], vts[s]
        t_in = [ready[s], state["t"]]
        free = z_used[s]
        for c0, n, C in ((0, P, 4), (4, 16, 1)):
            b = chain.take()
            for c in range(C):
                m = q.tr(b.ap[0:n, c * P:(c + 1) * P], vf[:, (c0 + c) * P:(c0 + c) * P + n], cs("ident"),
                         [*t_in, *b.free], mark=c == C - 1)
            t_vt = q.copy(vt[0:n, c0:c0 + C, :], b.ap[0:n, 0:C * P].rearrange("p (a b) -> p a b", b=P),
                          [m, free])
            b.free = [t_vt]
        yield
        for jb, n in enumerate(SIZES):
            for c0, w in spans(jb):
                b = chain.take()
                m = q.mm(b.ap[0:n, 0:w], kf[:, jb * P:jb * P + n], qf[:, c0:c0 + w], True, True,
                         [*t_in, *b.free])
                z, sp = Z[0:n, jb, c0:c0 + w], SP[0:n, jb, c0:c0 + w]
                q.copy(z, b.ap[0:n, 0:w], [m, free])
                e = q.act(sp, b.ap[0:n, 0:w], ACT.Abs)
                b.free = [e]
            used[s] = m
            lo = jb * P
            z, sp = Z[0:n, jb, lo:T2], SP[0:n, jb, lo:T2]
            q.act(sp, sp, ACT.Exp, scale=-1.0)
            t = q.act(sp, sp, ACT.Ln, bias=1.0)
            q.stt(sp, z, 0.0, sp, ALU.max, ALU.add, [t])
            t = q.tt(SP[0:n, jb, lo:lo + n], SP[0:n, jb, lo:lo + n], cs("strict", n, n), ALU.mult)
            yield
        state["sp", s] = (t, t_vt)

    def weights(h):
        s = h % 2
        Z, SP, vt = Zs[s], SPs[s], vts[s]
        t_sp, t_vt = state["sp", s]
        for jb in range(4, -1, -1):
            n = SIZES[jb]
            for c0, w in spans(jb):
                b = chain.take()
                terms = [(cs("tri", n, n), jb, c0, w)]
                for j2 in range(jb + 1, 5):
                    a = max(c0, j2 * P)
                    if a < c0 + w:
                        terms.append((cs("ones", SIZES[j2], n), j2, a, c0 + w - a))
                for i, (lhs, j2, a, ww) in enumerate(terms):
                    m = q.mm(b.ap[0:n, a - c0:a - c0 + ww], lhs, SP[0:SIZES[j2], j2, a:a + ww], i == 0,
                             i == len(terms) - 1, [t_sp, *b.free], mark=i == len(terms) - 1)
                z = Z[0:n, jb, c0:c0 + w]
                b.free = [q.tt(z, z, b.ap[0:n, 0:w], ALU.subtract, [m])]
            lo = jb * P
            d = Z[0:n, jb, lo:lo + n]
            t = q.ts(d, d, 0.0, None, ALU.min, None)
            t = q.act(Z[0:n, jb, lo:T2], Z[0:n, jb, lo:T2], ACT.Exp, [t])
            t_w = q.tt(d, d, cs("strict", n, n), ALU.mult, [t])
            yield
        for c0, w in COLS2:
            b = chain.take()
            terms = []
            for jb in range(5):
                a = max(c0, jb * P)
                if a < c0 + w:
                    terms.append((jb, a, c0 + w - a))
            for i, (jb, a, ww) in enumerate(terms):
                m = q.mm(b.ap[:, a - c0:a - c0 + ww], vt[0:SIZES[jb], jb, :], Z[0:SIZES[jb], jb, a:a + ww], i == 0,
                         i == len(terms) - 1, [t_vt, t_w, *b.free], mark=i == len(terms) - 1)
            e = q.copy(oc[:, c0:c0 + w], b.ap[:, 0:w], [m, state.get("oc")])
            b.free = [e]
            yield
        z_used[s] = m
        t_o[0] = state["oc"] = o.parts(oh[:, 0, :], ol[:, 0, :], oc[:], [e, o_free[0]])
        yield

    def branch(h, t_in):
        wh, wl, t_w = W.next(("w_bsb", h))
        for k in range(KT):
            b = pool.take()
            for i, (c0, n) in enumerate(COLS2):
                for p, (w, x) in enumerate(((wh, oh), (wh, ol), (wl, oh))):
                    tok = q.mm(b.ap[:, 512 * i:512 * i + n], w[:, k, :], x[:, 0, c0:c0 + n], p == 0, p == 2,
                               [*t_w, t_in, *b.free], mark=p == 2 and i == 1)
            a = ha(accs[:, k, :])
            if h == 0:
                b.free = [q.ts(a, halves(b.ap, COLS2), 1.0, None, ALU.mult, None, [tok])]
            else:
                b.free = [q.tt(a, a, halves(b.ap, COLS2), ALU.add, [tok])]
            if k % 2:
                yield
        W.release(tok)
        o_free[0] = tok

    def both(one, two):
        for _ in one:
            yield
            next(two, None)
            yield
        yield from two

    run(project(0))
    drive(scores(0), gates(73, acc, None), 8.0)
    run(project(1))
    for h in range(NH):
        def filler(h=h, t_prev=t_o[0]):
            p = project(h + 2) if h + 2 < NH else iter(())
            for _ in zip(range(8), p):
                yield
            if h:
                yield from branch(h - 1, t_prev)
            yield from p
        drive(both(weights(h), scores(h + 1) if h + 1 < NH else iter(())), filler(), 1.6)
    run(branch(NH - 1, t_o[0]))
    run(gates(81, accs, acc))


def _tiles(np, w, rows=None):
    k, n = w.shape
    return np.ascontiguousarray(w.reshape(k // P, P, n // P, P).transpose(2, 1, 0, 3)).reshape(n // P, P, k)


def _constants(np):
    i = np.arange(P)
    c = np.zeros((P, NCONST), np.float32)

    def put(name, a, at=0):
        c[:, CONST[name][0] + at:CONST[name][0] + at + a.shape[1]] = a

    put("ident", np.eye(P, dtype=np.float32))
    put("ones", np.ones((P, P), np.float32))
    put("tri", (i[:, None] >= i[None, :]).astype(np.float32))
    put("incl", (i[None, :] >= i[:, None]).astype(np.float32))
    put("strict", (i[None, :] > i[:, None]).astype(np.float32))
    for lv in range(7):
        b = 1 << lv
        m = (i[:, None] // (2 * b) == i[None, :] // (2 * b)) & ((i[:, None] // b) % 2 == 0) & \
            ((i[None, :] // b) % 2 == 1)
        put("level", m.astype(np.float32), lv * P)
    c1 = np.zeros((P, NCONST1), np.float32)
    c1[:, 0:128] = (i[:, None] // 64 == i[None, :] // 64)
    rot = np.zeros((P, P), np.float32)
    for a in range(0, P, 2):
        rot[a + 1, a] = -1.0
        rot[a, a + 1] = 1.0
    c1[:, 128:256] = rot
    tok = np.arange(TX)
    inv = (np.float32(10000.0) ** (-np.arange(16, dtype=np.float32) / np.float32(16))).astype(np.float32)
    row = (tok // 64).astype(np.float32)
    col = (tok % 64).astype(np.float32)
    ang = np.concatenate([row[:, None] * inv, col[:, None] * inv], axis=-1).astype(np.float32)
    pos = (i % 64) // 2
    c1[:, 256:768] = np.cos(ang).T[pos]
    c1[:, 768:1280] = np.sin(ang).T[pos]
    sel = np.zeros((64, NH * P), np.float32)
    for h in range(NH):
        sel[h, h * P:(h + 1) * P] = 1.0
        sel[32 + h, h * P:(h + 1) * P] = 1.0
    return c, c1, sel


def kernel(**inputs):
    import numpy as np
    import concourse.bacc as bacc
    from concourse.bass_utils import run_bass_kernel_spmd

    g = {k: np.asarray(v) for k, v in inputs.items()}

    def cols(v):
        return v.reshape(-1, P).T

    def feat(x):
        return x.T.reshape(KT, P, -1).transpose(1, 0, 2)

    a = {}
    sm = np.zeros((P, NSMALL), np.float32)

    def put(name, v, rows=P):
        s, n = SMALL[name]
        sm[0:rows, s:s + n] = v

    put("b_ada", cols(g["b_ada"][0]))
    put("norm_ffn1", cols(g["norm_ffn1"][0]))
    put("norm_mix", cols(g["norm_mix"][0]))
    put("norm_ffn2", cols(g["norm_ffn2"][0]))
    put("final_norm", cols(g["final_norm"]))
    put("q_norm", np.concatenate([g["q_norm"][0]] * 2)[:, None])
    put("k_norm", np.concatenate([g["k_norm"][0]] * 2)[:, None])
    put("attn_out", cols(g["attn_out_norm"][0]))
    put("conv_out", cols(g["conv_out_norm"][0]))
    put("conv_w", cols(g["conv_w"][0].reshape(-1)))
    put("norm_mix2", cols(g["norm_mix_gain_2"][0]))
    put("norm_ffn_2", cols(g["norm_ffn_gain_2"][0]))
    for n in "qkv":
        put("conv_" + n, cols(g[f"conv_{n}_2"][0].reshape(-1)))
    put("dn_gain", cols(g["dn_out_norm_gain_2"][0]))
    put("sbq", g["sb_q_norm_gain_2"][0][:, None])
    put("sbk", g["sb_k_norm_gain_2"][0][:, None])
    put("a_log", g["dn_a_log_2"][0][:, None], NH)
    put("dt_bias", g["dn_dt_bias_2"][0][:, None], NH)
    put("c", np.stack([cols(g["c"][0]), cols(g["c_ctx"])], axis=2).reshape(P, 16))
    a["small"] = sm
    a["const"], a["const1"], a["sel"] = _constants(np)
    a["x"] = np.concatenate([feat(g["x"][0]), feat(g["ctx"][0])], axis=2).reshape(P, -1)
    a["meta"] = np.ascontiguousarray(feat(g["meta_tokens_2"]))

    a["w_ada"] = np.ascontiguousarray(
        g["w_ada"][0].reshape(4, 2, P, 18, 512).transpose(3, 0, 2, 1, 4)).reshape(72, P, 1024)
    for n, wi, wo in (("1", "w_ffn1_in", "w_ffn1_out"), ("2", "w_ffn2_in", "w_ffn2_out"),
                      ("3", "w_ffn_in_2", "w_ffn_out_2")):
        a[f"w_in{n}"] = _tiles(np, g[wi][0])
        for p, (f0, nf) in enumerate(FF_PARTS):
            a[f"w_out{n}_{p}"] = _tiles(np, g[wo][0][f0 * P:(f0 + nf) * P])
    w = g["w_mix_in"][0]
    k0, k1 = w[:, 512:576], w[:, 576:640]
    order = [w[:, 0:512], k0, k0, k1, k1, w[:, 640:768]]
    for i in range(4):
        for base in (768, 1280, 1792):
            order.append(w[:, base + i * P:base + (i + 1) * P])
    a["w_mix_in"] = _tiles(np, np.concatenate(order, axis=1))
    a["w_mix_out"] = _tiles(np, g["w_mix_out"][0])
    w = g["w_in_2"][0]
    z = np.zeros((D, 24), np.float32)
    order = [w[:, 6144:6152], z, w[:, 6152:6160], z, np.zeros((D, 64), np.float32)]
    for h in range(NH):
        order += [w[:, h * P:(h + 1) * P], w[:, 1024 + h * P:1024 + (h + 1) * P],
                  w[:, 2048 + 256 * h:2048 + 256 * (h + 1)], w[:, 4096 + 256 * h:4096 + 256 * (h + 1)]]
    for h in range(NH):
        order += [w[:, 6160 + 1024 * j + h * P:6160 + 1024 * j + (h + 1) * P] for j in range(3)]
    order.append(w[:, 9232:11280])
    a["w_proj"] = _tiles(np, np.concatenate(order, axis=1))
    w = g["w_branch_dn_2"][0].reshape(NH, 2, P, 2, 4, P)
    a["w_bdn"] = np.ascontiguousarray(w.transpose(0, 3, 2, 4, 1, 5)).reshape(2 * NH, P, 8 * P)
    a["w_bsb"] = np.ascontiguousarray(g["w_branch_sb_2"][0]).reshape(NH, P, 8 * P)
    a["w_o2"] = _tiles(np, g["w_out_2"][0])

    nc = bacc.Bacc("TRN2", target_bir_lowering=False, num_devices=1)
    ins = {n: nc.dram_tensor("in_" + n, v.shape, F32, kind="ExternalInput").ap() for n, v in a.items()}
    out = nc.dram_tensor("out", (P, KT, TX), F32, kind="ExternalOutput").ap()
    program(nc, ins, out)
    r = run_bass_kernel_spmd(nc, [{"in_" + n: v for n, v in a.items()}], core_ids=[0])
    y = r.results[0]["out"]
    return np.ascontiguousarray(y.transpose(1, 0, 2).reshape(D, TX).T).reshape(1, TX, D)
```

```python
from contextlib import ExitStack

import concourse.bass as bass
from concourse import mybir

BASE = 16512
TOP = 229344
P = 128
F32 = mybir.dt.float32
F32R = mybir.dt.float32r
ALU = mybir.AluOpType
ACT = mybir.ActivationFunctionType
AX = mybir.AxisListType

D = 1024
KT = 8
TX = 512
TC = 256
T1 = TX + TC
T2 = 528
NH = 8
FF = 22
FF_PARTS = [(0, 8), (8, 7), (15, 7)]
CH = 128
EPS = 1e-6

SMALL = {}
_at = 0
for _name, _n in (("b_ada", 72), ("norm_ffn1", 8), ("norm_mix", 8), ("norm_ffn2", 8), ("final_norm", 8),
                  ("q_norm", 1), ("k_norm", 1), ("attn_out", 4), ("conv_out", 4), ("conv_w", 12),
                  ("norm_mix2", 8), ("norm_ffn_2", 8), ("conv_q", 32), ("conv_k", 32), ("conv_v", 64),
                  ("dn_gain", 2), ("sbq", 1), ("sbk", 1), ("a_log", 1), ("dt_bias", 1), ("c", 16)):
    SMALL[_name] = (_at, _n)
    _at += _n
NSMALL = _at

CONST = {}
_at = 0
for _name, _n in (("ident", 128), ("ones", 128), ("tri", 128), ("incl", 128), ("strict", 128),
                  ("level", 7 * 128), ("eps", 1)):
    CONST[_name] = (_at, _n)
    _at += _n
NCONST = _at
CONST1 = {"ones64": (0, 128), "rot": (128, 128), "cos": (256, 512), "sin": (768, 512)}
NCONST1 = 1280


def unit_plan():
    plan = []

    def ada(j):
        plan.extend(("w_ada", 8 * j + i, 8, False) for i in range(8))


    def ffn(n):
        for p, (f0, nf) in enumerate(FF_PARTS):
            for f in range(f0, f0 + nf):
                plan.append((f"w_in{n}", f, 8, True))
                plan.append((f"w_in{n}", FF + f, 8, True))
            plan.extend((f"w_out{n}_{p}", o, nf, True) for o in range(KT))

    for j in range(4):
        ada(j)
    ffn(1)
    ada(4)
    ada(5)
    ada(6)
    ada(7)
    plan.extend(("w_mix_in", i, 8, True) for i in range(19))
    ada(8)
    plan.extend(("w_mix_out", i, 8, True) for i in range(8))
    ffn(2)
    plan.append(("w_proj", 0, 8, True))
    dn = [[("w_proj", 1 + 6 * h + i, 8, True) for i in range(6)] for h in range(NH)]
    dnb = [[("w_bdn", 2 * h + i, 8, True) for i in range(2)] for h in range(NH)]
    sb = [[("w_proj", 49 + 3 * h + i, 8, True) for i in range(3)] for h in range(NH)]
    sbb = [[("w_bsb", h, 8, True)] for h in range(NH)]
    plan += dn[0][:4] + dn[1][:4]
    for h in range(NH):
        nxt = dn[h + 2] if h + 2 < NH else []
        plan += nxt[:4] + dn[h][4:] + (dnb[h - 1] if h else [])
    plan += dnb[NH - 1]
    g = [("w_proj", 73 + i, 8, True) for i in range(8)]
    plan += sb[0] + g[0:4] + sb[1] + g[4:8]
    for h in range(NH):
        plan += (sb[h + 2] if h + 2 < NH else []) + (sbb[h - 1] if h else [])
    plan += sbb[NH - 1]
    plan += [("w_proj", 81 + i, 8, True) for i in range(8)]
    plan += [("w_o2", i, 8, True) for i in range(8)]
    ffn(3)
    return plan


def width(ap):
    n = 1
    for d in ap.shape[1:]:
        n *= d
    return n


class Queues:

    def __init__(self, nc, ctx):
        self.nc = nc
        self.ctx = ctx
        self.engines = {"pe": nc.tensor, "act": nc.scalar, "dve": nc.vector, "pool": nc.gpsimd, "sp": nc.sync}
        self.queue = {e: [] for e in self.engines}
        self.sem = {e: self.semaphore(f"s_{e}") for e in ("pe", "act", "dve", "pool")}
        self.count = {e: 0 for e in self.sem}
        self.seen = {e: {} for e in self.engines}
        self.dma_count = {}
        self.table = None
        self.clock = {e: 0.0 for e in self.engines}
        self.dma_clock = 0.0
        self.done = {}

    def semaphore(self, name):
        return self.ctx.enter_context(self.nc.semaphore(name))

    def wait(self, eng, after):
        for tok in after:
            if tok is None:
                continue
            name, sem, value = tok
            if self.seen[eng].get(name, 0) < value:
                self.seen[eng][name] = value
                self.queue[eng].append(lambda e, sem=sem, value=value: e.wait_ge(sem, value))

    def when(self, after):
        return max((self.done[t[0], t[2]] for t in after if t is not None), default=0.0)

    def do(self, eng, instruction, after=(), mark=True, cost=300.0):
        self.clock[eng] = max(self.clock[eng], self.when(after) + 60.0) + cost
        if eng != "pe" and self.count[eng]:
            self.wait(eng, [self.last(eng)])
        self.wait(eng, after)
        if not mark:
            self.queue[eng].append(instruction)
            return None
        self.count[eng] += 1
        sem = self.sem[eng]
        self.queue[eng].append(lambda e: instruction(e).then_inc(sem, 1))
        self.done[eng, self.count[eng]] = self.clock[eng]
        return self.last(eng)

    def last(self, eng):
        return (eng, self.sem[eng], self.count[eng])

    def dma(self, eng, out, in_, name_sem, after=()):
        name, sem = name_sem
        self.wait(eng, after)
        self.dma_count[name] = self.dma_count.get(name, 0) + 16
        self.queue[eng].append(lambda e: e.dma_start(out, in_).then_inc(sem, 16))
        self.clock[eng] = max(self.clock[eng], self.when(after)) + 50.0
        self.dma_clock = max(self.dma_clock, self.clock[eng]) + 1500.0
        self.done[name, self.dma_count[name]] = self.dma_clock + 1500.0
        return (name, sem, self.dma_count[name])

    def act(self, out, in_, func, after=(), **kw):
        cost = 0.83 * width(out) + 100.0
        if func in (ACT.Exp, ACT.Ln, ACT.Silu, ACT.Sigmoid) and self.table not in ("exp", func):
            cost += 1300.0
        if func in (ACT.Exp, ACT.Ln) and self.table != "exp":
            self.queue["act"].append(lambda e: e.preload_act_table_set("natural_log_exp_and_others"))
            self.table = "exp"
        elif func in (ACT.Silu, ACT.Sigmoid):
            self.table = func
        return self.do("act", lambda e: e.activation(out, in_, func, **kw), after, cost=cost)

    def copy(self, out, in_, after=()):
        return self.act(out, in_, ACT.Copy, after)

    def tt(self, out, a, b, op, after=(), eng="dve"):
        return self.do(eng, lambda e: e.tensor_tensor(out, a, b, op), after,
                       cost=(2.25 if eng == "pool" else 1.04) * width(out) + 70.0)

    def ts(self, out, a, s1, s2, op0, op1, after=(), eng="dve"):
        if s2 is None:
            return self.do(eng, lambda e: e.tensor_scalar(out, a, s1, None, op0), after,
                           cost=0.7 * width(out) + 70.0)
        return self.do(eng, lambda e: e.tensor_scalar(out, a, s1, s2, op0, op1), after,
                       cost=0.7 * width(out) + 70.0)

    def stt(self, out, a, s, b, op0, op1, after=()):
        return self.do("dve", lambda e: e.scalar_tensor_tensor(out=out, in0=a, scalar=s, in1=b, op0=op0, op1=op1),
                       after, cost=1.04 * width(out) + 70.0)

    def mm(self, out, lhsT, rhs, start, stop, after=(), mark=True):
        fast = lhsT.dtype == F32R
        return self.do("pe", lambda e: e.matmul(out, lhsT, rhs, start=start, stop=stop), after, mark,
                       cost=max(width(out) / 2.4, 107.0) if fast else max(1.68 * width(out), 107.0))

    def tr(self, out, in_, ident, after=(), mark=True):
        return self.do("pe", lambda e: e.transpose(out, in_, ident), after, mark, cost=109.0)


class Mem:

    def __init__(self, nc, at):
        self.nc, self.at = nc, at

    def put(self, name, shape, dt=F32):
        n = 4
        for d in shape[1:]:
            n *= d
        t = self.nc.alloc_sbuf_tensor_at(name, shape, dt, offset=self.at)
        self.at += (n + 31) // 32 * 32
        assert self.at <= TOP, (name, self.at - TOP)
        return t


class Bank:

    def __init__(self, ap):
        self.ap = ap
        self.free = []
        self.taken = None


class Pool:

    def __init__(self, banks, q=None):
        self.banks = banks
        self.n = 0
        self.q = q

    def take(self):
        if self.q is not None:
            b = min((b for b in self.banks if b.free is not b.taken), key=lambda b: self.q.when(b.free))
            b.taken = b.free
            return b
        b = self.banks[self.n % len(self.banks)]
        self.n += 1
        return b


class Weights:

    RAW = 3
    PARTS = 4
    AHEAD = 3

    def __init__(self, q, mem, dram, plan):
        self.q, self.dram, self.plan = q, dram, plan
        sb = lambda name, dt: mem.put(name, [P, 8, P], dt)
        self.raw = [sb(f"w_raw{i}", F32) for i in range(self.RAW)]
        self.hi = [sb(f"w_hi{i}", F32R) for i in range(self.PARTS)]
        self.lo = [sb(f"w_lo{i}", F32R) for i in range(self.PARTS)]
        self.sems = [(f"s_w{i}", q.semaphore(f"s_w{i}")) for i in range(self.RAW)]
        self.loaded = []
        self.raw_free = {}
        self.part_free = []
        self.split = {}
        self.n_split = 0
        self.n_unit = 0
        self.used = 0
        self.now = None
        self.lo_engine = "dve"
        self.pump()

    def pump(self):
        while len(self.loaded) < len(self.plan):
            n = len(self.loaded)
            if n >= self.RAW and n - self.RAW not in self.raw_free:
                break
            name, i, nt, _ = self.plan[n]
            s = n % self.RAW
            self.loaded.append(self.q.dma("sp", self.raw[s][:, 0:nt, :].rearrange("p a b -> p (a b)"),
                                          self.dram[name][i], self.sems[s], self.raw_free.get(n - self.RAW, ())))

    def split_next(self):
        n = self.n_split
        self.n_split += 1
        name, i, nt, parts = self.plan[n]
        if not parts:
            return
        s = n % self.RAW
        m = self.used
        self.used += 1
        r = m % self.PARTS
        free = [self.part_free[m - self.PARTS]] if m >= self.PARTS else []
        raw, hi, lo = self.raw[s][:, 0:nt, :], self.hi[r][:, 0:nt, :], self.lo[r][:, 0:nt, :]
        t_hi = self.q.copy(hi, raw, [self.loaded[n], *free])
        t_lo = self.q.tt(lo, raw, hi.bitcast(F32), ALU.subtract, [self.loaded[n], t_hi, *free], eng=self.lo_engine)
        self.raw_free[n] = (t_hi, t_lo)
        self.split[n] = (hi, lo, [t_hi, t_lo])
        self.pump()

    def next(self, key):
        n = self.n_unit
        self.n_unit += 1
        name, i, nt, parts = self.plan[n]
        assert (name, i) == key, (key, self.plan[n])
        while self.n_split < len(self.plan) and self.n_split <= n + self.AHEAD:
            if self.used - len(self.part_free) >= self.PARTS and self.plan[self.n_split][3]:
                break
            if self.n_split >= len(self.loaded):
                break
            self.split_next()
        self.now = n
        if parts:
            return self.split[n]
        return self.raw[n % self.RAW][:, 0:nt, :], None, [self.loaded[n]]

    def release(self, tok):
        if self.plan[self.now][3]:
            self.part_free.append(tok)
        else:
            self.raw_free[self.now] = (tok,)
            self.pump()


BLOCKED = "blocked"


def weave(q, streams, margin=0.0):
    live = [[s, ()] for s in streams]

    def advance(x):
        x[1] = next(x[0], None)
        if x[1] is None:
            live.remove(x)

    while live:
        for x in [x for x in live if x[1] is BLOCKED]:
            advance(x)
        able = [x for x in live if x[1] is not BLOCKED]
        assert able or not live
        if able:
            now = q.clock["pe"]
            advance(min(able, key=lambda x: max(q.when(x[1]) + margin, now)))


def run(steps):
    while True:
        try:
            next(steps)
        except StopIteration as e:
            return e.value


def program(nc, ins, out):
    with ExitStack() as ctx:
        q = Queues(nc, ctx)
        build(q, ins, out)
        block = ctx.enter_context(nc.Block())
        for name, reg in (("pe", block.tensor), ("act", block.scalar), ("dve", block.vector),
                          ("pool", block.gpsimd), ("sp", block.sync)):
            def run(eng, name=name):
                for step in q.queue[name]:
                    step(eng)
            reg(run)


COLS1 = [(0, 512), (512, 256)]
COLSX = [(0, 512)]
COLS2 = [(0, 264), (264, 264)]


def halves(ap, cols):
    if cols == COLS2:
        return ap.rearrange("p (a b) -> p a b", a=2)[:, :, 0:264]
    return ap[:, 0:sum(n for _, n in cols)]


def as_halves(ap, cols):
    return ap.rearrange("p (a b) -> p a b", a=2) if cols == COLS2 else ap


class Ops:

    def __init__(self, q, mem, ins):
        self.q = q
        self.small = mem.put("small", [P, NSMALL])
        self.const = mem.put("const", [P, NCONST])
        self.t_small = q.dma("act", self.small[:], ins["small"], ("s_load", q.semaphore("s_load")))
        self.t_const = q.dma("act", self.const[:], ins["const"], ("s_load2", q.semaphore("s_load2")))

    def sm(self, name, i=0, n=1, rows=(0, P)):
        a, _ = SMALL[name]
        return self.small[rows[0]:rows[1], a + i:a + i + n]

    def cs(self, name, r=P, n=P, i=0):
        a, _ = CONST[name]
        return self.const[0:r, a + i * P:a + i * P + n]

    def product_steps(self, key, xh, xl, cols, pool, ready):
        q = self.q
        wh, wl, t_w = self.W.next(key)
        b = pool.take()
        nt = wh.shape[1]
        tok = None
        for k in range(nt):
            after = [*(t_w if k == 0 else ()), *(b.free if k == 0 else ()),
                     ready[k] if isinstance(ready, list) else ready]
            for i, (c0, n) in enumerate(cols):
                for p, (w, x) in enumerate(((wh, xh), (wh, xl), (wl, xh))):
                    end = i == len(cols) - 1 and k == nt - 1 and p == 2
                    tok = q.mm(b.ap[:, i * 512:i * 512 + n], w[:, k, :], x[:, k, c0:c0 + n], k == 0 and p == 0,
                               k == nt - 1 and p == 2, after, mark=end)
                    after = ()
            if k < nt - 1:
                yield ()
        self.W.release(tok)
        return b, tok

    def product(self, *args):
        return run(self.product_steps(*args))

    def parts(self, hi, lo, src, after=(), eng="dve"):
        t = self.q.copy(hi, src, after)
        return self.q.tt(lo, src, hi.bitcast(F32), ALU.subtract, [t, *after], eng=eng)

    def norm_steps(self, chain, sqs, scale, v, t, y, after):
        q = self.q
        banks = [(chain.take(), c0, n) for c0, n in COLS2]
        for b, c0, n in banks:
            for i, sq in enumerate(sqs):
                m = q.mm(b.ap[:, 0:n], self.cs("ones"), sq[:, c0:c0 + n], i == 0, i == len(sqs) - 1,
                         [*after, *b.free])
        yield [m]
        for b, c0, n in banks:
            a = q.act(t[:, c0:c0 + n], b.ap[:, 0:n], ACT.Ln, [m, *after], scale=scale, bias=self.cs("eps", n=1))
            b.free = [q.ts(v[:, c0:c0 + n], b.ap[:, 0:n], scale, EPS, ALU.mult, ALU.add, [a])]
        c = q.act(y, t, ACT.Exp, [a, *b.free], scale=-0.5)
        yield [c]
        q.stt(t, y, -0.5, v, ALU.mult, ALU.mult, [c])
        q.tt(t, t, y, ALU.mult)
        return m, q.stt(y, t, 1.5, y, ALU.add, ALU.mult)

    def rstd(self, src, scale, eps, v, t, y, after):
        q = self.q
        b = q.act(t, src, ACT.Ln, [*after, self.t_const], scale=scale, bias=self.cs("eps", n=1))
        a = q.ts(v, src, scale, eps, ALU.mult, ALU.add, [b])
        c = q.act(y, t, ACT.Exp, [b], scale=-0.5)
        q.stt(t, y, -0.5, v, ALU.mult, ALU.mult, [c])
        q.tt(t, t, y, ALU.mult)
        return a, q.stt(y, t, 1.5, y, ALU.add, ALU.mult)


class DirectStats:

    def __init__(self, o, sq, cols, pool, last):
        self.o, self.sq, self.cols, self.last = o, sq, cols, last
        self.n = 0
        self.free = [None] * len(sq)
        self.b = pool.take()

    def add(self, src, after, *more):
        q, i = self.o.q, self.n % len(self.sq)
        a = q.act(self.sq[i], src, ACT.Square, [*after, *more, self.free[i]])
        for j, (c0, n) in enumerate(self.cols):
            self.m = q.mm(self.b.ap[:, 512 * j:512 * j + n], self.o.cs("ones"), self.sq[i][:, c0:c0 + n],
                          self.n == 0, self.n == self.last, [a, self.o.t_const, *self.b.free])
        self.free[i] = self.m
        self.n += 1

    def finish(self, dim, v, t, y):
        q, cols = self.o.q, self.cols
        f, r = self.o.rstd(halves(self.b.ap, cols), 1.0 / dim, EPS, as_halves(v, cols), as_halves(t, cols),
                           as_halves(y, cols), [self.m, q.last("dve")])
        self.b.free = [f]
        return r


class Stats:

    def __init__(self, o, acc, sq, cols):
        self.o, self.acc, self.sq, self.cols = o, acc, sq, cols
        self.n = 0
        self.free = [None, None]
        self.t = None

    def add(self, src, after):
        q, i = self.o.q, self.n % 2
        if self.n == 0:
            self.t = q.act(self.acc, src, ACT.Square, after)
        else:
            a = q.act(self.sq[i], src, ACT.Square, [*after, self.free[i]])
            self.t = q.tt(self.acc, self.acc, self.sq[i], ALU.add, [a, self.t], eng="pool")
            self.free[i] = self.t
        self.n += 1

    def finish(self, pool, dim, v, t, y, after=()):
        q, cols = self.o.q, self.cols
        b = pool.take()
        for i, (c0, n) in enumerate(cols):
            m = q.mm(b.ap[:, 512 * i:512 * i + n], self.o.cs("ones"), self.acc[:, c0:c0 + n], True, True,
                     [self.t, self.o.t_const, *b.free])
        f, r = self.o.rstd(halves(b.ap, cols), 1.0 / dim, EPS, as_halves(v, cols), as_halves(t, cols),
                           as_halves(y, cols), [m, q.last("dve"), *after])
        b.free = [f]
        return r


def build(q, ins, out):
    nc, ctx = q.nc, q.ctx
    ps = ctx.enter_context(nc.psum_tensor("ps", [P, 8, 512], F32))
    flat = ps[:].rearrange("p a b -> p (a b)")
    mem = Mem(nc, BASE)
    o = Ops(q, mem, ins)
    W = o.W = Weights(q, mem, ins, unit_plan())
    sm, cs = o.sm, o.cs

    def pairs(lo, hi):
        return Pool([Bank(flat[:, i * 1024:(i + 1) * 1024]) for i in range(lo, hi)])

    def singles(lo, hi):
        return Pool([Bank(ps[:, i, :]) for i in range(lo, hi)])

    def load(name, dst, src, after=(), eng="act"):
        return q.dma(eng, dst, src, (name, q.semaphore(name)), after)

    def everyone():
        return [q.last(e) for e in q.sem]

    def barrier(*more):
        toks = everyone() + list(more)
        for eng in q.sem:
            q.wait(eng, toks)
        q.wait("sp", more)

    M = mem.put("M", [P, 9, KT, 2])
    AM = mem.put("AM", [P, 3, KT, 2])
    GM = mem.put("GM", [P, 2, KT, 2])
    sc = mem.put("sc", [P, 16])
    t_sc = q.act(sc[:], sm("c", 0, 16), ACT.Silu, [o.t_small])
    low = mem.at
    high = low + 2 * 4 * TX * 4 + 512
    x_spill = nc.dram_tensor("x_spill", (P, KT, TX), F32).ap()
    h_spill = nc.dram_tensor("h_spill", (P, KT, T2), F32).ap()

    mem = Mem(nc, low)
    mixc = mem.put("mixc", [P, 4, TX])
    att = mem.put("att", [P, 4, TX])
    mem = Mem(nc, high)
    xh = mem.put("x1h", [P, KT, T1], F32R)
    xl = mem.put("x1l", [P, KT, T1], F32R)
    after_xn = mem.at
    X = mem.put("X", [P, KT, T1])
    hh = mem.put("h1h", [P, 8, T1], F32R)
    hl = mem.put("h1l", [P, 8, T1], F32R)
    row = mem.put("row", [2, 2, 512])
    tmem = Mem(nc, low)
    tm = [(tmem if i < 5 else mem).put(f"f1_t{i}", [P, T1])[:] for i in range(6)]

    def ada(j, pool):
        run(ada_steps(j, pool))

    def ada_steps(j, pool):
        toks = []
        for u in range(2):
            b = pool.take()
            for v in range(4):
                w, _, t_w = W.next(("w_ada", 8 * j + 4 * u + v))
                w = w.rearrange("p a b -> p (a b)").rearrange("p (a b) -> p a b", a=2)
                for i in range(2):
                    k = 2 * v + i
                    tok = q.mm(b.ap[0:2, 0:512], sc[:, 2 * k:2 * k + 2], w[:, i, :], k == 0, k == KT - 1,
                               [*t_w, *b.free, t_sc], mark=i == 1)
                W.release(tok)
                if v < 3:
                    yield ()
            e = q.copy(row[:, u, :], b.ap[0:2, 0:512], [tok])
            b.free = [e]
            toks.append(e)
            yield ()
        yield toks
        b = pool.take()
        for i in range(8):
            m = q.tr(b.ap[:, 2 * i:2 * i + 2], row[:, i // 4, (i % 4) * P:(i % 4 + 1) * P], cs("ident", 2, 2),
                     [*toks, o.t_const, *b.free], mark=i == 7)
        bias = sm("b_ada", 8 * j, 8).unsqueeze(2).broadcast_to([P, 8, 2])
        b.free = [q.tt(M[:, j, :, :], b.ap[:, 0:16].rearrange("p (a b) -> p a b", b=2), bias, ALU.add, [m])]

    def scales(i, j, gain):
        g = sm(gain, 0, 8).unsqueeze(2).broadcast_to([P, KT, 2])
        return q.stt(AM[:, i, :, :], M[:, j, :, :], 1.0, g, ALU.add, ALU.mult)

    def modulate(*args):
        return run(modulate_steps(*args))

    def modulate_beside(js, *args):
        toks = []

        def main():
            toks.extend((yield from modulate_steps(*args)))

        def others():
            for j in js:
                yield from ada_steps(j, pool)
                yield ()

        weave(q, [main(), others()])
        return toks

    def modulate_steps(X, y, r, groups, A, B, h, l, s):
        out_toks = []
        for k in range(KT):
            yield [out_toks[k - 1] if k else r]
            t = s[k % len(s)]
            before = [out_toks[k - len(s)]] if k >= len(s) else []
            m = q.tt(t, X[:, k, :], y, ALU.mult, [r, *before], eng="pool" if k % 3 == 2 else "dve")
            for g, (c0, n) in enumerate(groups):
                m = q.ts(t[:, c0:c0 + n], t[:, c0:c0 + n], A(k, g), B(k, g), ALU.mult, ALU.add, [m])
            out_toks.append(o.parts(h[:, k, :], l[:, k, :], t, [m]))
        return out_toks

    def scaled(X, y, r, gain, h, l, s):
        out_toks = []
        for k in range(KT):
            t = s[k % len(s)]
            m = q.stt(t, X[:, k, :], sm(gain, k), y, ALU.mult, ALU.mult, [r, *out_toks[k - len(s):k - len(s) + 1]]
                      if k >= len(s) else [r])
            out_toks.append(o.parts(h[:, k, :], l[:, k, :], t, [m]))
        return out_toks

    def ffn(name, X, cols, groups, xh, xl, hh, hl, gate, pool, tmp, t_x, stats):
        s, hf = tmp
        m_old = [None, None]
        t_old = [None, None]
        for p, (f0, nf) in enumerate(FF_PARTS):
            t_h = []
            for f in range(f0, f0 + nf):
                i = f % 2
                b, tok = o.product((f"w_in{name}", f), xh, xl, cols, pool, t_x)
                a = q.act(as_halves(s[i], cols), halves(b.ap, cols), ACT.Silu, [tok, m_old[i]])
                b.free = [a]
                b2, tok2 = o.product((f"w_in{name}", FF + f), xh, xl, cols, pool, t_x)
                m = q.tt(as_halves(hf[i], cols), as_halves(s[i], cols), halves(b2.ap, cols), ALU.mult,
                         [tok2, a, t_old[i]])
                b2.free = [m]
                m_old[i] = m
                t_old[i] = o.parts(hh[:, f - f0, :], hl[:, f - f0, :], hf[i], [m])
                t_h.append(t_old[i])
            for k in range(KT):
                b, tok = o.product((f"w_out{name}_{p}", k), hh, hl, cols, pool, t_h)
                if gate is None:
                    x = as_halves(X[:, k, :], cols)
                    b.free = [q.tt(x, x, halves(b.ap, cols), ALU.add, [tok])]
                else:
                    for g, (c0, n) in enumerate(groups):
                        b.free = [q.stt(X[:, k, c0:c0 + n], b.ap[:, c0:c0 + n], gate(k, g), X[:, k, c0:c0 + n],
                                        ALU.mult, ALU.add, [tok])]
                if p == 2 and stats is not None:
                    stats.add(X[:, k, :], b.free)
        return b.free[0]

    t_x = load("s_x", X[:].rearrange("p a b -> p (a b)"), ins["x"])
    G1 = [(0, TX), (TX, TC)]
    GX = [(0, TX)]

    def Af(i):
        return lambda k, g: AM[:, i, k, g:g + 1]

    def Bf(j):
        return lambda k, g: M[:, j, k, g:g + 1]

    def Gf(i):
        return lambda k, g: GM[:, i, k, g:g + 1]

    pool = pairs(0, 4)
    st = Stats(o, tm[5], [tm[0], tm[1]], COLS1)
    for k in range(KT):
        st.add(X[:, k, :], [t_x])
    ada(0, pool)
    r = st.finish(pool, D, tm[2], tm[3], tm[4])
    ada(1, pool)
    scales(0, 1, "norm_ffn1")
    t = modulate_beside((2, 3), X, tm[4], r, G1, Af(0), Bf(0), xh, xl, [tm[0], tm[1], tm[2], tm[3]])
    q.ts(GM[:, 0, :, :], M[:, 2, :, :], 0.5, None, ALU.mult, None)
    st = Stats(o, tm[5], [tm[0], tm[1]], COLS1)
    ffn("1", X, COLS1, G1, xh, xl, hh, hl, Gf(0), pool, ([tm[0], tm[1]], [tm[2], tm[3]]), t, st)
    ada(4, pool)
    scales(1, 4, "norm_mix")
    r = st.finish(pool, D, tm[2], tm[3], tm[4], [q.last("act")])
    t_spill = load("s_xsp", x_spill, X[:, :, 0:TX], everyone(), "sp")
    t = modulate_beside((5, 6, 7), X, tm[4], r, G1, Af(1), Bf(3), xh, xl, [tm[0], tm[1], tm[2], tm[3]])
    scales(2, 7, "norm_ffn2")
    barrier(t_spill)

    mem = Mem(nc, after_xn)
    row = mem.put("row2", [2, 2, 512])
    const1 = mem.put("const1", [P, NCONST1])
    t_c1 = load("s_c1", const1[:], ins["const1"], everyone(), "sp")

    def c1(name):
        a, n = CONST1[name]
        return const1[:, a:a + n]

    qT = mem.put("qT", [P, 4, TX])
    kT = mem.put("kT", [P, 2, T1])
    vp = mem.put("vp", [P, 6, 4, P])
    qkt = [mem.put(f"m_t{i}", [P, T1])[:] for i in range(5)]
    gb = mem.put("gb", [P, TX])
    gc = mem.put("gc", [P, TX])
    cu = mem.put("cu", [P, TX + 2])
    PT = [mem.put(f"PT{i}", [P, 6, TX]) for i in range(2)]
    pr = [mem.put(f"pr{i}", [P, T1]) for i in range(2)]
    sx = mem.put("sx", [P, 4, 4])
    W.lo_engine = "pool"
    q.do("pool", lambda e: e.memset(cu[:], 0.0))
    t_vp = q.do("pool", lambda e: e.memset(vp[:], 0.0))

    def qk_norm(b, tok, dst, T, cols, gain):
        raw, v, w, y, sqv = (a[:, 0:T] for a in qkt)
        e = q.copy(raw, halves(b.ap, cols), [tok, q.last("dve"), q.last("pool")])
        b.free = [e]
        a = q.act(sqv, raw, ACT.Square, [e])
        yield [a]
        b2 = pool.take()
        for i, (c0, n) in enumerate(cols):
            m = q.mm(b2.ap[:, c0:c0 + n], c1("ones64"), sqv[:, c0:c0 + n], True, True, [a, t_c1, *b2.free])
        yield [m]
        d = q.act(w, b2.ap[:, 0:T], ACT.Ln, [m], scale=1.0 / 64, bias=cs("eps", n=1))
        f = q.ts(v, b2.ap[:, 0:T], 1.0 / 64, EPS, ALU.mult, ALU.add, [d])
        b2.free = [f]
        d = q.act(y, w, ACT.Exp, scale=-0.5)
        yield [d]
        q.stt(w, y, -0.5, v, ALU.mult, ALU.mult, [d])
        q.tt(w, w, y, ALU.mult)
        q.stt(y, w, 1.5, y, ALU.add, ALU.mult)
        n1 = q.stt(raw, raw, gain, y, ALU.mult, ALU.mult)
        yield [n1]
        b3 = pool.take()
        m = q.mm(b3.ap[:, 0:TX], c1("rot"), raw[:, 0:TX], True, True, [n1, *b3.free])
        x1 = q.tt(v[:, 0:TX], raw[:, 0:TX], c1("cos"), ALU.mult, [n1], eng="pool")
        if T > TX:
            q.ts(dst[:, TX:T], raw[:, TX:T], 1.0, None, ALU.mult, None)
        x2 = q.tt(w[:, 0:TX], b3.ap[:, 0:TX], c1("sin"), ALU.mult, [m])
        b3.free = [x2]
        yield [x1]
        q.tt(dst[:, 0:TX], v[:, 0:TX], w[:, 0:TX], ALU.add, [x1])

    found, begun = {}, {}

    def qkv_products():
        for i in range(7):
            found[i] = yield from o.product_steps(("w_mix_in", i), xh, xl, COLSX if i < 4 else COLS1, pool, t)
            yield ()
            while 0 < i < 6 and i - 1 not in begun:
                yield BLOCKED

    def qk_norms():
        for i in range(6):
            while i not in found:
                yield BLOCKED
            steps = qk_norm(*found[i], *((qT[:, i, :], TX, COLSX, sm("q_norm")) if i < 4 else
                                         (kT[:, i - 4, :], T1, COLS1, sm("k_norm"))))
            tokens = next(steps)
            begun[i] = True
            yield tokens
            yield from steps
            yield ()

    pool.q = q
    weave(q, [qk_norms(), qkv_products()])
    pool.q = None
    b, tok = found[6]
    e = q.copy(pr[0][:], b.ap[:, 0:T1], [tok])
    b.free = [e]
    for half in range(2):
        b = pool.take()
        for i in range(3):
            blk = 3 * half + i
            m = q.tr(b.ap[:, i * P:(i + 1) * P], pr[0][:, blk * P:(blk + 1) * P], cs("ident"), [e, *b.free],
                     mark=i == 2)
        src = b.ap[:, 0:384].rearrange("p (a b) -> p a b", b=P)
        for g in range(2):
            for par in range(2):
                b.free = [q.ts(vp[:, 3 * half:3 * half + 3, 2 * g + par, 64 * par:64 * par + 64],
                               src[:, :, 64 * g:64 * g + 64], 1.0, None, ALU.mult, None, [m, t_vp])]
    t_qkv = q.last("dve")
    m_v = m
    all_free = [f for bb in pool.banks for f in bb.free]
    pool = pairs(0, 3)
    poolo = singles(6, 7)
    poolc = singles(7, 8)
    for bb in pool.banks + poolo.banks + poolc.banks:
        bb.free = list(all_free)

    def conv_steps():
        for i in range(4):
            b, tok = yield from o.product_steps(("w_mix_in", 7 + 3 * i), xh, xl, COLSX, poolc, None)
            b.free = [q.copy(gb[:], b.ap[:, 0:TX], [tok, q.last("dve")])]
            yield ()
            b, tok = yield from o.product_steps(("w_mix_in", 8 + 3 * i), xh, xl, COLSX, poolc, None)
            g = q.copy(gc[:], b.ap[:, 0:TX], [tok, q.last("dve")])
            b.free = [g]
            yield ()
            b, tok = yield from o.product_steps(("w_mix_in", 9 + 3 * i), xh, xl, COLSX, poolc, None)
            b.free = [q.tt(cu[:, 1:TX + 1], gc[:], b.ap[:, 0:TX], ALU.mult, [tok, g, t_vp])]
            y = mixc[:, i, :]
            q.ts(y, cu[:, 0:TX], sm("conv_w", i), None, ALU.mult, None)
            q.stt(y, cu[:, 1:TX + 1], sm("conv_w", 4 + i), y, ALU.mult, ALU.add)
            q.stt(y, cu[:, 2:TX + 2], sm("conv_w", 8 + i), y, ALU.mult, ALU.add)
            q.tt(y, y, gb[:], ALU.mult)
            yield ()
        yield from ada_steps(8, poolc)
        q.ts(GM[:, 1, :, :], M[:, 8, :, :], 0.5, None, ALU.mult, None)

    def attention_steps():
        norm_tok, tr_tok, ev_tok = {}, {}, {}
        pv_tok = {}
        bo = None

        def scores(n):
            h, qb, z = n // 4, n % 4, n % 2
            pair, par, g = h // 2, h % 2, h // 4
            r0 = 64 * par
            b = pool.take()
            for i, (c0, nn) in enumerate(COLS1):
                m = q.mm(b.ap[:, c0:c0 + nn], qT[r0:r0 + 64, pair, qb * P:(qb + 1) * P],
                         kT[r0:r0 + 64, g, c0:c0 + nn], True, True, [t_qkv, *b.free], mark=i == 1)
            x = sx[:, n % 4, :]
            q.do("dve", lambda e, x=x, b=b: e.reduce_max(x[:, 0:1], b.ap[:, 0:T1], AX.X), [m])
            nm = q.ts(x[:, 1:2], x[:, 0:1], -0.125, None, ALU.mult, None)
            ex = q.act(pr[z][:], b.ap[:, 0:T1], ACT.Exp, [nm, tr_tok.get(n - 2, m_v)], bias=x[:, 1:2],
                       scale=0.125, accum_out=x[:, 2:3])
            b.free = [ex]
            q.do("dve", lambda e, x=x: e.reciprocal(x[:, 3:4], x[:, 2:3]), [ex])
            norm_tok[n] = q.ts(pr[z][:], pr[z][:], x[:, 3:4], None, ALU.mult, None)

        def turn(n):
            h, qb, z = n // 4, n % 4, n % 2
            b = pool.take()
            for i in range(6):
                c0 = i * P if i < 3 else 512 + (i - 3) * P
                m = q.tr(b.ap[:, c0:c0 + P], pr[z][:, i * P:(i + 1) * P], cs("ident"), [norm_tok[n], *b.free],
                         mark=i == 5)
            tr_tok[n] = m
            src = b.ap.rearrange("p (a b) -> p a b", a=2)[:, :, 0:384].rearrange("p a (b c) -> p a b c", c=P)
            dst = PT[h % 2][:, :, qb * P:(qb + 1) * P].rearrange("p (a b) c -> p a b c", a=2)
            for a in range(2):
                ev_tok[h] = q.copy(dst[:, a], src[:, a], [m, pv_tok.get(h - 2)])
            b.free = [ev_tok[h]]

        def values(h):
            nonlocal bo
            pair, par, g = h // 2, h % 2, h // 4
            if par == 0:
                bo = poolo.take()
            for i in range(6):
                m = q.mm(bo.ap, vp[:, i, 2 * g + par, :], PT[h % 2][:, i, :], par == 0 and i == 0,
                         par == 1 and i == 5, [ev_tok[h], *bo.free], mark=i == 5)
                if i % 2 == 1:
                    yield ()
            pv_tok[h] = m
            if par == 1:
                bo.free = [q.ts(att[:, pair, :], bo.ap, 1.0, None, ALU.mult, None, [m])]

        scores(0)
        yield ()
        for n in range(32):
            if n + 1 < 32:
                scores(n + 1)
                yield ()
            if n >= 4 and n % 4 == 0:
                yield from values(n // 4 - 1)
            yield [norm_tok[n]]
            turn(n)
            yield ()
        yield from values(7)

    weave(q, [attention_steps(), conv_steps()], 800.0)
    barrier()

    W.lo_engine = "dve"
    mem = Mem(nc, high)
    Nh = mem.put("Nh", [P, KT, T2], F32R)
    Nl = mem.put("Nl", [P, KT, T2], F32R)
    after_n = mem.at
    H = mem.put("H", [P, KT, T2])
    hh = mem.put("h2h", [P, 8, T2], F32R)
    hl = mem.put("h2l", [P, 8, T2], F32R)
    tm = [mem.put(f"f2_t{i}", [P, T2])[:] for i in range(6)]
    tv = [mem.put(f"tv{i}", [P, TX])[:] for i in range(3)]
    t_h = [load("s_meta", H[:, :, 0:16], ins["meta"], everyone(), "sp"),
           load("s_xback", H[:, :, 16:T2], x_spill, [t_spill], "sp")]
    XV = H[:, :, 16:T2]
    tmx = [a[:, 0:TX] for a in tm]
    mh, ml = Nh[:, :, 0:TX], Nl[:, :, 0:TX]
    pool = pairs(0, 4)
    t = [None] * 8
    sums = []
    sq_free = [None, None]
    for src in (mixc, att):
        st = DirectStats(o, [tv[0], tv[1]], COLSX, pool, 3)
        st.free = sq_free
        for k in range(4):
            st.add(src[:, k, :], [])
        sums.append(st)
    rs = [sums[0].finish(512, tmx[0], tmx[1], tmx[4]), sums[1].finish(512, tmx[2], tmx[3], tmx[5])]
    for half, (src, gain, y, r) in enumerate(((mixc, "conv_out", tmx[4], rs[0]), (att, "attn_out", tmx[5], rs[1]))):
        for k in range(4):
            kk = 4 * (1 - half) + k
            z = tv[k % 3]
            m = q.stt(z, src[:, k, :], sm(gain, k), y, ALU.mult, ALU.mult, [r])
            t[kk] = o.parts(mh[:, kk, :], ml[:, kk, :], z, [m])
    st = Stats(o, tmx[5], [tv[0], tv[1]], COLSX)
    for k in range(KT):
        b, tok = o.product(("w_mix_out", k), mh, ml, COLSX, pool, t)
        b.free = [q.stt(XV[:, k, :], b.ap[:, 0:TX], M[:, 5, k, 0:1], XV[:, k, :], ALU.mult, ALU.add,
                        [tok, *t_h])]
        st.add(XV[:, k, :], b.free)
    r = st.finish(pool, D, tmx[0], tmx[1], tmx[4], [q.last("act")])
    t = modulate(XV, tmx[4], r, GX, Af(2), Bf(6), mh, ml, [tmx[0], tmx[1], tmx[2], tmx[3]])
    st = Stats(o, tmx[5], [tv[0], tv[1]], COLSX)
    ffn("2", XV, COLSX, GX, mh, ml, hh[:, :, 0:TX], hl[:, :, 0:TX], Gf(1), pool,
        ([tmx[0], tmx[1]], [tmx[2], tmx[3]]), t, st)
    r = st.finish(pool, D, tmx[0], tmx[1], tmx[4], [q.last("act")])
    st = DirectStats(o, [tm[2], tm[3]], COLS2, pool, KT - 1)
    for k in range(KT):
        m = q.stt(XV[:, k, :], XV[:, k, :], sm("final_norm", k), tmx[4], ALU.mult, ALU.mult, [r])
        st.add(H[:, k, :], [m])

    t_spill = load("s_hsp", h_spill, H[:], everyone(), "sp")
    r = st.finish(D, tm[0], tm[1], tm[4])
    t_n = scaled(H, tm[4], r, "norm_mix2", Nh, Nl, [tm[0], tm[1], tm[2], tm[3]])
    held = [f for bb in pool.banks for f in bb.free]
    pool = pairs(0, 2)
    for bb in pool.banks:
        bb.free = list(held)
    gates = o.product(("w_proj", 0), Nh, Nl, COLS2, pool, t_n)
    toks = everyone()
    for eng in ("act", "dve", "pool"):
        q.wait(eng, [*toks, t_spill])
    q.wait("pe", toks)
    acc = Mem(nc, low).put("acc", [P, KT, T2])
    chain = singles(4, 8)
    chain.q = q
    W.lo_engine = "pool"
    delta_net(o, Mem(nc, after_n), gates, Nh, Nl, acc, pool, chain)
    barrier()
    stick(o, Mem(nc, after_n), Nh, Nl, acc, pool, chain)
    barrier()
    W.lo_engine = "dve"
    t_h = load("s_hback", H[:], h_spill, [t_spill, *everyone()], "sp")
    pool = pairs(0, 4)
    t = [o.parts(Nh[:, k, :], Nl[:, k, :], acc[:, k, :]) for k in range(KT)]
    st = Stats(o, tm[5], [tm[2], tm[3]], COLS2)
    for k in range(KT):
        b, tok = o.product(("w_o2", k), Nh, Nl, COLS2, pool, t)
        x = as_halves(H[:, k, :], COLS2)
        b.free = [q.tt(x, x, halves(b.ap, COLS2), ALU.add, [tok, t_h])]
        st.add(H[:, k, :], b.free)
    r = st.finish(pool, D, tm[0], tm[1], tm[4], [q.last("act")])
    t = scaled(H, tm[4], r, "norm_ffn_2", Nh, Nl, [tm[0], tm[1], tm[2], tm[3]])
    t = ffn("3", H, COLS2, None, Nh, Nl, hh, hl, None, pool, ([tm[0], tm[1]], [tm[2], tm[3]]), t, None)
    t = load("s_out", out, H[:, :, 16:T2], [t], "sp")
    q.wait("sp", [t])


def delta_net(o, mem, gates, hn_h, hn_l, acc, pool, chain):
    q, W, sm, cs = o.q, o.W, o.sm, o.cs
    WIDE = [(0, P, 4), (4, 16, 1)]
    GROUPS = [(0, P, 2), (2, P, 2), (4, 16, 1)]
    SIZES = [P] * 4 + [16]
    ha = lambda ap: as_halves(ap, COLS2)
    gbt = mem.put("gbt", [64, T2])
    gcol = mem.put("gcol", [P, 5, 16])
    nb = mem.put("nb", [P, 5, 8])
    rm = [mem.put(f"r{i}", [P, T2])[:] for i in range(6)]
    QK = [mem.put(f"qk{s}", [P, 2, T2]) for s in range(3)]
    VV = [mem.put(f"vv{s}", [P, 2, T2]) for s in range(2)]
    ZZ = mem.put("zz", [P, 2, T2])
    craw = mem.put("craw", [P, T2 + 3])
    gB = mem.put("gB", [P, T2])
    DT = mem.put("DT", [P, 5, P])
    AT2 = [mem.put(f"AT{i}", [P, 5, P]) for i in range(2)]
    LT = mem.put("LT", [P, 5, P])
    LM = [mem.put(f"LM{i}", [P, 5, P]) for i in range(2)]
    UT2 = [mem.put(f"UT{i}", [P, 2, 5, P]) for i in range(2)]
    Xm = mem.put("Xm", [P, 5, P])
    kd2 = [mem.put(f"kd{i}", [P, 5, P]) for i in range(2)]
    vb2 = [mem.put(f"vb{i}", [P, 5, 2 * P]) for i in range(2)]
    gl2 = [mem.put(f"gl{i}", [P, 4]) for i in range(2)]
    ekd = mem.put("ekd", [P, 5])
    S = mem.put("S", [P, 2 * P])
    R = mem.put("R", [P, 2 * P])
    V = mem.put("V", [P, 2 * P])
    O2 = [mem.put(f"O{i}", [P, 2, T2]) for i in range(2)]
    oh = mem.put("oh", [P, 2, T2], F32R)
    ol = mem.put("ol", [P, 2, T2], F32R)
    q.do("pool", lambda e: e.memset(craw[:], 0.0))
    t_z = q.do("pool", lambda e: e.memset(gbt[:], 0.0))
    b, tok = gates
    za, ea, la = (rm[i][0:8, :] for i in range(3))
    eb = rm[3][32:40, :]
    q.ts(ha(za), halves(b.ap, COLS2)[0:8], sm("dt_bias", 0, 1, (0, 8)), None, ALU.add, None, [tok])
    q.stt(ea, za, -1.0, za, ALU.mult, ALU.max)
    f = q.ts(ha(eb), halves(b.ap, COLS2)[32:40], -1.0, None, ALU.mult, None)
    b.free = [f]
    t = q.act(ea, ea, ACT.Exp, [f], scale=-1.0)
    t = q.act(la, ea, ACT.Ln, [t], bias=1.0)
    q.act(eb, eb, ACT.Exp, [f])
    al = rm[4][0:8, 0:1]
    t = q.act(al, sm("a_log", 0, 1, (0, 8)), ACT.Exp)
    q.ts(za, za, 0.0, None, ALU.max, None)
    q.tt(za, za, la, ALU.add, [t])
    q.ts(za, za, al, -1.0, ALU.mult, ALU.mult)
    q.do("dve", lambda e: e.memset(ea, 1.0))
    for c, n in enumerate(SIZES):
        s = slice(c * P, c * P + n)
        q.do("dve", lambda e, s=s: e.tensor_tensor_scan(gbt[0:8, s], ea[:, s], za[:, s], 0.0, ALU.mult, ALU.add),
             [t_z])
    q.ts(eb, eb, 1.0, None, ALU.add, None)
    t_g = q.do("dve", lambda e: e.reciprocal(gbt[32:40, :], eb))
    columns = {}

    def gate_columns():
        yield [t_g]
        b = chain.take()
        for c, n in enumerate(SIZES):
            m = q.tr(b.ap[0:n, 40 * c:40 * c + 40], gbt[0:40, c * P:c * P + n], cs("ident", 40, 40),
                     [t_g, *b.free])
        for c0, n, C in WIDE:
            src = b.ap[0:n, 40 * c0:40 * (c0 + C)].rearrange("p (a b) -> p a b", b=40)
            q.ts(gcol[0:n, c0:c0 + C, 0:8], src[:, :, 0:8], 1.0, None, ALU.mult, None, [m])
            q.ts(gcol[0:n, c0:c0 + C, 8:16], src[:, :, 32:40], 1.0, None, ALU.mult, None)
            columns[0] = q.ts(nb[0:n, c0:c0 + C, :], src[:, :, 32:40], -1.0, None, ALU.mult, None)
        b.free = [columns[0]]
        yield ()

    projected, qk_ready, v_ready, z_ready, prepped, turned, inverse, scanned, normed, merged = \
        ({} for _ in range(10))
    last = {}

    def project(h, tiles):
        for i in tiles:
            steps = o.product_steps(("w_proj", 1 + 6 * h + i), hn_h, hn_l, COLS2, pool, None)
            while True:
                try:
                    next(steps)
                except StopIteration as end:
                    b, tok = end.value
                    break
                if late:
                    late.pop(0)()
                yield ()
            while late:
                late.pop(0)()
            if i >= 4:
                e = q.copy(ha(ZZ[:, i - 4, :]), halves(b.ap, COLS2), [tok, normed.get(h - 1)])
                b.free = [e]
                last["z", h] = e
                if i == 5:
                    projected["z", h] = e
            else:
                dst = QK[h % 3][:, i, :] if i < 2 else VV[h % 2][:, i - 2, :]
                free = normed.get(h - 3) if i < 2 else turned.get(h - 2)
                e = q.copy(ha(craw[:, 3:T2 + 3]), halves(b.ap, COLS2), [tok, last.get("craw"), t_z])
                b.free = [e]
                name, base = (("conv_q", h), ("conv_k", h), ("conv_v", 2 * h), ("conv_v", 2 * h + 1))[i]
                tiles_ = 16 if name == "conv_v" else 8

                def tap(j, dst=dst, name=name, base=base, n=tiles_, e=e, free=free):
                    if j == 0:
                        t = q.ts(dst, craw[:, 0:T2], sm(name, base), None, ALU.mult, None, [e, free])
                    else:
                        t = q.stt(dst, craw[:, j:j + T2], sm(name, j * n + base), dst, ALU.mult, ALU.add)
                    last["craw"] = t

                late.extend(lambda j=j, tap=tap: tap(j) for j in range(4))
                if i == 3:
                    projected[h] = e
            yield ()

    def normalized(h):
        if h < NH:
            qk, vv = QK[h % 3], VV[h % 2]
            while late:
                late.pop(0)()
            t = q.act(qk[:], qk[:], ACT.Silu, [last["craw"]])
            a = q.act(rm[0], qk[:, 0, :], ACT.Square, [t, last.get("ones")])
            v_ready[h] = q.act(vv[:], vv[:], ACT.Silu)
        if h >= 2:
            z_ready[h - 2] = q.act(ZZ[:], ZZ[:], ACT.Silu, [last["z", h - 2]])
        if h >= NH:
            yield ()
            return
        for i in range(2):
            sqv, v, w, y = rm[0], rm[1], rm[2], rm[5]
            if i:
                a = q.act(sqv, qk[:, i, :], ACT.Square, [t, last.get("ones")])
            yield [a]
            m, r = yield from o.norm_steps(chain, [sqv], 1.0, v, w, y, [a, last.get("l2")])
            last["ones"] = m
            t_n2 = q.stt(qk[:, i, :], qk[:, i, :], float(P) ** -0.5 if i == 0 else 1.0, y, ALU.mult,
                         ALU.mult, [t, r])
            last["l2"] = t_n2
        qk_ready[h] = t_n2
        yield ()

    late = []

    def tok3(ap, c0, n, C):
        return ap[:, c0 * P:c0 * P + C * n].rearrange("p (a b) -> p a b", b=n)

    def wide(ap, n, C):
        return ap.unsqueeze(1).broadcast_to([n, C, n])

    def prepare(h):
        s = h % 2
        qf, kf = (QK[h % 3][:, i, :] for i in range(2))
        v0, v1 = (VV[s][:, i, :] for i in range(2))
        AT, UT, kd, vb, gl = AT2[s], UT2[s], kd2[s], vb2[s], gl2[s]
        bB = rm[3]
        free = scanned.get(h - 2)
        while not columns:
            yield BLOCKED
        yield [columns[0]]
        for dst, r in ((gB[:], 0), (bB, 32)):
            for i, (c0, n) in enumerate(COLS2):
                b = chain.take()
                m = q.mm(b.ap[:, 0:n], cs("ident")[r:r + 8, r + h:r + h + 1].broadcast_to([8, P]), gbt[r:r + 8, c0:c0 + n], True, True,
                         [t_g, *b.free])
                t_b = q.copy(dst[:, c0:c0 + n], b.ap[:, 0:n], [m, last.get("gB"), last.get("bB")])
                b.free = [t_b]
            yield ()
        for c0, n, C in WIDE:
            g3 = tok3(gB[0:n, :], c0, n, C)
            col = gcol[0:n, c0:c0 + C, h:h + 1]
            for c in range(C):
                q.ts(DT[0:n, c0 + c, 0:n], g3[:, c, :], gcol[0:n, c0 + c, h:h + 1], 0.0, ALU.subtract, ALU.min,
                     [t_b, columns[0], free, last.get("DT")])
            t_e = q.tt(ekd[0:n, c0:c0 + C].unsqueeze(2), g3[:, :, n - 1:n], col, ALU.subtract)
        yield [t_e]
        for c0, n, C in WIDE:
            t = q.act(DT[0:n, c0:c0 + C, 0:n], DT[0:n, c0:c0 + C, 0:n], ACT.Exp, [t_e])
        for c0, n, C in WIDE:
            t_kd = q.act(ekd[0:n, c0:c0 + C], ekd[0:n, c0:c0 + C], ACT.Exp, [t_e])
        t_eg = q.act(gB[:], gB[:], ACT.Exp, [t_e])
        yield [t_eg]
        for c0, n, C in WIDE:
            dt = DT[0:n, c0:c0 + C, 0:n]
            t_dt = q.tt(dt, dt, wide(cs("incl", n, n), n, C), ALU.mult, [t])
            t_db = q.tt(LT[0:n, c0:c0 + C, 0:n], dt, tok3(bB[0:n, :], c0, n, C), ALU.mult, [t_dt, t_b],
                        eng="pool")
        last["bB"] = t_db
        q.ts(gl[:].unsqueeze(2), tok3(gB[:], 0, P, 4)[:, :, P - 1:P], 1.0, None, ALU.mult, None, [t_eg])
        while h not in qk_ready:
            yield BLOCKED
        t_in = qk_ready[h]
        yield [t_in, t_db]
        t_u = {}
        for c0, n, C in WIDE:
            b, b2 = chain.take(), chain.take()
            for c in range(C):
                cc = slice((c0 + c) * P, (c0 + c) * P + n)
                m = q.mm(b.ap[0:n, c * n:(c + 1) * n], kf[:, cc], kf[:, cc], True, True, [t_in, *b.free],
                         mark=c == C - 1)
            for c in range(C):
                cc = slice((c0 + c) * P, (c0 + c) * P + n)
                m2 = q.mm(b2.ap[0:n, c * n:(c + 1) * n], kf[:, cc], qf[:, cc], True, True, b2.free,
                          mark=c == C - 1)
            dt, at, lt = (a[0:n, c0:c0 + C, 0:n] for a in (DT, AT, LT))
            v3 = lambda bb: bb.ap[0:n, 0:C * n].rearrange("p (a b) -> p a b", b=n)
            b.free = [q.tt(lt, lt, v3(b), ALU.mult, [m, t_db])]
            u = UT[0:n, 0, c0:c0 + C, 0:n]
            q.tt(u, lt, wide(cs("level", n, n, 0), n, C), ALU.mult)
            t_lt = q.tt(u, wide(cs("ident", n, n), n, C), u, ALU.subtract)
            b2.free = [q.tt(at, v3(b2), dt, ALU.mult, [m2])]
            last["DT"] = b2.free[0]
        yield [t_lt]

        t_ut = {}
        for c0, n, C in GROUPS:
            b = chain.take()
            for c in range(C):
                m = q.tr(b.ap[0:n, c * n:(c + 1) * n], UT[0:n, 0, c0 + c, 0:n], cs("ident", n, n), [t_lt, *b.free],
                         mark=c == C - 1)
            t = q.copy(UT[0:n, 1, c0:c0 + C, 0:n], b.ap[0:n, 0:C * n].rearrange("p (a b) -> p a b", b=n), [m])
            b.free = [t]
            t_ut[c0] = t
        turns, b_free = [], []

        def turn(src, dst, w, c0, n, C):
            b = chain.take()
            for c in range(C):
                m = q.tr(b.ap[0:n, c * P:(c + 1) * P], src[:, (c0 + c) * P:(c0 + c) * P + n], cs("ident"),
                         [v_ready[h], *b.free], mark=c == C - 1)
            ps3 = b.ap[0:n, 0:C * P].rearrange("p (a b) -> p a b", b=P)
            if dst is kd:
                last["kd"] = m
                col = ekd[0:n, c0:c0 + C].unsqueeze(2).broadcast_to([n, C, P])
            else:
                col = gcol[0:n, c0:c0 + C, 8 + h:9 + h].broadcast_to([n, C, P])
            b.free = b_free[:] = [q.tt(dst[0:n, c0:c0 + C, w:w + P], ps3, col, ALU.mult, [m, t_kd])]

        for src, dst, w in ((kf, kd, 0), (v0, vb, 0), (v1, vb, P)):
            for g in WIDE:
                if not (dst is kd and g[1] == 16):
                    turns.append((src, dst, w, *g))
        x_used, t_m = {}, {}

        def level_mask(i):
            for c0, n, C in [g for g in WIDE if g[1] > (1 << i)]:
                t_m[i] = q.tt(LM[i % 2][0:n, c0:c0 + C, 0:n], LT[0:n, c0:c0 + C, 0:n],
                              wide(cs("level", n, n, i), n, C), ALU.mult,
                              [t_lt, last.get(("LM", i % 2))], eng="pool")

        level_mask(1)
        yield [t_ut[0], t_m[1]]
        for i in range(1, 7):
            todo = [g for g in GROUPS if g[1] > (1 << i)]
            lm = LM[i % 2]
            t_lm = t_m[i]
            if i < 6:
                level_mask(i + 1)
            t_x = {}
            for c0, n, C in todo:
                b = chain.take()
                for c in range(C):
                    m = q.mm(b.ap[0:n, c * n:(c + 1) * n], lm[0:n, c0 + c, 0:n], UT[0:n, 1, c0 + c, 0:n], True,
                             True, [t_lm, t_ut[c0], *b.free], mark=c == C - 1)
                last["LM", i % 2] = m
                t_x[c0] = q.copy(Xm[0:n, c0:c0 + C, 0:n], b.ap[0:n, 0:C * n].rearrange("p (a b) -> p a b", b=n),
                                 [m, x_used.get(c0), last.get("X")])
                b.free = [t_x[c0]]
            if turns:
                turn(*turns.pop(0))
            yield [t_x[0]]
            for c0, n, C in todo:
                b = chain.take()
                both = (2 << i) < n
                for c in range(C):
                    m = q.mm(b.ap[0:n, c * n:(c + 1) * n], Xm[0:n, c0 + c, 0:n], UT[0:n, 0, c0 + c, 0:n], True,
                             True, [t_x[c0], t_ut[c0], *b.free], mark=c == C - 1)
                if both:
                    for c in range(C):
                        m = q.mm(b.ap[0:n, (C + c) * n:(C + c + 1) * n], UT[0:n, 0, c0 + c, 0:n],
                                 Xm[0:n, c0 + c, 0:n], True, True, mark=c == C - 1)
                x_used[c0] = last["X"] = m
                if both:
                    a = UT[0:n, :, c0:c0 + C, 0:n]
                    d = b.ap[0:n, 0:2 * C * n].rearrange("p (x a b) -> p x a b", x=2, b=n)
                else:
                    a = UT[0:n, 0, c0:c0 + C, 0:n]
                    d = b.ap[0:n, 0:C * n].rearrange("p (a b) -> p a b", b=n)
                t_ut[c0] = q.tt(a, a, d, ALU.subtract, [m])
                b.free = [t_ut[c0]]
            if i == 2:
                q.tt(qf, qf, gB[:], ALU.mult, [t_eg, m2, t_in], eng="pool")
            if i == 4:
                t_k = q.tt(kf, kf, gB[:], ALU.mult, [last["kd"], t_eg, t_in], eng="pool")
            if i < 6:
                yield [t_ut[0], t_m[i + 1]]
        while turns:
            turn(*turns.pop(0))
        prepped[h] = last["gB"] = t_k
        inverse[h] = [t_ut[0], t_ut[2], t_ut[4]]
        turned[h] = b_free[0]
        yield ()

    def scan(h):
        s = h % 2
        qf, kf = (QK[h % 3][:, i, :] for i in range(2))
        AT, UT, kd, vb, gl, O = AT2[s], UT2[s], kd2[s], vb2[s], gl2[s], O2[s]
        t_k = prepped[h]
        t_vb = turned[h]
        for c, n in enumerate(SIZES):
            cc = slice(c * P, c * P + n)
            if c:
                b = chain.take()
                m = q.mm(b.ap[0:n, 0:256], kf[:, cc], S[:], True, True, [t_k, t_s, *b.free])
                t_r = q.stt(R[0:n, :], b.ap[0:n, 0:256], nb[0:n, c, h:h + 1], vb[0:n, c, :], ALU.mult,
                            ALU.add, [m])
                b.free = [t_r]
                rhs = R[0:n, :]
                yield [t_r]
            else:
                rhs, t_r = vb[0:n, c, :], t_vb
            b = chain.take()
            m = q.mm(b.ap[0:n, 0:256], UT[0:n, 0, c, 0:n], rhs, True, True, [t_r, *inverse[h], *b.free])
            t_v = q.copy(V[0:n, :], b.ap[0:n, 0:256], [m])
            b.free = [t_v]
            yield [t_v]
            bo = chain.take()
            if c < 4:
                b = chain.take()
                m2 = q.mm(b.ap[:, 0:256], kd[0:n, c, :], V[0:n, :], True, True, [t_v, *b.free])
            for x in range(2):
                ob = bo.ap[:, x * P:x * P + n]
                if c:
                    q.mm(ob, S[:, x * P:(x + 1) * P], qf[:, cc], True, False, [t_s, *bo.free], mark=False)
                m = q.mm(ob, V[0:n, x * P:(x + 1) * P], AT[0:n, c, 0:n], c == 0, True, [t_v, *bo.free],
                         mark=x == 1)
            if c < 4:
                if c:
                    t_s = q.stt(S[:], S[:], gl[:, c:c + 1], b.ap[:, 0:256], ALU.mult, ALU.add, [m2, m])
                else:
                    t_s = q.ts(S[:], b.ap[:, 0:256], 1.0, None, ALU.mult, None, [m2, last.get("S")])
                b.free = [t_s]
            t_o = q.copy(O[:, :, cc], bo.ap[:, 0:2 * P].rearrange("p (a b) -> p a b", a=2)[:, :, 0:n],
                         [m, normed.get(h - 2)])
            bo.free = [t_o]
            if c < 4:
                yield [t_s]
        last["S"] = m
        last["O", h] = t_o
        scanned[h] = m
        yield ()

    def norm(h):
        qf, kf = (QK[h % 3][:, i, :] for i in range(2))
        O, y = O2[h % 2], rm[4]
        sqs = (qf, kf)
        for x in range(2):
            a = q.act(sqs[x], O[:, x, :], ACT.Square, [last["O", h], scanned[h]])
        yield [a]
        m, r = yield from o.norm_steps(chain, sqs, 1.0 / 256, kf, qf, y, [a, last.get("gained")])
        for x in range(2):
            q.stt(O[:, x, :], O[:, x, :], sm("dn_gain", x), y, ALU.mult, ALU.mult, [r])
        last["gained"] = q.last("dve")
        while h not in z_ready or (h and h - 1 not in merged):
            yield BLOCKED
        for x in range(2):
            w = q.tt(O[:, x, :], O[:, x, :], ZZ[:, x, :], ALU.mult, [z_ready[h]])
            t = o.parts(oh[:, x, :], ol[:, x, :], O[:, x, :], [w, merged.get(h - 1)], eng="pool")
            yield ()
        normed[h] = t
        yield ()

    def branch(h):
        t_in = normed[h]
        yield [t_in]
        for u in range(2):
            wh, wl, t_w = W.next(("w_bdn", 2 * h + u))
            for j in range(4):
                k8 = 4 * u + j
                b = pool.take()
                for i, (c0, n) in enumerate(COLS2):
                    for k in range(2):
                        for p, (w, x) in enumerate(((wh, oh), (wh, ol), (wl, oh))):
                            end = k == 1 and p == 2
                            tok = q.mm(b.ap[:, 512 * i:512 * i + n], w[:, 2 * j + k, :], x[:, k, c0:c0 + n],
                                       k == 0 and p == 0, end, [*t_w, t_in, *b.free], mark=end and i == 1)
                if j == 3:
                    W.release(tok)
                a = ha(acc[:, k8, :])
                if h == 0:
                    b.free = [q.ts(a, halves(b.ap, COLS2), 1.0, None, ALU.mult, None, [tok])]
                else:
                    b.free = [q.tt(a, a, halves(b.ap, COLS2), ALU.add, [tok])]
                if late:
                    late.pop(0)()
                yield ()
        merged[h] = tok

    def until(done, h):
        if h != -1 and h != -2:
            while h not in done:
                yield BLOCKED

    def units():
        for h in range(NH + 2):
            if h < NH:
                yield from until(projected, h)
            if h >= 2:
                yield from until(projected, ("z", h - 2))
            yield from normalized(h)

    def fills():
        for h in range(2):
            yield from project(h, range(4))
            yield from until(v_ready, h)
        for h in range(NH):
            if h + 2 < NH:
                yield from until(normed, h - 1)
                yield from until(prepped, h)
                yield from project(h + 2, range(4))
            yield from until(normed, h - 1)
            yield from project(h, range(4, 6))
            if h:
                yield from branch(h - 1)
            yield from until(z_ready, h)
        yield from until(normed, NH - 1)
        yield from branch(NH - 1)

    def heads(part, *before):
        for h in range(NH):
            for done, back in before:
                yield from until(done, h - back)
            yield from part(h)

    weave(q, [heads(scan, (prepped, 0)), heads(norm, (scanned, 0)), heads(prepare, (scanned, 2)), units(),
              gate_columns(), fills()], 250.0)


def stick(o, mem, hn_h, hn_l, acc, pool, chain):
    q, W, sm, cs = o.q, o.W, o.sm, o.cs
    SIZES = [P] * 4 + [16]
    ha = lambda ap: as_halves(ap, COLS2)
    accs = mem.put("accs", [P, KT, T2])
    rm = [mem.put(f"sr{i}", [P, T2])[:] for i in range(6)]
    Fs = [mem.put(f"sbf{s}", [P, 3, T2]) for s in range(2)]
    vts = [mem.put(f"vt{i}", [P, 5, P]) for i in range(2)]
    Zs = [mem.put(f"Z{i}", [P, 5, T2]) for i in range(2)]
    SPs = [mem.put(f"SP{i}", [P, 5, T2]) for i in range(2)]
    oh = mem.put("sbh", [P, 1, T2], F32R)
    ol = mem.put("sbl", [P, 1, T2], F32R)
    oc = mem.put("oc", [P, T2])
    projected, prepped, scored, weighed, merged, evac = ({} for _ in range(6))
    last = {}

    def gates(base, tiles, a, add):
        for k in tiles:
            b, tok = yield from o.product_steps(("w_proj", base + k), hn_h, hn_l, COLS2, pool, None)
            t = rm[3 + k % 2]
            e = q.act(ha(t), halves(b.ap, COLS2), ACT.Sigmoid, [tok, last.get(("rm", k % 2))])
            b.free = [e]
            last["rm", k % 2] = q.tt(a[:, k, :], a[:, k, :], t, ALU.mult, [e])
            if add is not None:
                q.tt(add[:, k, :], add[:, k, :], a[:, k, :], ALU.add)
            yield ()

    def project(h):
        s = h % 2
        for i in range(3):
            b, tok = yield from o.product_steps(("w_proj", 49 + 3 * h + i), hn_h, hn_l, COLS2, pool, None)
            e = q.copy(ha(Fs[s][:, i, :]), halves(b.ap, COLS2), [tok, scored.get(h - 2)])
            b.free = [e]
            evac[h, i] = e
            yield ()
        projected[h] = e

    def units():
        for h in range(NH):
            for i in range(2):
                yield from until(evac, (h, i))
                dst = Fs[h % 2][:, i, :]
                a = q.act(rm[2], dst, ACT.Square, [evac[h, i], last.get("ones")])
                yield [a]
                m, r = yield from o.norm_steps(chain, [rm[2]], 1.0 / P, rm[5], rm[0], rm[1], [a, last.get("n")])
                last["ones"] = m
                t = q.stt(dst, dst, sm("sbq" if i == 0 else "sbk"), rm[1], ALU.mult, ALU.mult, [r])
                if i == 0:
                    t = q.ts(dst, dst, float(P) ** -0.5, None, ALU.mult, None)
                last["n"] = t
            prepped[h] = t
            yield ()

    def spans(jb):
        lo = jb * P
        if T2 - lo > 512:
            return [(lo, 264), (lo + 264, 264)]
        return [(lo, T2 - lo)]

    def scores(h):
        s = h % 2
        qf, kf, vf = (Fs[s][:, i, :] for i in range(3))
        Z, SP, vt = Zs[s], SPs[s], vts[s]
        t_in = [projected[h], prepped[h]]
        free = weighed.get(h - 2)
        for jb, n in enumerate(SIZES):
            for c0, w in spans(jb):
                b = chain.take()
                m = q.mm(b.ap[0:n, 0:w], kf[:, jb * P:jb * P + n], qf[:, c0:c0 + w], True, True,
                         [*t_in, *b.free])
                z, sp = Z[0:n, jb, c0:c0 + w], SP[0:n, jb, c0:c0 + w]
                q.copy(z, b.ap[0:n, 0:w], [m, free])
                e = q.act(sp, b.ap[0:n, 0:w], ACT.Abs)
                b.free = [e]
            yield [e]
            lo = jb * P
            z, sp = Z[0:n, jb, lo:T2], SP[0:n, jb, lo:T2]
            q.act(sp, sp, ACT.Exp, scale=-1.0)
            t = q.act(sp, sp, ACT.Ln, bias=1.0)
            yield [t]
            q.stt(sp, z, 0.0, sp, ALU.max, ALU.add, [t])
            t = q.tt(SP[0:n, jb, lo:lo + n], SP[0:n, jb, lo:lo + n], cs("strict", n, n), ALU.mult)
        for c0, n, C in ((0, P, 4), (4, 16, 1)):
            b = chain.take()
            for c in range(C):
                m = q.tr(b.ap[0:n, c * P:(c + 1) * P], vf[:, (c0 + c) * P:(c0 + c) * P + n], cs("ident"),
                         [*t_in, *b.free], mark=c == C - 1)
            t_vt = q.copy(vt[0:n, c0:c0 + C, :], b.ap[0:n, 0:C * P].rearrange("p (a b) -> p a b", b=P),
                          [m, free])
            b.free = [t_vt]
        scored[h] = m
        last["sp", h] = (t, t_vt)
        yield ()

    def weights(h):
        s = h % 2
        Z, SP, vt = Zs[s], SPs[s], vts[s]
        t_sp, t_vt = last["sp", h]
        yield [t_sp]
        for jb in range(4, -1, -1):
            n = SIZES[jb]
            for c0, w in spans(jb):
                b = chain.take()
                terms = [(cs("tri", n, n), jb, c0, w)]
                for j2 in range(jb + 1, 5):
                    a = max(c0, j2 * P)
                    if a < c0 + w:
                        terms.append((cs("ones", SIZES[j2], n), j2, a, c0 + w - a))
                for i, (lhs, j2, a, ww) in enumerate(terms):
                    m = q.mm(b.ap[0:n, a - c0:a - c0 + ww], lhs, SP[0:SIZES[j2], j2, a:a + ww], i == 0,
                             i == len(terms) - 1, [t_sp, *b.free], mark=i == len(terms) - 1)
                z = Z[0:n, jb, c0:c0 + w]
                b.free = [q.tt(z, z, b.ap[0:n, 0:w], ALU.subtract, [m])]
                if w == 264:
                    yield ()
            lo = jb * P
            d = Z[0:n, jb, lo:lo + n]
            t = q.ts(d, d, 0.0, None, ALU.min, None)
            yield [t]
            t = q.act(Z[0:n, jb, lo:T2], Z[0:n, jb, lo:T2], ACT.Exp, [t])
            yield [t]
            t_w = q.tt(d, d, cs("strict", n, n), ALU.mult, [t])
        yield [t_w]
        for c0, w in COLS2:
            b = chain.take()
            terms = []
            for jb in range(5):
                a = max(c0, jb * P)
                if a < c0 + w:
                    terms.append((jb, a, c0 + w - a))
            for i, (jb, a, ww) in enumerate(terms):
                m = q.mm(b.ap[:, a - c0:a - c0 + ww], vt[0:SIZES[jb], jb, :], Z[0:SIZES[jb], jb, a:a + ww], i == 0,
                         i == len(terms) - 1, [t_vt, t_w, *b.free], mark=i == len(terms) - 1)
            e = q.copy(oc[:, c0:c0 + w], b.ap[:, 0:w], [m, last.get("oc")])
            b.free = [e]
            if c0 == 0:
                yield ()
        last["pv"] = m
        while h and h - 1 not in merged:
            yield BLOCKED
        yield [e]
        weighed[h] = last["oc"] = o.parts(oh[:, 0, :], ol[:, 0, :], oc[:], [e, merged.get(h - 1)])
        yield ()

    def branch(h):
        t_in = weighed[h]
        wh, wl, t_w = W.next(("w_bsb", h))
        for k in range(KT):
            b = pool.take()
            for i, (c0, n) in enumerate(COLS2):
                for p, (w, x) in enumerate(((wh, oh), (wh, ol), (wl, oh))):
                    tok = q.mm(b.ap[:, 512 * i:512 * i + n], w[:, k, :], x[:, 0, c0:c0 + n], p == 0, p == 2,
                               [*t_w, t_in, *b.free], mark=p == 2 and i == 1)
            if k == KT - 1:
                W.release(tok)
            a = ha(accs[:, k, :])
            if h == 0:
                b.free = [q.ts(a, halves(b.ap, COLS2), 1.0, None, ALU.mult, None, [tok])]
            else:
                b.free = [q.tt(a, a, halves(b.ap, COLS2), ALU.add, [tok])]
            yield ()
        merged[h] = tok

    def until(done, h):
        if h != -1 and h != -2:
            while h not in done:
                yield BLOCKED
            yield [done[h]]

    def fills():
        yield from project(0)
        yield from gates(73, range(4), acc, None)
        yield from project(1)
        yield from gates(73, range(4, 8), acc, None)
        for h in range(NH):
            if h + 2 < NH:
                yield from until(scored, h)
                yield from project(h + 2)
            if h:
                yield from until(weighed, h - 1)
                yield from branch(h - 1)
        yield from until(weighed, NH - 1)
        yield from branch(NH - 1)
        yield from gates(81, range(8), accs, acc)

    def heads(part, *before):
        for h in range(NH):
            for done, back in before:
                yield from until(done, h - back)
            yield from part(h)

    weave(q, [heads(weights, (scored, 0)), heads(scores, (prepped, 0), (projected, 0), (weighed, 2)), units(),
              fills()])


def _tiles(np, w, rows=None):
    k, n = w.shape
    return np.ascontiguousarray(w.reshape(k // P, P, n // P, P).transpose(2, 1, 0, 3)).reshape(n // P, P, k)


def _constants(np):
    i = np.arange(P)
    c = np.zeros((P, NCONST), np.float32)

    def put(name, a, at=0):
        c[:, CONST[name][0] + at:CONST[name][0] + at + a.shape[1]] = a

    put("ident", np.eye(P, dtype=np.float32))
    put("ones", np.ones((P, P), np.float32))
    put("tri", (i[:, None] >= i[None, :]).astype(np.float32))
    put("incl", (i[None, :] >= i[:, None]).astype(np.float32))
    put("eps", np.full((P, 1), EPS, np.float32))
    put("strict", (i[None, :] > i[:, None]).astype(np.float32))
    for lv in range(7):
        b = 1 << lv
        m = (i[:, None] // (2 * b) == i[None, :] // (2 * b)) & ((i[:, None] // b) % 2 == 0) & \
            ((i[None, :] // b) % 2 == 1)
        put("level", m.astype(np.float32), lv * P)
    c1 = np.zeros((P, NCONST1), np.float32)
    c1[:, 0:128] = (i[:, None] // 64 == i[None, :] // 64)
    rot = np.zeros((P, P), np.float32)
    for a in range(0, P, 2):
        rot[a + 1, a] = -1.0
        rot[a, a + 1] = 1.0
    c1[:, 128:256] = rot
    tok = np.arange(TX)
    inv = (np.float32(10000.0) ** (-np.arange(16, dtype=np.float32) / np.float32(16))).astype(np.float32)
    row = (tok // 64).astype(np.float32)
    col = (tok % 64).astype(np.float32)
    ang = np.concatenate([row[:, None] * inv, col[:, None] * inv], axis=-1).astype(np.float32)
    pos = (i % 64) // 2
    c1[:, 256:768] = np.cos(ang).T[pos]
    c1[:, 768:1280] = np.sin(ang).T[pos]
    return c, c1


def kernel(**inputs):
    import numpy as np
    import concourse.bacc as bacc
    from concourse.bass_utils import run_bass_kernel_spmd

    g = {k: np.asarray(v) for k, v in inputs.items()}

    def cols(v):
        return v.reshape(-1, P).T

    def feat(x):
        return x.T.reshape(KT, P, -1).transpose(1, 0, 2)

    a = {}
    sm = np.zeros((P, NSMALL), np.float32)

    def put(name, v, rows=P):
        s, n = SMALL[name]
        sm[0:rows, s:s + n] = v

    put("b_ada", cols(g["b_ada"][0]))
    put("norm_ffn1", cols(g["norm_ffn1"][0]))
    put("norm_mix", cols(g["norm_mix"][0]))
    put("norm_ffn2", cols(g["norm_ffn2"][0]))
    put("final_norm", cols(g["final_norm"]))
    put("q_norm", np.concatenate([g["q_norm"][0]] * 2)[:, None])
    put("k_norm", np.concatenate([g["k_norm"][0]] * 2)[:, None])
    put("attn_out", cols(g["attn_out_norm"][0]))
    put("conv_out", cols(g["conv_out_norm"][0]))
    put("conv_w", cols(g["conv_w"][0].reshape(-1)))
    put("norm_mix2", cols(g["norm_mix_gain_2"][0]))
    put("norm_ffn_2", cols(g["norm_ffn_gain_2"][0]))
    for n in "qkv":
        put("conv_" + n, cols(g[f"conv_{n}_2"][0].reshape(-1)))
    put("dn_gain", cols(g["dn_out_norm_gain_2"][0]))
    put("sbq", g["sb_q_norm_gain_2"][0][:, None])
    put("sbk", g["sb_k_norm_gain_2"][0][:, None])
    put("a_log", g["dn_a_log_2"][0][:, None], NH)
    put("dt_bias", g["dn_dt_bias_2"][0][:, None], NH)
    put("c", np.stack([cols(g["c"][0]), cols(g["c_ctx"])], axis=2).reshape(P, 16))
    a["small"] = sm
    a["const"], a["const1"] = _constants(np)
    a["x"] = np.concatenate([feat(g["x"][0]), feat(g["ctx"][0])], axis=2).reshape(P, -1)
    a["meta"] = np.ascontiguousarray(feat(g["meta_tokens_2"]))

    a["w_ada"] = np.ascontiguousarray(
        g["w_ada"][0].reshape(4, 2, P, 18, 512).transpose(3, 0, 2, 1, 4)).reshape(72, P, 1024)
    for n, wi, wo in (("1", "w_ffn1_in", "w_ffn1_out"), ("2", "w_ffn2_in", "w_ffn2_out"),
                      ("3", "w_ffn_in_2", "w_ffn_out_2")):
        a[f"w_in{n}"] = _tiles(np, g[wi][0])
        for p, (f0, nf) in enumerate(FF_PARTS):
            a[f"w_out{n}_{p}"] = _tiles(np, g[wo][0][f0 * P:(f0 + nf) * P])
    w = g["w_mix_in"][0]
    k0, k1 = w[:, 512:576], w[:, 576:640]
    order = [w[:, 0:512], k0, k0, k1, k1, w[:, 640:768]]
    for i in range(4):
        for base in (768, 1280, 1792):
            order.append(w[:, base + i * P:base + (i + 1) * P])
    a["w_mix_in"] = _tiles(np, np.concatenate(order, axis=1))
    a["w_mix_out"] = _tiles(np, g["w_mix_out"][0])
    w = g["w_in_2"][0]
    z = np.zeros((D, 24), np.float32)
    order = [w[:, 6144:6152], z, w[:, 6152:6160], z, np.zeros((D, 64), np.float32)]
    for h in range(NH):
        order += [w[:, h * P:(h + 1) * P], w[:, 1024 + h * P:1024 + (h + 1) * P],
                  w[:, 2048 + 256 * h:2048 + 256 * (h + 1)], w[:, 4096 + 256 * h:4096 + 256 * (h + 1)]]
    for h in range(NH):
        order += [w[:, 6160 + 1024 * j + h * P:6160 + 1024 * j + (h + 1) * P] for j in range(3)]
    order.append(w[:, 9232:11280])
    a["w_proj"] = _tiles(np, np.concatenate(order, axis=1))
    w = g["w_branch_dn_2"][0].reshape(NH, 2, P, 2, 4, P)
    a["w_bdn"] = np.ascontiguousarray(w.transpose(0, 3, 2, 4, 1, 5)).reshape(2 * NH, P, 8 * P)
    a["w_bsb"] = np.ascontiguousarray(g["w_branch_sb_2"][0]).reshape(NH, P, 8 * P)
    a["w_o2"] = _tiles(np, g["w_out_2"][0])

    nc = bacc.Bacc("TRN2", target_bir_lowering=False, num_devices=1)
    ins = {n: nc.dram_tensor("in_" + n, v.shape, F32, kind="ExternalInput").ap() for n, v in a.items()}
    out = nc.dram_tensor("out", (P, KT, TX), F32, kind="ExternalOutput").ap()
    program(nc, ins, out)
    r = run_bass_kernel_spmd(nc, [{"in_" + n: v for n, v in a.items()}], core_ids=[0])
    y = r.results[0]["out"]
    return np.ascontiguousarray(y.transpose(1, 0, 2).reshape(D, TX).T).reshape(1, TX, D)
```
